# Optimizing a Trainium2 kernel written in Bass

```python
import math
import jax, jax.numpy as jnp
from jax import lax
import numpy as np

D_MODEL = 1024
BATCH = 1
SEQ = 256
DEPTH = 2

MEM_LEN = 256
EPS = 1e-6
RWKV_WIDTH = D_MODEL // 2
RWKV_HEAD = 64
RWKV_HEADS = RWKV_WIDTH // RWKV_HEAD
DECAY_RANK = 64
ICLR_RANK = 64
GATE_RANK = 128
VRES_RANK = 32
GN_EPS = 64e-5
DIFF_WIDTH = D_MODEL - RWKV_WIDTH
DIFF_HEADS = 4
DIFF_VDIM = DIFF_WIDTH // DIFF_HEADS
DIFF_QDIM = DIFF_VDIM // 2
ROPE_DIMS = DIFF_QDIM // 4
ROPE_THETA = 500000.0
Q_BLOCK = 128
XATTN_HEADS = 4
XATTN_HEAD = D_MODEL // XATTN_HEADS
D_FF_DENSE = 2816
N_EXPERTS = 8
TOP_K = 2
D_FF_EXPERT = 3584
N_DENSE = (DEPTH + 1) // 2
N_MOE = DEPTH // 2
RWKV_COLS = 3 * RWKV_WIDTH + DECAY_RANK + ICLR_RANK + GATE_RANK
DIFF_COLS = 3 * DIFF_WIDTH
IN_COLS = RWKV_COLS + DIFF_COLS
RWKV_SPLITS = (RWKV_WIDTH, 2 * RWKV_WIDTH, 3 * RWKV_WIDTH, 3 * RWKV_WIDTH + DECAY_RANK, 3 * RWKV_WIDTH + DECAY_RANK + ICLR_RANK)

kernel_name = "hybrid_rwkv7_diffattn_moe_block"

def rms_norm(x, g):
    xf = x.astype(jnp.float32)
    y = xf * lax.rsqrt(jnp.mean(xf * xf, axis=-1, keepdims=True) + EPS)
    return (y * g.astype(jnp.float32)).astype(x.dtype)

def token_shift(p, mu):
    prev = jnp.pad(p, ((0, 0), (1, 0), (0, 0)))[:, :-1]
    return p + (prev - p) * mu

def rwkv7_step(state, inp):
    r, w, k, v, kk, a = inp
    sa = jnp.einsum('bhij,bhj->bhi', state, -kk)
    state = state * w[:, :, None, :] + sa[..., None] * (kk * a)[:, :, None, :] + v[..., None] * k[:, :, None, :]
    y = jnp.einsum('bhij,bhj->bhi', state, r)
    return state, y

def rwkv7_time_mix(p, v_first, v_mix_logit, w0, w_up, a0, a_up, g_up, k_k, k_a, r_k, gn_w, gn_b):
    B, S, _ = p.shape
    f32 = jnp.float32
    r, k, v, d_w, d_a, d_g = jnp.split(p, RWKV_SPLITS, axis=-1)
    w_log = -jax.nn.softplus(-(w0 + jnp.tanh(d_w) @ w_up).astype(f32)) - 0.5
    decay = jnp.exp(-jnp.exp(w_log))
    a = jax.nn.sigmoid(a0 + d_a @ a_up)
    g = jax.nn.sigmoid(d_g) @ g_up
    if v_first is not None:
        v = v + (v_first - v) * jax.nn.sigmoid(v_mix_logit)
    heads = lambda t: t.reshape(B, S, RWKV_HEADS, RWKV_HEAD)
    kk = heads(k * k_k).astype(f32)
    kk = kk * lax.rsqrt(jnp.maximum(jnp.sum(kk * kk, -1, keepdims=True), 1e-24))
    k = k * (1 + (a - 1) * k_a)
    rh, kh, vh, ah = heads(r), heads(k), heads(v), heads(a)
    seq_major = lambda t: jnp.swapaxes(t.astype(f32), 0, 1)
    xs = (seq_major(rh), seq_major(heads(decay)), seq_major(kh), seq_major(vh), seq_major(kk), seq_major(ah))
    state0 = jnp.zeros((B, RWKV_HEADS, RWKV_HEAD, RWKV_HEAD), f32)
    _, y = lax.scan(rwkv7_step, state0, xs)
    y = jnp.swapaxes(y, 0, 1)
    mean = jnp.mean(y, -1, keepdims=True)
    var = jnp.mean(jnp.square(y - mean), -1, keepdims=True)
    y = ((y - mean) * lax.rsqrt(var + GN_EPS)).reshape(B, S, RWKV_WIDTH)
    y = y.astype(p.dtype) * gn_w + gn_b
    bonus = jnp.sum(rh * kh * r_k, -1, keepdims=True) * vh
    y = (y + bonus.reshape(B, S, RWKV_WIDTH)) * g
    return y, v

def rope_partial(x, cos, sin):
    half = ROPE_DIMS // 2
    x1 = x[..., :half]
    x2 = x[..., half:ROPE_DIMS]
    return jnp.concatenate([x1 * cos - x2 * sin, x2 * cos + x1 * sin, x[..., ROPE_DIMS:]], axis=-1)

def diff_attention(p, cos, sin, q_g, k_g, lq1, lk1, lq2, lk2, subln_g, lam_init):
    B, S, _ = p.shape
    q, k, v = jnp.split(p, [DIFF_WIDTH, 2 * DIFF_WIDTH], axis=-1)
    q = q.reshape(B, S, DIFF_HEADS, 2, DIFF_QDIM)
    k = k.reshape(B, S, DIFF_HEADS, 2, DIFF_QDIM)
    v = v.reshape(B, S, DIFF_HEADS, DIFF_VDIM)
    q = rope_partial(rms_norm(q, q_g), cos, sin)
    k = rope_partial(rms_norm(k, k_g), cos, sin)
    f32 = jnp.float32
    lam = (jnp.exp(jnp.sum(lq1.astype(f32) * lk1.astype(f32))) - jnp.exp(jnp.sum(lq2.astype(f32) * lk2.astype(f32))) + lam_init)
    q = jnp.transpose(q, (0, 2, 3, 1, 4)) * (DIFF_QDIM ** -0.5)
    k = jnp.transpose(k, (0, 2, 3, 1, 4))
    v = jnp.transpose(v, (0, 2, 1, 3))
    n_blocks = S // Q_BLOCK
    qb = jnp.moveaxis(q.reshape(B, DIFF_HEADS, 2, n_blocks, Q_BLOCK, DIFF_QDIM), 3, 0)
    key_pos = jnp.arange(S)

    def one_block(args):
        q_blk, i = args
        s = jnp.einsum('bhmqd,bhmkd->bhmqk', q_blk, k).astype(f32)
        q_pos = i * Q_BLOCK + jnp.arange(Q_BLOCK)
        s = jnp.where(key_pos[None, :] <= q_pos[:, None], s, -1e30)
        pr = jax.nn.softmax(s, axis=-1)
        attn = pr[:, :, 0] - lam * pr[:, :, 1]
        return jnp.einsum('bhqk,bhkd->bhqd', attn.astype(v.dtype), v)

    o = lax.map(one_block, (qb, jnp.arange(n_blocks)))
    o = jnp.transpose(o, (1, 0, 3, 2, 4)).reshape(B, S, DIFF_HEADS, DIFF_VDIM)
    o = rms_norm(o, subln_g) * (1 - lam_init)
    return o.reshape(B, S, DIFF_WIDTH)

def memory_cross_attention(h, m, wq, wkv, wo, q_g, k_g):
    B, S, _ = h.shape
    q = rms_norm((h @ wq).reshape(B, S, XATTN_HEADS, XATTN_HEAD), q_g)
    k, v = jnp.split(m @ wkv, 2, axis=-1)
    k = rms_norm(k.reshape(B, MEM_LEN, XATTN_HEADS, XATTN_HEAD), k_g)
    v = v.reshape(B, MEM_LEN, XATTN_HEADS, XATTN_HEAD)
    s = jnp.einsum('bqhd,bkhd->bhqk', q, k).astype(jnp.float32) * (XATTN_HEAD ** -0.5)
    pr = jax.nn.softmax(s, axis=-1)
    o = jnp.einsum('bhqk,bkhd->bqhd', pr.astype(v.dtype), v).reshape(B, S, D_MODEL)
    return o @ wo

def swiglu(h, w_gu, w_down):
    gate, up = jnp.split(h @ w_gu, 2, axis=-1)
    return (jax.nn.silu(gate) * up) @ w_down

def moe_swiglu(h, w_router, w_gu, w_down):
    logits = (h @ w_router).astype(jnp.float32)
    vals, idx = lax.top_k(logits, TOP_K)
    wts = jax.nn.softmax(vals, axis=-1)
    gates = jnp.einsum('bske,bsk->bse', jax.nn.one_hot(idx, N_EXPERTS, dtype=jnp.float32), wts).astype(h.dtype)
    out = jnp.zeros_like(h)
    for e in range(N_EXPERTS):
        out = out + gates[..., e:e + 1] * swiglu(h, w_gu[e], w_down[e])
    return out

def setup_inputs(seed: int = 0) -> dict:
    key = jax.random.key(seed)
    ks = iter(jax.random.split(key, 64))
    f32 = jnp.float32

    def nrm(shape, scale):
        return scale * jax.random.normal(next(ks), shape, f32)

    def gain(shape):
        return 1.0 + nrm(shape, 0.02)

    def unif(shape, lo, hi):
        return jax.random.uniform(next(ks), shape, f32, lo, hi)

    L, Lv = DEPTH, DEPTH - 1
    x = nrm((BATCH, SEQ, D_MODEL), 1.0)
    mem = nrm((BATCH, MEM_LEN, D_MODEL), 1.0)
    offsets = jax.random.randint(next(ks), (BATCH, 1), 0, 4096, dtype=jnp.int32)
    positions = offsets + jnp.arange(SEQ, dtype=jnp.int32)[None, :]
    return {
        "x": x,
        "mem": mem,
        "positions": positions,
        "mix_norm": gain((L, D_MODEL)),
        "in_proj": nrm((L, D_MODEL, IN_COLS), D_MODEL ** -0.5),
        "shift_mu": unif((L, RWKV_COLS), 0.0, 1.0),
        "decay_bias": unif((L, RWKV_WIDTH), -5.0, -1.0),
        "decay_up": nrm((L, DECAY_RANK, RWKV_WIDTH), 0.1 * DECAY_RANK ** -0.5),
        "iclr_bias": nrm((L, RWKV_WIDTH), 0.1),
        "iclr_up": nrm((L, ICLR_RANK, RWKV_WIDTH), ICLR_RANK ** -0.5),
        "gate_up": nrm((L, GATE_RANK, RWKV_WIDTH), GATE_RANK ** -0.5),
        "key_kk_scale": 0.85 + nrm((L, RWKV_WIDTH), 0.05),
        "key_iclr_scale": 1.0 + nrm((L, RWKV_WIDTH), 0.05),
        "bonus_rk": nrm((L, RWKV_HEADS, RWKV_HEAD), 0.1),
        "rwkv_gn_w": gain((L, RWKV_WIDTH)),
        "rwkv_gn_b": nrm((L, RWKV_WIDTH), 0.02),
        "vres_down": nrm((Lv, D_MODEL, VRES_RANK), D_MODEL ** -0.5),
        "vres_shift_mu": unif((Lv, VRES_RANK), 0.0, 1.0),
        "vres_bias": 0.5 + nrm((Lv, RWKV_WIDTH), 0.1),
        "vres_up": nrm((Lv, VRES_RANK, RWKV_WIDTH), 0.5 * VRES_RANK ** -0.5),
        "q_norm": gain((L, DIFF_QDIM)),
        "k_norm": gain((L, DIFF_QDIM)),
        "lambda_q1": nrm((L, DIFF_QDIM), 0.1),
        "lambda_k1": nrm((L, DIFF_QDIM), 0.1),
        "lambda_q2": nrm((L, DIFF_QDIM), 0.1),
        "lambda_k2": nrm((L, DIFF_QDIM), 0.1),
        "diff_subln": gain((L, DIFF_VDIM)),
        "out_proj": nrm((L, D_MODEL, D_MODEL), D_MODEL ** -0.5),
        "xattn_norm": gain((L, D_MODEL)),
        "mem_norm": gain((L, D_MODEL)),
        "xattn_wq": nrm((L, D_MODEL, D_MODEL), D_MODEL ** -0.5),
        "xattn_wkv": nrm((L, D_MODEL, 2 * D_MODEL), D_MODEL ** -0.5),
        "xattn_wo": nrm((L, D_MODEL, D_MODEL), D_MODEL ** -0.5),
        "xattn_q_norm": gain((L, XATTN_HEAD)),
        "xattn_k_norm": gain((L, XATTN_HEAD)),
        "ffn_norm": gain((L, D_MODEL)),
        "dense_w_gu": nrm((N_DENSE, D_MODEL, 2 * D_FF_DENSE), D_MODEL ** -0.5),
        "dense_w_down": nrm((N_DENSE, D_FF_DENSE, D_MODEL), D_FF_DENSE ** -0.5),
        "router": nrm((N_MOE, D_MODEL, N_EXPERTS), D_MODEL ** -0.5),
        "expert_w_gu": nrm((N_MOE, N_EXPERTS, D_MODEL, 2 * D_FF_EXPERT), D_MODEL ** -0.5),
        "expert_w_down": nrm((N_MOE, N_EXPERTS, D_FF_EXPERT, D_MODEL), D_FF_EXPERT ** -0.5),
    }

def reference(x, mem, positions, mix_norm, in_proj, shift_mu, decay_bias, decay_up, iclr_bias, iclr_up, gate_up,
              key_kk_scale, key_iclr_scale, bonus_rk, rwkv_gn_w, rwkv_gn_b, vres_down, vres_shift_mu, vres_bias,
              vres_up, q_norm, k_norm, lambda_q1, lambda_k1, lambda_q2, lambda_k2, diff_subln, out_proj, xattn_norm,
              mem_norm, xattn_wq, xattn_wkv, xattn_wo, xattn_q_norm, xattn_k_norm, ffn_norm, dense_w_gu,
              dense_w_down, router, expert_w_gu, expert_w_down):
    f32 = jnp.float32
    inv_freq = ROPE_THETA ** (-jnp.arange(0, ROPE_DIMS, 2, dtype=f32) / ROPE_DIMS)
    ang = positions.astype(f32)[..., None] * inv_freq
    cos = jnp.cos(ang)[:, :, None, None, :].astype(x.dtype)
    sin = jnp.sin(ang)[:, :, None, None, :].astype(x.dtype)
    v_first = None
    for l in range(DEPTH):
        h = rms_norm(x, mix_norm[l])
        w_in = in_proj[l] if l == 0 else jnp.concatenate([in_proj[l], vres_down[l - 1]], axis=1)
        proj = h @ w_in
        p_rwkv = token_shift(proj[..., :RWKV_COLS], shift_mu[l])
        p_diff = proj[..., RWKV_COLS:IN_COLS]
        v_mix_logit = None
        if l > 0:
            v_mix_logit = vres_bias[l - 1] + token_shift(proj[..., IN_COLS:], vres_shift_mu[l - 1]) @ vres_up[l - 1]
        y_rwkv, v_l = rwkv7_time_mix(p_rwkv, v_first, v_mix_logit, decay_bias[l], decay_up[l], iclr_bias[l],
                                     iclr_up[l], gate_up[l], key_kk_scale[l], key_iclr_scale[l], bonus_rk[l],
                                     rwkv_gn_w[l], rwkv_gn_b[l])
        if l == 0:
            v_first = v_l
        lam_init = 0.8 - 0.6 * math.exp(-0.3 * l)
        y_diff = diff_attention(p_diff, cos, sin, q_norm[l], k_norm[l], lambda_q1[l], lambda_k1[l], lambda_q2[l],
                                lambda_k2[l], diff_subln[l], lam_init)
        x = x + jnp.concatenate([y_rwkv, y_diff], axis=-1) @ out_proj[l]
        h = rms_norm(x, xattn_norm[l])
        m = rms_norm(mem, mem_norm[l])
        x = x + memory_cross_attention(h, m, xattn_wq[l], xattn_wkv[l], xattn_wo[l], xattn_q_norm[l], xattn_k_norm[l])
        h = rms_norm(x, ffn_norm[l])
        if l % 2 == 0:
            x = x + swiglu(h, dense_w_gu[l // 2], dense_w_down[l // 2])
        else:
            x = x + moe_swiglu(h, router[l // 2], expert_w_gu[l // 2], expert_w_down[l // 2])
    return x


_drawn_inputs = setup_inputs


def setup_inputs(seed=0):
    import zlib

    import numpy as np

    out = dict(_drawn_inputs(seed))
    spreads = {}
    factors = {'decay_up': 8.0,
     'xattn_norm': 5.12,
     'mem_norm': 4.746,
     'xattn_q_norm': 8.0,
     'xattn_k_norm': 3.64,
     'vres_bias': 3.944,
     'ffn_norm': 3.468}
    for name, (base, spread) in spreads.items():
        noise = np.random.default_rng([zlib.crc32(name.encode()), seed]).standard_normal(out[name].shape)
        drawn = base * np.exp(spread * noise) if base else spread * noise
        out[name] = __import__('jax').numpy.asarray(drawn.astype(out[name].dtype))
    for name, factor in factors.items():
        out[name] = (out[name] * factor).astype(out[name].dtype)
    return out
```

```python
import concourse.bass as bass
from concourse import mybir
from contextlib import ExitStack
import math

P = 128
D = 1024
SEQ = 256
TT = SEQ // P
KD = D // P
DEPTH = 2
EPS = 1e-6
RW, RH, HD = 512, 8, 64
GN_EPS = 64e-5
LORA = 256
RC = 3 * RW + LORA
VR = 32
DH, DV, DQ = 4, 128, 64
ROPE = 16
XH, XD = 4, 256
FD, FE, NE = 2816, 3584, 8
CH = 64
NOVER = 3
NITEM = NE + NOVER
RING, BLK = 6, 2048
DVE_STEPS = 1
FC = 256
DEC = -math.exp(-0.5)

VEC = {}
_at = 0
for _n, _w in (("mu", RC), ("vmu", VR), ("decay_b", RW), ("iclr_b", RW), ("kk_s", RW), ("ka_s", RW), ("bonus", RW),
               ("gn_w", RW), ("gn_b", RW), ("vres_b", RW), ("q_norm", DQ), ("k_norm", DQ), ("lq1", DQ), ("lq2", DQ),
               ("lk1", DQ), ("lk2", DQ), ("subln", DV)):
    VEC[_n] = (_at, _w)
    _at += _w
NV = _at
COL = {"mix": 0, "xattn": 8, "mem": 16, "ffn": 24, "xq": 32, "xk": 40}
NCOL = 48
CST = {}
_at = 0
for _n, _w in (("ident", P), ("mask_in", 256), ("lvl", 5 * P), ("neg1", P), ("neg1T", P), ("tri", P), ("tri_s", P),
               ("causal", 384), ("bd", P), ("last", 2), ("ones", P), ("utri", P), ("iota", P), ("freq", 8)):
    CST[_n] = (_at, _w)
    _at += _w
NCST = _at


class Banks:

    def __init__(self, psum, ready, evacuated):
        self.psum, self.ready, self.evacuated = psum, ready, evacuated
        self.n, self.use = [0] * 8, {}

    def open(self, pe, name, bank, more=0):
        self.use[name] = (bank, self.n[bank])
        if self.n[bank]:
            pe.wait_ge(self.evacuated[bank], self.n[bank] + more)
        self.n[bank] += 1
        return self.psum[bank]

    def filled(self, last, name):
        last.then_inc(self.ready[self.use[name][0]], 1)

    def wait_filled(self, eng, name, more=0):
        bank, nth = self.use[name]
        eng.wait_ge(self.ready[bank], nth + 1 + more)
        return self.psum[bank]

    def wait_evacuated(self, eng, name, more=0):
        bank, nth = self.use[name]
        eng.wait_ge(self.evacuated[bank], nth + 1 + more)

    def release(self, ins, name):
        ins.then_inc(self.evacuated[self.use[name][0]], 1)


def decoder_trunk(nc, x_in, mem_in, pos_in, vecs, cols, consts, in_proj, decay_up, iclr_up, gate_up, vres_down, vres_up,
                  out_proj, wq, wkv, wo, dense_gu, dense_down, router, expert_gu, expert_down, out):
    F32, I32, U32 = mybir.dt.float32, mybir.dt.int32, mybir.dt.uint32
    ACT, ALU, AX = mybir.ActivationFunctionType, mybir.AluOpType, mybir.AxisListType
    MUL, ADD, SUB = ALU.mult, ALU.add, ALU.subtract

    ctx = ExitStack()
    with ctx:
        def sb(name, shape, dt=F32):
            return ctx.enter_context(nc.sbuf_tensor(name, shape, dt))

        def sem(name):
            return ctx.enter_context(nc.semaphore(name))

        ring = sb("ring", [P, RING, BLK])
        x = sb("x", [P, TT, D])
        v_first = sb("v_first", [P, TT, RW])
        vec = sb("vec", [P, NV])
        col = sb("col", [P, DEPTH, NCOL])
        lora_w = sb("lora_w", [P, RW])
        gate_w = sb("gate_w", [P, RW])
        vres_w = sb("vres_w", [VR, RW])
        vresd_w = sb("vresd_w", [P, KD, VR])
        router_w = sb("router_w", [P, KD, NE])
        cst = sb("cst", [P, NCST])
        proj = sb("proj", [P, TT * (RC + VR)])
        dproj = sb("dproj", [P, TT, 3 * RW])
        NB = sb("NB", [P, 9, 1024])
        SH = sb("SH", [P, 4096])
        hN = sb("hN", [P, 2048])
        hT = sb("hT", [P, 2048])
        W1 = sb("W1", [P, 1024])
        state = sb("state", [P, 4, P])
        keep = sb("keep", [P, 4, P])
        rope = sb("rope", [P, 4, TT * 8])
        posi = sb("posi", [P, TT], I32)
        st = sb("st", [P, 192])
        psum = [ctx.enter_context(nc.psum_tensor(f"psum{b}", [P, 512], F32)) for b in range(8)]

        def C(name):
            a, w = CST[name]
            return cst[:, a:a + w]

        def V(name):
            a, w = VEC[name]
            return vec[:, a:a + w]

        def bc(ap, *shape):
            return ap.to_broadcast([P, *shape])

        ident = C("ident")
        pv = proj[:, :].rearrange("p (t c) -> p t c", t=TT)
        prev = SH[:, 0:TT * (RC + VR)].rearrange("p (t c) -> p t c", t=TT)
        nbf = NB[:, :, :].rearrange("p a b -> p (a b)")

        def nb(i):
            return NB[:, i, :].rearrange("p (t c) -> p t c", t=TT)
        A_, G_, EC, ENC, ECP, KK, B_, RHO, TMP = range(9)
        hNv = hN[:, :].rearrange("p (t c) -> p t c", t=TT)
        hTv = hT[:, :].rearrange("p (k t) -> p k t", k=KD)
        arT = hN[:, 0:1024].rearrange("p (b q t) -> p b q t", b=4, q=2)
        bT = hN[:, 1024:1536].rearrange("p (b t) -> p b t", b=4)
        kT = hN[:, 1536:2048].rearrange("p (b t) -> p b t", b=4)
        mats = SH[:, :].rearrange("p (h q t) -> p h q t", h=8, q=4)
        Tm = hT[:, 0:1024].rearrange("p (h t) -> p h t", h=8)
        TTm = hT[:, 1024:2048].rearrange("p (h t) -> p h t", h=8)
        Xm = NB[:, KK, :].rearrange("p (h t) -> p h t", h=8)
        Cm = NB[:, A_, :].rearrange("p (h t) -> p h t", h=8)
        aiT = W1[:, 0:512].rearrange("p (b t) -> p b t", b=4)
        U_ = W1[:, 512:1024]
        SA0 = NB[:, TMP, 0:512]
        SA = NB[:, TMP, 512:1024]
        yraw = nb(EC)
        lT = W1[:, 0:512].rearrange("p (b t) -> p b t", b=2)
        vrT = U_[0:VR, 0:256]
        sb_items = sb("items", [1, 4], I32)
        ss, ss2, rst, rtmp = st[:, 0:32], st[:, 32:64], st[:, 64:96], st[:, 96:128]
        sm = st[:, 128:192]

        ready = [sem(f"psum_ready{b}") for b in range(8)]
        evacuated = [sem(f"psum_evacuated{b}") for b in range(8)]
        B = Banks(psum, ready, evacuated)
        block_in = [sem(f"block_in{s}") for s in range(RING)]
        block_used = sem("block_used")
        x_in_s, small_in, vec_in, mem_in_s, out_s = sem("x_in"), sem("small_in"), sem("vec_in"), sem("mem_in"), sem("out_s")
        lw_in = sem("layer_weights_in")
        dve_step, act_step, pool_step = sem("dve_step"), sem("act_step"), sem("pool_step")
        sq_done, hn_done = sem("squares_done"), sem("normed")
        msq_done, mn_done = sem("mem_squares_done"), sem("mem_normed")
        shifted_in = [sem(f"shifted_in{g}") for g in range(5)]
        row0_ready, lora_ready, sg_scan, rate_done, vmix_done = (sem("row0_cleared"), sem("lora_shifted"), sem("decay_sigmoid"),
                                                                 sem("rate_sigmoid"), sem("value_mix_sigmoid"))
        v_final, expc, elem, qs_ready = sem("v_final"), sem("exp_cum_done"), sem("recurrence_inputs"), sem("qk_roped")
        c_ready, t_ready, state_ready, sa_ready = sem("C_masked"), sem("T_started"), sem("state_ready"), sem("SA_ready")
        keep_ready, ycat, smx, pexp, attn_ready = sem("keep_ready"), sem("y_cat"), sem("row_max"), sem("p_exp"), sem("attn_ready")
        lam_in, lam_exp, rope_in, rope_sin = sem("lambda_in"), sem("lambda_exp"), sem("rope_in"), sem("rope_sin")
        xq_n, xk_n, xs_mx = sem("xq_normed"), sem("xk_normed"), sem("x_row_max")
        silu_done, w_in, w_sig, rt_sel, items_in = sem("silu_done"), sem("gate_in"), sem("gate_sigmoid"), sem("selected"), sem("items_ready")
        sel_done, final = sem("selection_done"), sem("final")

        def rows(w, k0, c0, cw):
            return w[k0 * P:(k0 + 4) * P, c0:c0 + cw].rearrange("(k p) n -> p k n", p=P)
        chunks_in = [(0, 512), (512, 512), (1024, 512), (1536, 256), (1792, 512), (2304, 512), (2816, 512)]

        def square_blocks(w, cs):
            return [("w", rows(w, k0, c0, cw), cw) for c0, cw in cs for k0 in (0, 4)]

        def half_chunks(n):
            return [(c * 512, 512) for c in range(n)]

        def gu_block(w, c, g):
            c0 = g * (w.shape[-1] // 2) + c * FC
            return w[:, c0:c0 + FC].rearrange("(k p) f -> p k f", p=P)

        def down_block(w, c):
            return w[c * FC:(c + 1) * FC, :].rearrange("(k p) n -> p k n", p=P)

        blocks = []
        for l in range(DEPTH):
            blocks += square_blocks(in_proj[l], chunks_in)
            blocks += square_blocks(out_proj[l], half_chunks(2))
            blocks += square_blocks(wq[l], half_chunks(2))
            blocks += square_blocks(wkv[l], half_chunks(4))
            blocks += square_blocks(wo[l], half_chunks(2))
            if l == 0:
                for c in range(FD // FC + 1):
                    if c < FD // FC:
                        blocks += [("gu", gu_block(dense_gu[0], c, g), 0) for g in (0, 1)]
                    if c:
                        blocks.append(("down", down_block(dense_down[0], c - 1), 0))
        NPRE = len(blocks)
        STEPS = FE // FC
        PER = 3 * STEPS
        assert PER % RING == 0

        def slot_view(s, kind, cw):
            if kind == "gu":
                return ring[:, s, :].rearrange("p (k f) -> p k f", k=KD)
            if kind == "down":
                return ring[:, s, :].rearrange("p (k n) -> p k n", k=2)
            return ring[:, s, 0:4 * cw].rearrange("p (k n) -> p k n", k=4)

        MOE_PER = [STEPS // 2, STEPS // 2, STEPS, 1, 1, 1, 3, 3]
        MOE_USED = 2 * STEPS - 1
        freed = []

        block = ctx.enter_context(nc.Block())

        @block.tensor
        def _(pe):
            at = [0]
            n_used = [0]
            work = [0]

            def take(kind, cw=512):
                n = at[0]
                at[0] += 1
                pe.wait_ge(block_in[n % RING], 16 * (n // RING + 1))
                return slot_view(n % RING, kind, cw)

            def used(last):
                last.then_inc(block_used, 1)
                n_used[0] += 1
                freed.append((block_used, n_used[0], MOE_USED))

            def used_with(name):
                bank, nth = B.use[name]
                freed.append((ready[bank], nth + 1, MOE_PER[bank]))

            def open_work(name):
                work[0] += 1
                return B.open(pe, name, 4 + (work[0] - 1) % 4)
            nproj = [0]

            def transposes(name, srcs, opener=None):
                bank = (opener or open_work)(name)
                for i, s in enumerate(srcs):
                    n = s.shape[0]
                    m = s.shape[1]
                    last = pe.transpose(bank[0:m, i * P:i * P + n], s, ident[0:n, 0:n])
                B.filled(last, name)

            def to_hT(name, src, wait):
                for t in range(TT):
                    wait(t)
                    for g in range(2):
                        transposes((*name, t, g), [src[:, t, (4 * g + i) * P:(4 * g + i + 1) * P] for i in range(4)])

            def project(name, src, n_cols, src_ready):
                for c, (c0, cw) in enumerate(n_cols):
                    banks = []
                    for t in range(TT):
                        banks.append(B.open(pe, (*name, c, t), nproj[0] % 4))
                        nproj[0] += 1
                    if c == 0:
                        src_ready()
                    for half in range(2):
                        w = take("w", cw)
                        for t in range(TT):
                            for k in range(4):
                                kk = half * 4 + k
                                last = pe.matmul(banks[t][:, 0:cw], src(kk, t), w[:, k, :], start=(kk == 0), stop=(kk == 7))
                            if half:
                                B.filled(last, (*name, c, t))
                        if half == 0:
                            used(last)
                        else:
                            used_with((*name, c, TT - 1))

            pe.wait_ge(small_in, 48)

            def lhs_h(kk, t):
                return hTv[:, kk, t * P:(t + 1) * P]

            def h_ready(name):
                def wait():
                    for t in range(TT):
                        for g in range(2):
                            B.wait_evacuated(pe, (*name, t, g))
                return wait

            for l in range(DEPTH):
                to_hT(("hT", l, 0), hNv, lambda t: pe.wait_ge(hn_done, 2 * 3 * l + t + 1))
                project(("in", l), lhs_h, chunks_in, h_ready(("hT", l, 0)))
                if l:
                    pe.wait_ge(lw_in, 96 + 48 * l)
                    for t in range(TT):
                        bank = B.open(pe, ("vr", l, t), nproj[0] % 4)
                        nproj[0] += 1
                        for k in range(KD):
                            last = pe.matmul(bank[:, 0:VR], lhs_h(k, t), vresd_w[:, k, :], start=(k == 0), stop=(k == 7))
                        B.filled(last, ("vr", l, t))
                pe.wait_ge(lora_ready, l + 1)
                transposes(("lt", l), [pv[:, t, 1536 + b * P:1536 + (b + 1) * P] for b in range(2) for t in range(TT)])
                if l:
                    pe.wait_ge(lora_ready, l + 2)
                    transposes(("vt", l), [pv[:, t, RC:RC + VR] for t in range(TT)])
                pe.wait_ge(lw_in, 96 + 48 * l)
                B.wait_evacuated(pe, ("lt", l))
                for t in range(TT):
                    ts = slice(t * P, (t + 1) * P)
                    for name, lhs, rhs in (("wup", lT[0:64, 0, ts], lora_w[0:64, :]), ("aup", lT[64:128, 0, ts], lora_w[64:128, :]),
                                           ("gup", lT[:, 1, ts], gate_w[:, :])):
                        bank = open_work((name, l, t))
                        B.filled(pe.matmul(bank[:, :], lhs, rhs, start=True, stop=True), (name, l, t))
                    if l:
                        if t == 0:
                            B.wait_evacuated(pe, ("vt", l))
                        bank = open_work(("vup", l, t))
                        B.filled(pe.matmul(bank[:, :], vrT[:, ts], vres_w[:, :], start=True, stop=True), ("vup", l, t))
                for t in range(TT):
                    pe.wait_ge(sg_scan, TT * l + t + 1)
                    for name, m in (("cum", C("tri")), ("cums", C("tri_s"))):
                        bank = open_work((name, l, t))
                        B.filled(pe.matmul(bank[:, :], m, nb(TMP)[:, t, :], start=True, stop=True), (name, l, t))
                pe.wait_ge(expc, 2 * l + 2)
                bank = open_work(("wt", l))
                for t in range(TT):
                    for b in range(4):
                        last = pe.matmul(bank[:, (t * 4 + b) * 2:(t * 4 + b) * 2 + 2], nb(EC)[:, t, b * P:(b + 1) * P], C("last"),
                                         start=True, stop=True)
                B.filled(last, ("wt", l))

                for t in range(TT):
                    pe.wait_ge(elem, l + 1)
                    for name, q in (("aT", ECP), ("rT", RHO), ("bT", B_), ("kT", ENC)):
                        transposes((name, l, t), [nb(q)[:, t, b * P:(b + 1) * P] for b in range(4)])
                    for name in ("aT", "rT", "bT", "kT"):
                        B.wait_evacuated(pe, (name, l, t))
                    for h in (0, 2, 4, 6, 1, 3, 5, 7):
                        b, r = h // 2, slice(64 * (h % 2), 64 * (h % 2) + 64)
                        bank = open_work(("m12", l, t, h))
                        pe.matmul(bank[:, 0:256], bT[r, b, :], arT[r, b, :, :].rearrange("p q t -> p (q t)"), start=True, stop=True)
                        B.filled(pe.matmul(bank[:, 256:512], kT[r, b, :], arT[r, b, :, :].rearrange("p q t -> p (q t)"),
                                           start=True, stop=True), ("m12", l, t, h))
                    for par in range(2):
                        r = slice(64 * par, 64 * par + 64)
                        bank = open_work(("m3", l, t, par))
                        for b in range(4):
                            last = pe.matmul(bank[:, b * P:(b + 1) * P], arT[r, b, 0, :], bT[r, b, :], start=True, stop=True)
                        B.filled(last, ("m3", l, t, par))
                    for par in range(2):
                        for h in range(par, 8, 2):
                            B.wait_evacuated(pe, ("m12", l, t, h))
                    bank = open_work(("U", l, t))
                    for h in range(8):
                        last = pe.matmul(bank[:, h * HD:(h + 1) * HD], mats[:, h, 2, :], pv[:, t, 2 * RW + h * HD:2 * RW + (h + 1) * HD],
                                         start=True, stop=True)
                    B.filled(last, ("U", l, t))
                    for lv in range(5):
                        for g in range(2):
                            pe.wait_ge(c_ready, 10 * (TT * l + t) + lv * 2 + g + 1)
                            if lv == 0:
                                pe.wait_ge(t_ready, TT * l + t + 1)
                            else:
                                B.wait_evacuated(pe, ("Z", l, t, lv - 1, g))
                                B.wait_evacuated(pe, ("ZT", l, t, lv - 1, g))
                            bank = open_work(("X", l, t, lv, g))
                            for h in range(4 * g, 4 * g + 4):
                                last = pe.matmul(bank[:, (h % 4) * P:(h % 4 + 1) * P], Cm[:, h, :], Tm[:, h, :], start=True, stop=True)
                            B.filled(last, ("X", l, t, lv, g))
                        for g in range(2):
                            B.wait_evacuated(pe, ("X", l, t, lv, g))
                            if lv < 4:
                                bank = open_work(("Z", l, t, lv, g))
                                for h in range(4 * g, 4 * g + 4):
                                    last = pe.matmul(bank[:, (h % 4) * P:(h % 4 + 1) * P], TTm[:, h, :], Xm[:, h, :], start=True, stop=True)
                                B.filled(last, ("Z", l, t, lv, g))
                            bank = open_work(("ZT", l, t, lv, g))
                            for h in range(4 * g, 4 * g + 4):
                                last = pe.matmul(bank[:, (h % 4) * P:(h % 4 + 1) * P], Xm[:, h, :], TTm[:, h, :], start=True, stop=True)
                            B.filled(last, ("ZT", l, t, lv, g))
                    for g in range(2):
                        B.wait_evacuated(pe, ("ZT", l, t, 4, g))
                    for par in range(2):
                        bank = open_work(("ai", l, t, par))
                        for h in range(par, 8, 2):
                            last = pe.matmul(bank[64 * par:64 * par + 64, (h // 2) * P:(h // 2 + 1) * P],
                                             nb(ECP)[:, t, h * HD:(h + 1) * HD], TTm[:, h, :], start=True, stop=True)
                        B.filled(last, ("ai", l, t, par))
                    B.wait_evacuated(pe, ("U", l, t))
                    bank = open_work(("SA0", l, t))
                    for h in range(8):
                        last = pe.matmul(bank[:, h * HD:(h + 1) * HD], TTm[:, h, :], U_[:, h * HD:(h + 1) * HD], start=True, stop=True)
                    B.filled(last, ("SA0", l, t))
                    for par in range(2):
                        B.wait_evacuated(pe, ("ai", l, t, par))
                    ybank = None
                    for p in range(2):
                        tk = slice(64 * p, 64 * p + 64)
                        n = 2 * (TT * l + t) + p
                        pe.wait_ge(state_ready, n + l + 1)
                        bank = open_work(("sa", l, t, p))
                        for b in range(4):
                            last = pe.matmul(bank[tk, b * P:(b + 1) * P], aiT[:, b, tk], state[:, b, :], start=True, stop=True)
                        B.filled(last, ("sa", l, t, p))
                        bank = open_work(("y1", l, t, p))
                        for b in range(4):
                            last = pe.matmul(bank[tk, b * P:(b + 1) * P], arT[:, b, 1, tk], state[:, b, :], start=True, stop=True)
                        B.filled(last, ("y1", l, t, p))
                        bank = open_work(("s", l, t, p))
                        pe.wait_ge(sa_ready, n + 1)
                        for b in range(4):
                            cs = slice(b * P, (b + 1) * P)
                            pe.matmul(bank[:, cs], nb(ENC)[tk, t, cs], pv[tk, t, 2 * RW + b * P:2 * RW + (b + 1) * P], start=True, stop=False)
                            last = pe.matmul(bank[:, cs], nb(B_)[tk, t, cs], SA[tk, cs], start=False, stop=True)
                        B.filled(last, ("s", l, t, p))
                    bank = open_work(("y2", l, t))
                    for h in range(8):
                        hs = slice(h * HD, (h + 1) * HD)
                        pe.matmul(bank[:, hs], mats[:, h, 1, :], SA[:, hs], start=True, stop=False)
                        last = pe.matmul(bank[:, hs], mats[:, h, 3, :], pv[:, t, 2 * RW + h * HD:2 * RW + (h + 1) * HD],
                                         start=False, stop=True)
                    B.filled(last, ("y2", l, t))

                qT = hT[:, 0:1024].rearrange("p (h t) -> p h t", h=4)
                kTd = hT[:, 1024:2048].rearrange("p (h t) -> p h t", h=4)
                pe.wait_ge(qs_ready, l + 1)
                for which in range(2):
                    for t in range(TT):
                        transposes(("qkT", l, which, t), [dproj[:, t, which * RW + h * P:which * RW + (h + 1) * P] for h in range(4)])
                for which in range(2):
                    for t in range(TT):
                        B.wait_evacuated(pe, ("qkT", l, which, t))
                aT = W1[:, :].rearrange("p (s n) -> p s n", s=2)

                def diff_scores(h):
                    for m in range(2):
                        r = slice(64 * m, 64 * m + 64)
                        bank = open_work(("ds", l, h, m))
                        pe.matmul(bank[:, 0:128], qT[r, h, 0:128], kTd[r, h, 0:128], start=True, stop=True)
                        B.filled(pe.matmul(bank[:, 128:384], qT[r, h, 128:256], kTd[r, h, :], start=True, stop=True), ("ds", l, h, m))
                diff_scores(0)
                for h in range(4):
                    if h < 3:
                        diff_scores(h + 1)
                    pe.wait_ge(attn_ready, 4 * l + h + 1)
                    bank = open_work(("atT", l, h))
                    att = SH[:, 2304 + 384 * (h % 2):2304 + 384 * (h % 2) + 384]
                    for i in range(3):
                        last = pe.transpose(bank[:, i * P:(i + 1) * P], att[:, i * P:(i + 1) * P], ident)
                    B.filled(last, ("atT", l, h))
                    B.wait_evacuated(pe, ("atT", l, h))
                    bank = open_work(("pv", l, h))
                    vv = [dproj[:, t, 2 * RW + h * DV:2 * RW + (h + 1) * DV] for t in range(TT)]
                    pe.matmul(bank[:, 0:128], aT[:, h % 2, 0:128], vv[0], start=True, stop=True)
                    pe.matmul(bank[:, 128:256], aT[:, h % 2, 128:256], vv[0], start=True, stop=False)
                    B.filled(pe.matmul(bank[:, 128:256], aT[:, h % 2, 256:384], vv[1], start=False, stop=True), ("pv", l, h))
                to_hT(("hT", l, 1), hNv, lambda t: pe.wait_ge(ycat, 2 * l + 2))
                project(("op", l), lhs_h, half_chunks(2), h_ready(("hT", l, 1)))

                to_hT(("hT", l, 2), hNv, lambda t: pe.wait_ge(hn_done, 2 * (3 * l + 1) + t + 1))
                project(("xq", l), lhs_h, half_chunks(2), h_ready(("hT", l, 2)))
                memn = nbf[:, 4096:6144].rearrange("p (t c) -> p t c", t=TT)
                mT = nbf[:, 6144:8192].rearrange("p (k t) -> p k t", k=KD)
                to_hT(("mT", l), memn, lambda t: pe.wait_ge(mn_done, 2 * l + t + 1))
                project(("kv", l), lambda kk, t: mT[:, kk, t * P:(t + 1) * P], half_chunks(4), h_ready(("mT", l)))
                qn = proj[:, 0:2048].rearrange("p (t c) -> p t c", t=TT)
                kn = dproj[:, :, :].rearrange("p t c -> p (t c)")[:, 0:2048].rearrange("p (t c) -> p t c", t=TT)
                vx = SH[:, 0:2048].rearrange("p (t c) -> p t c", t=TT)
                kTx = nbf[:, 0:2048].rearrange("p (k t) -> p k t", k=KD)
                qTx = nbf[:, 2048:4096].rearrange("p (k t) -> p k t", k=KD)
                to_hT(("xqT", l), qn, lambda t: pe.wait_ge(xq_n, l + 1))
                to_hT(("xkT", l), kn, lambda t: pe.wait_ge(xk_n, l + 1))
                h_ready(("xqT", l))()
                h_ready(("xkT", l))()
                PT = nbf[:, 8192:9216].rearrange("p (s n) -> p s n", s=2)
                px = SH[:, 2048:3072].rearrange("p (s q k) -> p s q k", s=2, q=2)

                def x_scores(h):
                    bank = open_work(("xs", l, h))
                    for t in range(TT):
                        for kb in range(2):
                            last = pe.matmul(bank[:, t * 256:(t + 1) * 256], qTx[:, 2 * h + kb, t * P:(t + 1) * P], kTx[:, 2 * h + kb, :],
                                             start=(kb == 0), stop=(kb == 1))
                    B.filled(last, ("xs", l, h))
                x_scores(0)
                for h in range(XH):
                    if h < XH - 1:
                        x_scores(h + 1)
                    B.wait_evacuated(pe, ("xs", l, h))
                    transposes(("xpT", l, h), [px[:, h % 2, q, m * P:(m + 1) * P] for m in range(2) for q in range(2)])
                    B.wait_evacuated(pe, ("xpT", l, h))
                    bank = open_work(("xo", l, h))
                    for q in range(TT):
                        for m in range(2):
                            last = pe.matmul(bank[:, q * 256:(q + 1) * 256], PT[:, h % 2, (m * 2 + q) * P:(m * 2 + q + 1) * P],
                                             vx[:, m, h * XD:(h + 1) * XD], start=(m == 0), stop=(m == 1))
                    B.filled(last, ("xo", l, h))
                on = memn
                to_hT(("oT", l), on, lambda t: [B.wait_evacuated(pe, ("xo", l, h)) for h in range(XH)])
                project(("wo", l), lhs_h, half_chunks(2), h_ready(("oT", l)))

                to_hT(("hT", l, 3), hNv, lambda t: pe.wait_ge(hn_done, 2 * (3 * l + 2) + t + 1))
                if l == 0:
                    h_ready(("hT", l, 3))()
                    nch = FD // FC
                    ybanks = []
                    act = nbf[:, 0:1024].rearrange("p (s t n) -> p s t n", s=2, t=2)
                    actT = nbf[:, 1024:1536].rearrange("p (k t) -> p k t", k=2)

                    def hidden_T(c):
                        bank = B.open(pe, ("fT", c), 2 + c % 2)
                        for k in range(2):
                            for t in range(TT):
                                if k == 0:
                                    B.wait_evacuated(pe, ("gu", c, t))
                                last = pe.transpose(bank[:, (k * 2 + t) * P:(k * 2 + t + 1) * P], act[:, c % 2, t, k * P:(k + 1) * P], ident)
                        B.filled(last, ("fT", c))

                    def down(c):
                        w = take("down")
                        B.wait_evacuated(pe, ("fT", c))
                        if c == 0:
                            ybanks.extend(B.open(pe, ("fy", i), 4 + i) for i in range(4))
                        for t in range(TT):
                            for n in range(2):
                                for k in range(2):
                                    last = pe.matmul(ybanks[t * 2 + n][:, :], actT[:, k, t * P:(t + 1) * P], w[:, k, n * 512:(n + 1) * 512],
                                                     start=(c == 0 and k == 0), stop=(c == nch - 1 and k == 1), skip_group_check=True)
                                if c == nch - 1 and (t, n) != (1, 1):
                                    B.filled(last, ("fy", t * 2 + n))
                        if c == nch - 1:
                            B.filled(last, ("fy", 3))
                            used_with(("fy", 3))
                        else:
                            used(last)
                    for c in range(nch):
                        banks = [B.open(pe, ("gu", c, t), t) for t in range(TT)]
                        for half in range(2):
                            w = take("gu")
                            for t in range(TT):
                                for k in range(KD):
                                    last = pe.matmul(banks[t][:, half * FC:(half + 1) * FC], lhs_h(k, t), w[:, k, :],
                                                     start=(k == 0), stop=(k == 7))
                                if half:
                                    B.filled(last, ("gu", c, t))
                            if half == 0:
                                used(last)
                                if c:
                                    hidden_T(c - 1)
                            else:
                                used_with(("gu", c, TT - 1))
                        if c:
                            down(c - 1)
                    hidden_T(nch - 1)
                    down(nch - 1)

            assert at[0] == NPRE == len(freed)
            l = 1
            h_ready(("hT", l, 3))()
            pe.wait_ge(lw_in, 64 * DEPTH)
            bank = B.open(pe, ("logit",), 6)
            for t in range(TT):
                for k in range(KD):
                    last = pe.matmul(bank[:, t * NE:(t + 1) * NE], lhs_h(k, t), router_w[:, k, :], start=(k == 0), stop=(k == KD - 1))
            B.filled(last, ("logit",))
            sel = nbf[:, 8192:8192 + 2 * NE].rearrange("p (t e) -> p t e", t=TT)
            pe.wait_ge(rt_sel, 1)
            bank = B.open(pe, ("pos",), 7)
            pe.matmul(bank[:, 0:8], C("utri"), sel[:, 0, :], start=True, stop=True)
            pe.matmul(bank[:, 8:16], C("ones"), sel[:, 0, :], start=True, stop=False)
            pe.matmul(bank[:, 8:16], C("utri"), sel[:, 1, :], start=False, stop=True)
            pe.matmul(bank[:, 16:24], C("ones"), sel[:, 0, :], start=True, stop=False)
            B.filled(pe.matmul(bank[:, 16:24], C("ones"), sel[:, 1, :], start=False, stop=True), ("pos",))

            start, start_used = list(B.n), n_used[0]

            def expert(i):
                B.n = list(start)
                n_used[0] = start_used
                del freed[NPRE:]

                def more(bank):
                    return i * MOE_PER[bank]

                def open_(name, bank):
                    return B.open(pe, name, bank, more(bank))

                def take_e(j, kind):
                    n = NPRE + j
                    pe.wait_ge(block_in[n % RING], 16 * (n // RING + 1) + i * (16 * PER // RING))
                    return slot_view(n % RING, kind, 512)
                pe.wait_ge(sel_done, i * 2 + 1)
                Psel = nbf[:, 2048:2304].rearrange("p (t j) -> p t j", t=TT)
                Pg = nbf[:, 2304:2560].rearrange("p (t j) -> p t j", t=TT)
                PgT = nbf[:, 2560:2816]
                heT = nbf[:, 3072:4096].rearrange("p (k j) -> p k j", k=KD)
                for g in range(2):
                    bank = open_(("he", g), 6 + g)
                    for k in range(4):
                        for t in range(TT):
                            last = pe.matmul(bank[:, k * P:(k + 1) * P], hNv[:, t, (4 * g + k) * P:(4 * g + k + 1) * P], Psel[:, t, :],
                                             start=(t == 0), stop=(t == 1))
                    B.filled(last, ("he", g))
                pe.wait_ge(sel_done, i * 2 + 2)
                bank = open_(("pgT",), 3)
                for t in range(TT):
                    last = pe.transpose(bank[:, t * P:(t + 1) * P], Pg[:, t, :], ident)
                B.filled(last, ("pgT",))
                for g in range(2):
                    B.wait_evacuated(pe, ("he", g), more(6 + g))
                act = nbf[:, 0:512].rearrange("p (s n) -> p s n", s=2)
                actT = nbf[:, 512:768].rearrange("p (k t) -> p k t", k=2)
                ybanks = []

                def hidden_T(c):
                    bank = open_(("eT", c), 2)
                    B.wait_evacuated(pe, ("egu", c), more(c % 2))
                    for k in range(2):
                        last = pe.transpose(bank[:, k * P:(k + 1) * P], act[:, c % 2, k * P:(k + 1) * P], ident)
                    B.filled(last, ("eT", c))

                def down(c):
                    w = take_e(3 * c + (4 if c < STEPS - 1 else 2), "down")
                    B.wait_evacuated(pe, ("eT", c), more(2))
                    if c == 0:
                        ybanks.extend(open_(("ey", n), 4 + n) for n in range(2))
                    for n in range(2):
                        for k in range(2):
                            last = pe.matmul(ybanks[n][:, :], actT[:, k, :], w[:, k, n * 512:(n + 1) * 512],
                                             start=(c == 0 and k == 0), stop=(c == STEPS - 1 and k == 1), skip_group_check=True)
                        if c == STEPS - 1 and n == 0:
                            B.filled(last, ("ey", 0))
                    if c < STEPS - 1:
                        used(last)
                    else:
                        B.filled(last, ("ey", 1))
                        used_with(("ey", 1))
                for c in range(STEPS):
                    bank = open_(("egu", c), c % 2)
                    for half in range(2):
                        w = take_e((2 * c + (c - 1 if c else 0)) + half, "gu")
                        for k in range(KD):
                            last = pe.matmul(bank[:, half * FC:(half + 1) * FC], heT[:, k, :], w[:, k, :], start=(k == 0), stop=(k == 7))
                        if half == 0:
                            used(last)
                            if c:
                                hidden_T(c - 1)
                        else:
                            B.filled(last, ("egu", c))
                            used_with(("egu", c))
                    if c:
                        down(c - 1)
                hidden_T(STEPS - 1)
                down(STEPS - 1)
                B.wait_evacuated(pe, ("pgT",), more(3))
                for n in range(2):
                    B.wait_evacuated(pe, ("ey", n), more(4 + n))
                Ysb = nbf[:, 4096:5120]
                for t in range(TT):
                    for n in range(2):
                        name = ("sc", t, n)
                        bank = open_(name, 6 + n)
                        B.filled(pe.matmul(bank[:, :], PgT[:, t * P:(t + 1) * P], Ysb[:, n * 512:(n + 1) * 512], start=True, stop=True), name)

            with pe.Fori(0, NE) as i:
                expert(i)
            pe.wait_ge(items_in, 1)
            n_over = pe.value_load(sb_items[0:1, 0:1], min_val=0, max_val=NOVER)
            with pe.If(n_over > 0):
                with pe.Fori(NE, n_over + NE) as i:
                    expert(i)

        @block.sync
        def _(sp):
            sp.dma_start(cst[:, :], consts).then_inc(small_in, 16)
            for n, (kind, src, cw) in enumerate(blocks):
                if n >= RING:
                    s_, v_, _p = freed[n - RING]
                    sp.wait_ge(s_, v_)
                sp.dma_start(slot_view(n % RING, kind, cw), src).then_inc(block_in[n % RING], 16)

            def expert_blocks(gu_src, down_src, i, first):
                j = 0
                for c in range(STEPS + 1):
                    todo = [("gu", g) for g in (0, 1)] if c < STEPS else []
                    todo += [("down", 0)] if c else []
                    for kind, g in todo:
                        if j < RING:
                            if first:
                                s_, v_, _p = freed[NPRE + j - RING]
                                sp.wait_ge(s_, v_)
                            else:
                                s_, v_, per = freed[NPRE + PER + j - RING]
                                sp.wait_ge(s_, v_ + (i - 1) * per)
                        else:
                            s_, v_, per = freed[NPRE + j - RING]
                            sp.wait_ge(s_, v_ + i * per)
                        s = (NPRE + j) % RING
                        if kind == "gu":
                            sp.dma_start(slot_view(s, "gu", 0), gu_src(c, g)).then_inc(block_in[s], 16)
                        else:
                            sp.dma_start(slot_view(s, "down", 0), down_src(c - 1)).then_inc(block_in[s], 16)
                        j += 1

            def of(e):
                def gu(c, g):
                    c0 = g * FE + c * FC
                    return expert_gu[0, bass.ds(e, 1), :, c0:c0 + FC].rearrange("a (k p) f -> p (a k) f", p=P)

                def down(c):
                    return expert_down[0, bass.ds(e, 1), c * FC:(c + 1) * FC, :].rearrange("a (k p) n -> p (a k) n", p=P)
                return gu, down
            expert_blocks(*of(0), 0, True)
            with sp.Fori(1, NE) as i:
                expert_blocks(*of(i), i, False)
            sp.wait_ge(items_in, 1)
            n_over = sp.value_load(sb_items[0:1, 0:1], min_val=0, max_val=NOVER)
            with sp.If(n_over > 0):
                with sp.Fori(NE, n_over + NE) as i:
                    e = sp.value_load(sb_items[0:1, bass.ds(i - (NE - 1), 1)], min_val=0, max_val=NE - 1)
                    expert_blocks(*of(e), i, False)
            sp.wait_ge(final, 1)
            sp.dma_start(out[0].rearrange("(t p) d -> p t d", p=P), x[:, :, :]).then_inc(out_s, 16)
            sp.wait_ge(out_s, 16)

        @block.gpsimd
        def _(pool):
            n = [0]

            def step(ins):
                n[0] += 1
                ins.then_inc(pool_step, 1)
                pool.wait_ge(pool_step, n[0])
            for w, s in ((vres_w[:, :], vres_up[0]), (vresd_w[:, :, :], vres_down[0].rearrange("(k p) n -> p k n", p=P)),
                         (router_w[:, :, :], router[0].rearrange("(k p) n -> p k n", p=P))):
                pool.dma_start(w, s).then_inc(lw_in, 16)
            pool.dma_start(vec[:, :], vecs[0].partition_broadcast(P)).then_inc(vec_in, 16)
            for l in range(DEPTH):
                if l:
                    pool.wait_ge(ycat, 2 * l - 1)
                pool.dma_start(lora_w[0:64, :], decay_up[l]).then_inc(lw_in, 16)
                pool.dma_start(lora_w[64:128, :], iclr_up[l]).then_inc(lw_in, 16)
                pool.dma_start(gate_w[:, :], gate_up[l]).then_inc(lw_in, 16)
                if l:
                    pool.wait_ge(ycat, 2 * l)
                    pool.dma_start(vec[:, :], vecs[l].partition_broadcast(P)).then_inc(vec_in, 16)
                    B.wait_evacuated(pool, ("wo", l - 1, 1, 1))
                pool.memset(prev[0:1, 0, :], 0.0).then_inc(row0_ready, 1)
                for t in range(TT):
                    for lv in range(5):
                        for g in range(2):
                            if lv == 0:
                                for h in range(4 * g, 4 * g + 4):
                                    B.wait_evacuated(pool, ("m12", l, t, h))
                                if t:
                                    B.wait_filled(pool, ("X", l, t - 1, 4, g))
                            else:
                                B.wait_filled(pool, ("X", l, t, lv - 1, g))
                            m = C("lvl")[:, lv * P:(lv + 1) * P].unsqueeze(1)
                            pool.tensor_tensor(Cm[:, 4 * g:4 * g + 4, :], mats[:, 4 * g:4 * g + 4, 0, :], bc(m, 4, P), MUL)\
                                .then_inc(c_ready, 1)
                    for p in range(2):
                        c = TT * t + p
                        if c:
                            pool.wait_ge(state_ready, 5 * l + c + 1)
                        else:
                            B.wait_evacuated(pool, ("wt", l))
                        wts = sm[:, 0:16].rearrange("p (t b c) -> p t b c", t=TT, b=4)[:, t, :, p:p + 1]
                        pool.tensor_tensor(keep[:, :, :], bc(C("bd").unsqueeze(1), 4, P), bc(wts, 4, P), MUL).then_inc(keep_ready, 1)
                pool.wait_ge(ycat, 2 * l + 1)
                pool.dma_start(nbf[:, 4096:6144].rearrange("p (t c) -> p t c", t=TT), mem_in[0].rearrange("(t p) d -> p t d", p=P))\
                    .then_inc(mem_in_s, 16)

        @block.scalar
        def _(act):
            act.dma_start(x[:, :, :], x_in[0].rearrange("(t p) d -> p t d", p=P)).then_inc(x_in_s, 16)
            act.dma_start(col[:, :, :], cols.rearrange("l p c -> p l c")).then_inc(small_in, 16)
            act.dma_start(posi[:, :], pos_in).then_inc(small_in, 16)

            def copy(dst, name, src=None, scale=1.0, func=ACT.Copy):
                bank = B.wait_filled(act, name)
                B.release(act.activation(dst, bank[:, :] if src is None else src(bank), func, scale=scale), name)

            def squares(srcs, junk, cols_, done):
                for t in range(TT):
                    act.activation(junk[:, t, :], srcs[:, t, :], ACT.Square, accum_out=cols_[:, t:t + 1]).then_inc(done, 1)
            act.wait_ge(x_in_s, 16)
            squares(x, hNv, sm[:, 32:34], sq_done)
            act.wait_ge(rope_in, 1)
            act.activation(rope[:, 0:2, :], rope[:, 2:4, :], ACT.Sin).then_inc(rope_sin, 1)
            for l in range(DEPTH):
                for c, (c0, cw) in enumerate(chunks_in + ([(RC, VR)] if l else [])):
                    for t in range(TT):
                        name = ("in", l, c, t) if c < 7 else ("vr", l, t)
                        if 4 <= c < 7:
                            copy(dproj[:, t, c0 - RC:c0 - RC + cw], name)
                        else:
                            copy(pv[:, t, c0:c0 + cw], name, lambda b, cw=cw: b[:, 0:cw])
                    if c < 4 or c == 7:
                        g = c if c < 4 else 4
                        for t in range(TT):
                            B.wait_evacuated(act, ("in", l, c, t) if c < 7 else ("vr", l, t))
                        if c == 0:
                            act.wait_ge(row0_ready, l + 1)
                        cs = slice(c0, c0 + cw)
                        act.dma_start(prev[1:113, :, cs], pv[0:112, :, cs]).then_inc(shifted_in[g], 16)
                        act.dma_start(prev[113:128, :, cs], pv[112:127, :, cs]).then_inc(shifted_in[g], 16)
                        act.dma_start(prev[0:1, 1, cs], pv[127:128, 0, cs]).then_inc(shifted_in[g], 16)
                bank = B.wait_filled(act, ("lt", l))
                act.activation(lT[0:64, 0, :], bank[0:64, 0:256], ACT.Tanh)
                act.activation(lT[64:128, 0, :], bank[64:128, 0:256], ACT.Copy)
                B.release(act.activation(lT[:, 1, :], bank[:, 256:512], ACT.Sigmoid), ("lt", l))
                if l:
                    copy(vrT, ("vt", l), lambda b: b[0:VR, 0:256])
                for t in range(TT):
                    B.wait_evacuated(act, ("wup", l, t))
                    act.activation(nb(TMP)[:, t, :], nb(TMP)[:, t, :], ACT.Sigmoid).then_inc(sg_scan, 1)
                    B.wait_evacuated(act, ("aup", l, t))
                    act.activation(nb(A_)[:, t, :], nb(A_)[:, t, :], ACT.Sigmoid).then_inc(rate_done, 1)
                    if l:
                        B.wait_evacuated(act, ("vup", l, t))
                        act.activation(nb(KK)[:, t, :], nb(KK)[:, t, :], ACT.Sigmoid).then_inc(vmix_done, 1)
                    copy(nb(G_)[:, t, :], ("gup", l, t))
                for t in range(TT):
                    bank = B.wait_filled(act, ("cum", l, t))
                    act.activation(nb(EC)[:, t, :], bank[:, :], ACT.Exp).then_inc(expc, 1)
                    copy(nb(ENC)[:, t, :], ("cum", l, t), scale=-1.0, func=ACT.Exp)
                    copy(nb(ECP)[:, t, :], ("cums", l, t), func=ACT.Exp)
                copy(sm[:, 0:16], ("wt", l), lambda b: b[:, 0:16])
                for t in range(TT):
                    copy(arT[:, :, 0, :], ("aT", l, t))
                    copy(arT[:, :, 1, :], ("rT", l, t))
                    copy(bT, ("bT", l, t))
                    copy(kT, ("kT", l, t))
                    copy(U_, ("U", l, t), scale=-1.0)
                    for lv in range(5):
                        for g in range(2):
                            copy(Xm[:, 4 * g:4 * g + 4, :], ("X", l, t, lv, g))
                    for par in range(2):
                        r = slice(64 * par, 64 * par + 64)
                        copy(aiT[r, :, :], ("ai", l, t, par), lambda b, r=r: b[r, :])
                    copy(SA0, ("SA0", l, t))
                    for p in range(2):
                        r = slice(64 * p, 64 * p + 64)
                        copy(yraw[r, t, :], ("y1", l, t, p), lambda b, r=r: b[r, :])
                act.wait_ge(lam_in, l + 1)
                act.activation(sm[:, 38:40], sm[:, 36:38], ACT.Exp).then_inc(lam_exp, 1)
                qk = hT[:, :].rearrange("p (w h t) -> p w h t", w=2, h=4)
                for which in range(2):
                    for t in range(TT):
                        copy(qk[:, which, :, t * P:(t + 1) * P], ("qkT", l, which, t))

                def diff_out(h):
                    copy(W1[:, 512 * (h % 2):512 * (h % 2) + 384], ("atT", l, h), lambda b: b[:, 0:384])
                    copy(hNv[:, :, RW + h * DV:RW + (h + 1) * DV], ("pv", l, h), lambda b: b[:, 0:256].rearrange("p (t c) -> p t c", t=TT))
                for h in range(DH):
                    for m in range(2):
                        act.wait_ge(smx, 8 * l + 2 * h + m + 1)
                        if h >= 2:
                            act.wait_ge(attn_ready, 4 * l + h - 1)
                        s_, p_ = 384 * m, 768 + 384 * (2 * (h % 2) + m)
                        for q, (a, b) in enumerate(((0, 128), (128, 384))):
                            j = 4 * h + 2 * m + q
                            ins = act.activation(SH[:, p_ + a:p_ + b], SH[:, s_ + a:s_ + b], ACT.Exp, bias=ss[:, j:j + 1],
                                                 scale=DQ ** -0.5, accum_out=ss2[:, j:j + 1])
                        ins.then_inc(pexp, 1)
                    if h:
                        diff_out(h - 1)
                diff_out(DH - 1)
                act.wait_ge(mem_in_s, 16 * (l + 1))
                memn = nbf[:, 4096:6144].rearrange("p (t c) -> p t c", t=TT)
                squares(memn, nbf[:, 6144:8192].rearrange("p (t c) -> p t c", t=TT), sm[:, 34:36], msq_done)

                def plain_hT(name):
                    for t in range(TT):
                        for g in range(2):
                            copy(hTv[:, 4 * g:4 * g + 4, t * P:(t + 1) * P], (*name, t, g))

                def x_squares(name):
                    for t in range(TT):
                        for c in range(2):
                            B.wait_evacuated(act, (*name, c, t))
                    squares(x, hNv, sm[:, 32:34], sq_done)
                plain_hT(("hT", l, 1))
                x_squares(("op", l))
                qn = proj[:, 0:2048].rearrange("p (t c) -> p t c", t=TT)
                kn = dproj[:, :, :].rearrange("p t c -> p (t c)")[:, 0:2048].rearrange("p (t c) -> p t c", t=TT)
                vx = SH[:, 0:2048].rearrange("p (t c) -> p t c", t=TT)
                for c in range(2):
                    for t in range(TT):
                        copy(qn[:, t, c * 512:(c + 1) * 512], ("xq", l, c, t))
                for c in range(4):
                    for t in range(TT):
                        copy((kn if c < 2 else vx)[:, t, (c % 2) * 512:(c % 2 + 1) * 512], ("kv", l, c, t))
                px = SH[:, 2048:3072].rearrange("p (s q k) -> p s q k", s=2, q=2)
                for h in range(XH):
                    bank = B.wait_filled(act, ("xs", l, h))
                    act.wait_ge(xs_mx, XH * l + h + 1)
                    if h >= 2:
                        B.wait_filled(act, ("xpT", l, h - 2))
                    for q in range(TT):
                        ins = act.activation(px[:, h % 2, q, :], bank[:, q * 256:(q + 1) * 256], ACT.Exp, bias=ss[:, 16 + 2 * h + q:17 + 2 * h + q],
                                             scale=XD ** -0.5, accum_out=ss2[:, 16 + 2 * h + q:17 + 2 * h + q])
                    B.release(ins, ("xs", l, h))
                plain_hT(("oT", l))
                x_squares(("wo", l))
                if l == 0:
                    sil = nbf[:, 1536:2048].rearrange("p (t n) -> p t n", t=TT)
                    actT = nbf[:, 1024:1536]
                    for c in range(FD // FC):
                        for t in range(TT):
                            bank = B.wait_filled(act, ("gu", c, t))
                            act.activation(sil[:, t, :], bank[:, 0:FC], ACT.Silu).then_inc(silu_done, 1)
                        copy(actT, ("fT", c))
                    for t in range(TT):
                        for n in range(2):
                            B.wait_evacuated(act, ("fy", 2 * t + n))
                    squares(x, hNv, sm[:, 32:34], sq_done)
            wt = nbf[:, 8256:8260]
            act.wait_ge(w_in, 1)
            act.activation(wt, wt, ACT.Sigmoid).then_inc(w_sig, 1)

            def expert(i):
                def copy_e(dst, name, bank_no, src):
                    bank = B.wait_filled(act, name, i * MOE_PER[bank_no])
                    B.release(act.activation(dst, src(bank), ACT.Copy), name)
                copy_e(nbf[:, 2560:2816], ("pgT",), 3, lambda b: b[:, 0:256])
                sil = nbf[:, 1536:2048].rearrange("p (s n) -> p s n", s=2)
                for c in range(STEPS):
                    bank = B.wait_filled(act, ("egu", c), i * MOE_PER[c % 2])
                    act.activation(sil[:, c % 2, :], bank[:, 0:FC], ACT.Silu).then_inc(silu_done, 1)
                    copy_e(nbf[:, 512:768], ("eT", c), 2, lambda b: b[:, 0:256])
                copy_e(nbf[:, 4096:4608], ("ey", 0), 4, lambda b: b[:, :])
            with act.Fori(0, NE) as i:
                expert(i)
            act.wait_ge(items_in, 1)
            n_over = act.value_load(sb_items[0:1, 0:1], min_val=0, max_val=NOVER)
            with act.If(n_over > 0):
                with act.Fori(NE, n_over + NE) as i:
                    expert(i)

        @block.vector
        def _(dve):
            n = [0]

            def step(ins, more=0):
                n[0] += 1
                ins.then_inc(dve_step, 1)
                dve.wait_ge(dve_step, n[0] + more)

            def tt(o, a, b, op, more=0):
                step(dve.tensor_tensor(o, a, b, op), more)

            def ts(o, a, s1, s2, op0, op1=None, more=0):
                step(dve.tensor_scalar(o, a, s1, s2, op0, op1) if op1 is not None else dve.tensor_scalar(o, a, s1, None, op0), more)

            def stt(o, a, s, b, op0, op1):
                step(dve.scalar_tensor_tensor(o, a, s, b, op0, op1))

            def total(o, a):
                step(dve.tensor_reduce(o, a, AX.X, ADD))

            def rsqrt(v, w, scale, eps):
                y, t, z = rst[:, 0:w], rtmp[:, 0:w], v[:, 0:w]
                ts(z, z, scale, eps, MUL, ADD)
                ts(y.bitcast(I32), z.bitcast(I32), 1, None, ALU.logical_shift_right)
                ts(y.bitcast(I32), y.bitcast(I32), -1.0, 1597463007.0, MUL, ADD)
                for _ in range(3):
                    tt(t, y, y, MUL)
                    stt(t, t, -0.5, z, MUL, MUL)
                    stt(y, t, 1.5, y, ADD, MUL)
                return y

            def evac(dst, name, src, other, op):
                bank = B.wait_filled(dve, name)
                B.release(dve.tensor_tensor(dst, src(bank), other, op), name)
                B.wait_evacuated(dve, name)

            def four(b):
                return b[:, :].rearrange("p (b t) -> p b t", b=4)

            def gain_hT(name, dst, gains):
                for t in range(TT):
                    for g in range(2):
                        evac(dst[:, 4 * g:4 * g + 4, t * P:(t + 1) * P], (*name, t, g), four, bc(gains[:, 4 * g:4 * g + 4].unsqueeze(2), 4, P), MUL)

            def gains(l, name, w=8):
                return col[:, l, COL[name]:COL[name] + w]

            def normalize(l, s, gain, name):
                for t in range(TT):
                    dve.wait_ge(sq_done, 2 * (3 * l + s) + t + 1)
                r = rsqrt(sm[:, 32:34], TT, 1.0 / D, EPS)
                for t in range(TT):
                    dve.tensor_scalar(hNv[:, t, :], x[:, t, :], r[:, t:t + 1], None, MUL).then_inc(hn_done, 1)
                gain_hT(name, hTv, gains(l, gain))

            def add_x(name):
                for c in range(2):
                    for t in range(TT):
                        xs = x[:, t, c * 512:(c + 1) * 512]
                        evac(xs, (*name, c, t), lambda b: b[:, :], xs, ADD)

            dve.wait_ge(small_in, 48)
            posf = sm[:, 40:42]
            step(dve.tensor_copy(posf, posi[:, :]))
            ang, k_, r_ = rope[:, 0, :], rope[:, 1, :], rope[:, 2, :]
            tt(ang.rearrange("p (t f) -> p t f", t=TT), bc(posf.unsqueeze(2), TT, 8), bc(C("freq").unsqueeze(1), TT, 8), MUL)
            ts(k_, ang, 1.0 / (2 * math.pi), 12582912.0, MUL, ADD)
            ts(k_, k_, -12582912.0, None, ADD)
            stt(r_, k_, -6.28125, ang, MUL, ADD)
            stt(r_, k_, -(2 * math.pi - 6.28125), r_, MUL, ADD)
            ts(r_, r_, -3.1415925, 3.1415925, ALU.max, ALU.min)
            ts(rope[:, 3, :], r_, 0.5, None, MUL)
            step(dve.tensor_copy(rope[:, 0, :], r_))
            dve.tensor_copy(rope[:, 1, :], r_).then_inc(rope_in, 1)
            dve.wait_ge(rope_sin, 1)
            tt(rope[:, 1, :], rope[:, 1, :], rope[:, 1, :], MUL)
            ts(rope[:, 1, :], rope[:, 1, :], -2.0, 1.0, MUL, ADD)
            sin = rope[:, 0, :].rearrange("p (t f) -> p t f", t=TT)
            cos = rope[:, 1, :].rearrange("p (t f) -> p t f", t=TT)

            for l in range(DEPTH):
                lam_init = 0.8 - 0.6 * math.exp(-0.3 * l)
                normalize(l, 0, "mix", ("hT", l, 0))
                dve.wait_ge(vec_in, 16 * (l + 1))
                for g, (c0, cw) in enumerate(chunks_in[0:4] + ([(RC, VR)] if l else [])):
                    dve.wait_ge(shifted_in[g], 48 * (l + 1) if g < 4 else 48)
                    p_, q_ = pv[:, :, c0:c0 + cw], prev[:, :, c0:c0 + cw]
                    mu = (vec[:, VEC["mu"][0] + c0:VEC["mu"][0] + c0 + cw] if g < 4 else V("vmu")).unsqueeze(1)
                    tt(q_, q_, p_, SUB)
                    tt(q_, q_, bc(mu, TT, cw), MUL)
                    if g < 3:
                        tt(p_, p_, q_, ADD)
                    else:
                        dve.tensor_tensor(p_, p_, q_, ADD).then_inc(lora_ready, 1)
                r_, k_, v_ = (pv[:, :, i * RW:(i + 1) * RW] for i in range(3))
                for t in range(TT):
                    evac(nb(TMP)[:, t, :], ("wup", l, t), lambda b: b[:, :], V("decay_b"), ADD)
                    evac(nb(A_)[:, t, :], ("aup", l, t), lambda b: b[:, :], V("iclr_b"), ADD)
                    if l:
                        evac(nb(KK)[:, t, :], ("vup", l, t), lambda b: b[:, :], V("vres_b"), ADD)
                if l:
                    tt(nb(B_), v_first[:, :, :], v_, SUB)
                    dve.wait_ge(vmix_done, TT)
                    tt(nb(B_), nb(B_), nb(KK), MUL)
                    tt(v_, v_, nb(B_), ADD)
                else:
                    step(dve.tensor_copy(v_first[:, :, :], v_))
                heads = lambda a: a.rearrange("p (n c) -> p n c", c=HD)
                kkf, bf = NB[:, KK, :], NB[:, B_, :]
                tt(nb(KK), k_, bc(V("kk_s").unsqueeze(1), TT, RW), MUL)
                tt(bf, kkf, kkf, MUL)
                total(ss[:, 0:16], heads(bf))
                ts(ss[:, 0:16], ss[:, 0:16], 1e-24, None, ALU.max)
                rs = rsqrt(ss, 16, 1.0, 0.0)
                tt(heads(kkf), heads(kkf), bc(rs.unsqueeze(2), 16, HD), MUL)
                dve.wait_ge(rate_done, TT * (l + 1))
                stt(nb(B_), nb(A_), -1.0, bc(V("ka_s").unsqueeze(1), TT, RW), ADD, MUL)
                stt(k_, nb(B_), 1.0, k_, ADD, MUL)
                tt(bf, kkf, NB[:, A_, :], MUL)
                for t in range(TT):
                    B.wait_evacuated(dve, ("cum", l, t))
                    B.wait_evacuated(dve, ("cums", l, t))
                tt(NB[:, ECP, :], kkf, NB[:, ECP, :], MUL)
                tt(bf, bf, NB[:, ENC, :], MUL)
                tt(nb(ENC), k_, nb(ENC), MUL)
                tt(nb(RHO), r_, nb(EC), MUL)
                if l:
                    dve.wait_ge(state_ready, 5 * l)
                dve.memset(state[:, :, :], 0.0).then_inc(state_ready, 1)
                tt(nb(KK), r_, k_, MUL)
                dve.engine_nop().then_inc(elem, 1)
                tt(nb(KK), nb(KK), bc(V("bonus").unsqueeze(1), TT, RW), MUL)
                total(sm[:, 16:32], heads(kkf))
                for t in range(TT):
                    for h in (0, 2, 4, 6, 1, 3, 5, 7):
                        evac(mats[:, h, :, :].rearrange("p (a q) t -> p a (q t)", a=2), ("m12", l, t, h),
                             lambda b: b[:, :].rearrange("p (a q) -> p a q", a=2), bc(C("mask_in").unsqueeze(1), 2, 256), MUL)
                    for par in range(2):
                        tp = Tm.rearrange("p (b q) t -> p b q t", q=2)[:, :, par, :]
                        evac(tp, ("m3", l, t, par), four, bc(C("neg1").unsqueeze(1), 4, P), MUL)
                    tt(Tm, Tm, bc(ident.unsqueeze(1), 8, P), ADD)
                    tt(TTm, mats[:, :, 0, :], bc(C("neg1T").unsqueeze(1), 8, P), MUL)
                    dve.tensor_tensor(TTm, TTm, bc(ident.unsqueeze(1), 8, P), ADD).then_inc(t_ready, 1)
                    dve.wait_ge(t_ready, TT * l + t + 1)
                    for lv in range(5):
                        for g in range(2):
                            hs = slice(4 * g, 4 * g + 4)
                            if lv < 4:
                                bank = B.wait_filled(dve, ("Z", l, t, lv, g))
                                B.release(dve.tensor_tensor(Tm[:, hs, :], Tm[:, hs, :], four(bank), SUB), ("Z", l, t, lv, g))
                            bank = B.wait_filled(dve, ("ZT", l, t, lv, g))
                            B.release(dve.tensor_tensor(TTm[:, hs, :], TTm[:, hs, :], four(bank), SUB), ("ZT", l, t, lv, g))
                            if lv < 4:
                                B.wait_evacuated(dve, ("Z", l, t, lv, g))
                            B.wait_evacuated(dve, ("ZT", l, t, lv, g))
                    B.wait_evacuated(dve, ("SA0", l, t))
                    for p in range(2):
                        c = 2 * (TT * l + t) + p
                        r = slice(64 * p, 64 * p + 64)
                        bank = B.wait_filled(dve, ("sa", l, t, p))
                        step(dve.tensor_tensor(SA[r, :], SA0[r, :], bank[r, :], SUB))
                        B.release(dve.engine_nop(), ("sa", l, t, p))
                        dve.engine_nop().then_inc(sa_ready, 1)
                        evac(state[:, :, :], ("s", l, t, p), four, state[:, :, :], ADD)
                        dve.wait_ge(keep_ready, c + 1)
                        dve.tensor_tensor(state[:, :, :], state[:, :, :], keep[:, :, :], MUL).then_inc(state_ready, 1)
                        dve.wait_ge(state_ready, c + l + 2)
                    for p in range(2):
                        B.wait_evacuated(dve, ("y1", l, t, p))
                    evac(yraw[:, t, :], ("y2", l, t), lambda b: b[:, :], yraw[:, t, :], ADD)
                y, yf, rho = NB[:, EC, :], heads(NB[:, EC, :]), NB[:, RHO, :]
                total(ss[:, 0:16], yf)
                ts(ss[:, 0:16], ss[:, 0:16], 1.0 / HD, None, MUL)
                tt(yf, yf, bc(ss[:, 0:16].unsqueeze(2), 16, HD), SUB)
                tt(rho, y, y, MUL)
                total(ss[:, 0:16], heads(rho))
                rs = rsqrt(ss, 16, 1.0 / HD, GN_EPS)
                tt(yf, yf, bc(rs.unsqueeze(2), 16, HD), MUL)
                tt(nb(EC), nb(EC), bc(V("gn_w").unsqueeze(1), TT, RW), MUL)
                tt(nb(EC), nb(EC), bc(V("gn_b").unsqueeze(1), TT, RW), ADD)
                vh = v_.rearrange("p t (n c) -> p t n c", c=HD)
                bon = sm[:, 16:32].rearrange("p (t n) -> p t n", t=TT).unsqueeze(3)
                tt(nb(RHO).rearrange("p t (n c) -> p t n c", c=HD), vh, bc(bon, TT, 8, HD), MUL)
                tt(y, y, rho, ADD)
                dve.tensor_tensor(hNv[:, :, 0:RW], nb(EC), nb(G_), MUL).then_inc(ycat, 1)
                dve.wait_ge(ycat, 2 * l + 1)

                lp = SH[:, 3072:3200]
                tt(lp, vec[:, VEC["lq1"][0]:VEC["lq1"][0] + 128], vec[:, VEC["lk1"][0]:VEC["lk1"][0] + 128], MUL)
                step(dve.tensor_reduce(sm[:, 36:38], lp.rearrange("p (a c) -> p a c", a=2), AX.X, ADD))
                dve.engine_nop().then_inc(lam_in, 1)
                qk = dproj[:, :, 0:1024].rearrange("p t (n c) -> p t n c", c=DQ)
                sq = SH[:, 0:2048].rearrange("p (t n c) -> p t n c", t=TT, c=DQ)
                for c in (4, 5, 6):
                    for t in range(TT):
                        B.wait_evacuated(dve, ("in", l, c, t))
                tt(sq, qk, qk, MUL)
                total(ss[:, 0:32], SH[:, 0:2048].rearrange("p (n c) -> p n c", c=DQ))
                rs = rsqrt(ss, 32, 1.0 / DQ, EPS).rearrange("p (t n) -> p t n", t=TT).unsqueeze(3)
                tt(qk, qk, bc(rs, TT, 16, DQ), MUL)
                for w, nm in ((0, "q_norm"), (1, "k_norm")):
                    part = qk[:, :, 8 * w:8 * w + 8, :]
                    tt(part, part, bc(V(nm).unsqueeze(1).unsqueeze(1), TT, 8, DQ), MUL)
                x1, x2 = qk[:, :, :, 0:8], qk[:, :, :, 8:16]
                t1 = SH[:, 2048:2304].rearrange("p (t n c) -> p t n c", t=TT, c=8)
                t2 = SH[:, 2304:2560].rearrange("p (t n c) -> p t n c", t=TT, c=8)
                sn, cs = bc(sin.unsqueeze(2), TT, 16, 8), bc(cos.unsqueeze(2), TT, 16, 8)
                tt(t1, x1, sn, MUL)
                tt(t2, x2, sn, MUL)
                tt(x1, x1, cs, MUL)
                tt(x2, x2, cs, MUL)
                tt(x1, x1, t2, SUB)
                dve.tensor_tensor(x2, x2, t1, ADD).then_inc(qs_ready, 1)
                dve.wait_ge(lam_exp, l + 1)
                nlam = sm[:, 42:43]
                tt(nlam, sm[:, 39:40], sm[:, 38:39], SUB)
                ts(nlam, nlam, -lam_init, None, ADD)

                def row_max(h):
                    for m in range(2):
                        S = SH[:, 384 * m:384 * m + 384]
                        if h:
                            dve.wait_ge(pexp, 8 * l + 2 * (h - 1) + m + 1)
                        evac(S, ("ds", l, h, m), lambda b: b[:, 0:384], C("causal"), ADD)
                        j = 4 * h + 2 * m
                        step(dve.tensor_reduce(ss[:, j:j + 1], S[:, 0:128], AX.X, ALU.max))
                        step(dve.tensor_reduce(ss[:, j + 1:j + 2], S[:, 128:384], AX.X, ALU.max))
                        dve.tensor_scalar(ss[:, j:j + 2], ss[:, j:j + 2], -DQ ** -0.5, None, MUL).then_inc(smx, 1)

                def attend(h):
                    dve.wait_ge(pexp, 8 * l + 2 * h + 2)
                    j = 4 * h
                    step(dve.reciprocal(ss2[:, j:j + 4], ss2[:, j:j + 4]))
                    ts(ss2[:, j + 2:j + 4], ss2[:, j + 2:j + 4], nlam, None, MUL)
                    if h >= 2:
                        B.wait_filled(dve, ("atT", l, h - 2))
                    o, p0, p1 = 2304 + 384 * (h % 2), 768 + 768 * (h % 2), 768 + 768 * (h % 2) + 384
                    for q, (a, b) in enumerate(((0, 128), (128, 384))):
                        ts(SH[:, o + a:o + b], SH[:, p0 + a:p0 + b], ss2[:, j + q:j + q + 1], None, MUL)
                        stt(SH[:, o + a:o + b], SH[:, p1 + a:p1 + b], ss2[:, j + 2 + q:j + 3 + q], SH[:, o + a:o + b], MUL, ADD)
                    dve.engine_nop().then_inc(attn_ready, 1)
                for h in range(DH + 1):
                    if h < DH:
                        row_max(h)
                    if h:
                        attend(h - 1)
                for h in range(DH):
                    B.wait_evacuated(dve, ("pv", l, h))
                o4 = hNv[:, :, RW:].rearrange("p t (h c) -> p t h c", h=DH)
                tt(SH[:, 0:1024].rearrange("p (t h c) -> p t h c", t=TT, h=DH), o4, o4, MUL)
                total(ss[:, 0:8], SH[:, 0:1024].rearrange("p (n c) -> p n c", c=DV))
                rs = rsqrt(ss, 8, 1.0 / DV, EPS)
                ts(rs, rs, 1.0 - lam_init, None, MUL)
                tt(o4, o4, bc(rs.rearrange("p (t h) -> p t h", t=TT).unsqueeze(3), TT, DH, DV), MUL)
                dve.tensor_tensor(o4, o4, bc(V("subln").unsqueeze(1).unsqueeze(1), TT, DH, DV), MUL).then_inc(ycat, 1)
                dve.wait_ge(ycat, 2 * l + 2)
                memn = nbf[:, 4096:6144].rearrange("p (t c) -> p t c", t=TT)
                dve.wait_ge(msq_done, 2 * l + 2)
                r = rsqrt(sm[:, 34:36], TT, 1.0 / D, EPS)
                for t in range(TT):
                    dve.tensor_scalar(memn[:, t, :], memn[:, t, :], r[:, t:t + 1], None, MUL).then_inc(mn_done, 1)
                dve.wait_ge(mn_done, 2 * l + 2)
                add_x(("op", l))
                normalize(l, 1, "xattn", ("hT", l, 2))
                mT = nbf[:, 6144:8192].rearrange("p (k t) -> p k t", k=KD)

                def head_norm(src, scratch, done):
                    tt(scratch, src, src, MUL)
                    total(ss[:, 0:8], scratch.rearrange("p (n c) -> p n c", c=XD))
                    rs = rsqrt(ss, 8, 1.0 / XD, EPS)
                    s8 = src.rearrange("p (n c) -> p n c", c=XD)
                    dve.tensor_tensor(s8, s8, bc(rs.unsqueeze(2), 8, XD), MUL).then_inc(done, 1)
                    dve.wait_ge(done, l + 1)
                gain_hT(("mT", l), mT, gains(l, "mem"))
                for c in range(2):
                    for t in range(TT):
                        B.wait_evacuated(dve, ("xq", l, c, t))
                head_norm(proj[:, 0:2048], nbf[:, 2048:4096], xq_n)
                for c in range(2):
                    for t in range(TT):
                        B.wait_evacuated(dve, ("kv", l, c, t))
                head_norm(dproj[:, :, :].rearrange("p t c -> p (t c)")[:, 0:2048], nbf[:, 0:2048], xk_n)
                gain_hT(("xqT", l), nbf[:, 2048:4096].rearrange("p (k t) -> p k t", k=KD), gains(l, "xq"))
                gain_hT(("xkT", l), nbf[:, 0:2048].rearrange("p (k t) -> p k t", k=KD), gains(l, "xk"))
                PT = nbf[:, 8192:9216].rearrange("p (s n) -> p s n", s=2)
                for h in range(XH + 1):
                    if h < XH:
                        bank = B.wait_filled(dve, ("xs", l, h))
                        j = 16 + 2 * h
                        step(dve.tensor_reduce(ss[:, j:j + 2], bank[:, :].rearrange("p (q k) -> p q k", q=2), AX.X, ALU.max))
                        dve.tensor_scalar(ss[:, j:j + 2], ss[:, j:j + 2], -XD ** -0.5, None, MUL).then_inc(xs_mx, 1)
                    if h:
                        bank = B.wait_filled(dve, ("xpT", l, h - 1))
                        B.release(dve.tensor_copy(PT[:, (h - 1) % 2, :], bank[:, :]), ("xpT", l, h - 1))
                        j = 16 + 2 * (h - 1)
                        B.wait_evacuated(dve, ("xs", l, h - 1))
                        step(dve.reciprocal(ss2[:, j:j + 2], ss2[:, j:j + 2]))
                        bank = B.wait_filled(dve, ("xo", l, h - 1))
                        for q in range(TT):
                            ins = dve.tensor_scalar(memn[:, q, (h - 1) * XD:h * XD], bank[:, q * 256:(q + 1) * 256], ss2[:, j + q:j + q + 1], None, MUL)
                        B.release(ins, ("xo", l, h - 1))
                add_x(("wo", l))
                normalize(l, 2, "ffn", ("hT", l, 3))
                if l == 0:
                    sil = nbf[:, 1536:2048].rearrange("p (t n) -> p t n", t=TT)
                    actv = nbf[:, 0:1024].rearrange("p (s t n) -> p s t n", s=2, t=2)
                    for c in range(FD // FC):
                        for t in range(TT):
                            bank = B.wait_filled(dve, ("gu", c, t))
                            dve.wait_ge(silu_done, TT * c + t + 1)
                            B.release(dve.tensor_tensor(actv[:, c % 2, t, :], sil[:, t, :], bank[:, FC:2 * FC], MUL), ("gu", c, t))
                    for t in range(TT):
                        for nn in range(2):
                            xs = x[:, t, nn * 512:(nn + 1) * 512]
                            evac(xs, ("fy", t * 2 + nn), lambda b: b[:, :], xs, ADD)
            SILU0 = TT * (FD // FC)

            sc = nbf[:, 8192:9216]
            sel, lg = (sc[:, a:a + 16].rearrange("p (t e) -> p t e", t=TT) for a in (0, 16))
            mx8 = sc[:, 32:48].rearrange("p (t e) -> p t e", t=TT)
            w4 = sc[:, 64:68].rearrange("p (t j) -> p t j", t=TT)
            ix = sc[:, 80:96]
            ixf = sc[:, 96:112].rearrange("p (t e) -> p t e", t=TT)
            oh = sc[:, 112:144].rearrange("p (j t e) -> p j t e", j=2, t=TT)
            gate = sc[:, 144:160].rearrange("p (t e) -> p t e", t=TT)
            pos = sc[:, 160:184]
            ov, rank, R, tmp = (sc[:, a:a + 8] for a in (184, 192, 200, 208))
            tmp2 = sc[:, 224:240].rearrange("p (t e) -> p t e", t=TT)
            itf = sc[:, 240:244]
            IT = sc[:, 256:256 + 6 * NITEM].rearrange("p (q t i) -> p q t i", q=3, t=TT)
            iota8 = C("iota")[:, 0:NE]
            bank = B.wait_filled(dve, ("logit",))
            B.release(dve.tensor_copy(sc[:, 16:32], bank[:, 0:16]), ("logit",))
            B.wait_evacuated(dve, ("logit",))
            for t in range(TT):
                step(dve.max(mx8[:, t, :], lg[:, t, :]))
                step(dve.max_index(ix.bitcast(U32)[:, t * 8:(t + 1) * 8], mx8[:, t, :], lg[:, t, :]))
            step(dve.tensor_copy(sc[:, 96:112], ix.bitcast(U32)))
            tt(w4[:, :, 0], mx8[:, :, 0], mx8[:, :, 1], SUB)
            dve.tensor_tensor(w4[:, :, 1], mx8[:, :, 1], mx8[:, :, 0], SUB).then_inc(w_in, 1)
            for j in range(2):
                for t in range(TT):
                    ts(oh[:, j, t, :], iota8, ixf[:, t, j:j + 1], None, ALU.is_equal)
            dve.tensor_tensor(sel, oh[:, 0, :, :], oh[:, 1, :, :], ADD).then_inc(rt_sel, 1)
            dve.wait_ge(rt_sel, 1)
            dve.wait_ge(w_sig, 1)
            for t in range(TT):
                ts(gate[:, t, :], oh[:, 0, t, :], w4[:, t, 0:1], None, MUL)
                stt(gate[:, t, :], oh[:, 1, t, :], w4[:, t, 1:2], gate[:, t, :], MUL, ADD)
            bank = B.wait_filled(dve, ("pos",))
            B.release(dve.tensor_copy(pos, bank[:, 0:24]), ("pos",))
            B.wait_evacuated(dve, ("pos",))
            posv = pos[:, 0:16].rearrange("p (t e) -> p t e", t=TT)
            for q, src in enumerate((posv, sel, gate)):
                step(dve.tensor_copy(IT[:, q, :, 0:NE], src))
            ts(ov, pos[:, 16:24], float(P), None, ALU.is_gt)
            step(dve.tensor_tensor_scan(rank, C("ones")[:, 0:NE], ov, 0.0, MUL, ADD))
            step(dve.tensor_copy(itf[:, 0:1], rank[:, NE - 1:NE]))
            tt(rank, rank, ov, SUB)
            for r in range(NOVER):
                ts(R, rank, float(r), None, ALU.is_equal)
                tt(R, R, ov, MUL)
                for q, src in enumerate((posv, sel, gate)):
                    tt(tmp2, src, bc(R.unsqueeze(1), TT, NE), MUL)
                    step(dve.tensor_reduce(IT[:, q, :, NE + r], tmp2, AX.X, ADD))
                ts(IT[:, 0, :, NE + r], IT[:, 0, :, NE + r], -float(P), None, ADD)
                tt(tmp, R, iota8, MUL)
                step(dve.tensor_reduce(itf[:, r + 1:r + 2], tmp, AX.X, ADD))
            dve.tensor_copy(sb_items[:, :], itf[0:1, :]).then_inc(items_in, 1)

            first_step = n[0]

            def expert(i):
                n[0] = first_step
                more = i * DVE_STEPS

                def evac_e(dst, name, bank_no, src, other, op):
                    bank = B.wait_filled(dve, name, i * MOE_PER[bank_no])
                    B.release(dve.tensor_tensor(dst, src(bank), other, op), name)
                    B.wait_evacuated(dve, name, i * MOE_PER[bank_no])
                cur = sm[:, 44:50]
                step(dve.tensor_copy(cur.rearrange("p (q t) -> p q t", q=3).unsqueeze(3), IT[:, :, :, bass.ds(i, 1)]), more)
                Psel = nbf[:, 2048:2304].rearrange("p (t j) -> p t j", t=TT)
                Pg = nbf[:, 2304:2560].rearrange("p (t j) -> p t j", t=TT)
                for q, dst in ((1, Psel), (2, Pg)):
                    for t in range(TT):
                        ins = dve.tensor_scalar(dst[:, t, :], C("iota"), cur[:, t:t + 1], cur[:, 2 * q + t:2 * q + t + 1], ALU.is_equal, MUL)
                    ins.then_inc(sel_done, 1)
                heT = nbf[:, 3072:4096].rearrange("p (k j) -> p k j", k=KD)
                for g in range(2):
                    evac_e(heT[:, 4 * g:4 * g + 4, :], ("he", g), 6 + g, four, bc(gains(1, "ffn")[:, 4 * g:4 * g + 4].unsqueeze(2), 4, P), MUL)
                actv = nbf[:, 0:512].rearrange("p (s n) -> p s n", s=2)
                sil = nbf[:, 1536:2048].rearrange("p (s n) -> p s n", s=2)
                for c in range(STEPS):
                    bank = B.wait_filled(dve, ("egu", c), i * MOE_PER[c % 2])
                    dve.wait_ge(silu_done, SILU0 + c + 1 + i * STEPS)
                    B.release(dve.tensor_tensor(actv[:, c % 2, :], sil[:, c % 2, :], bank[:, FC:2 * FC], MUL), ("egu", c))
                bank = B.wait_filled(dve, ("ey", 1), i * MOE_PER[5])
                B.release(dve.tensor_copy(nbf[:, 4608:5120], bank[:, :]), ("ey", 1))
                for t in range(TT):
                    for nn in range(2):
                        xs = x[:, t, nn * 512:(nn + 1) * 512]
                        evac_e(xs, ("sc", t, nn), 6 + nn, lambda b: b[:, :], xs, ADD)
                assert n[0] == first_step + DVE_STEPS
            with dve.Fori(0, NE) as i:
                expert(i)
            n_over = dve.value_load(sb_items[0:1, 0:1], min_val=0, max_val=NOVER)
            with dve.If(n_over > 0):
                with dve.Fori(NE, n_over + NE) as i:
                    expert(i)
            dve.engine_nop().then_inc(final, 1)


def constants():
    import numpy as np
    f = np.float32
    i = np.arange(P)
    row, c = i[:, None], i[None, :]
    same = (row // CH) == (c // CH)
    part = {
        "ident": (row == c), "bd": same, "ones": np.ones((P, P)), "utri": row < c, "iota": np.broadcast_to(c, (P, P)),
        "mask_in": np.concatenate([same & (row < c), same & (row <= c)], 1),
        "tri": DEC * (same & (row <= c)), "tri_s": DEC * (same & (row < c)),
        "neg1": -1.0 * ((row == c + 1) & (row % 2 == 1)), "neg1T": -1.0 * ((c == row + 1) & (c % 2 == 1)),
        "lvl": np.concatenate([(row // (2 * b) == c // (2 * b)) & (row % (2 * b) < b) & (c % (2 * b) >= b) for b in (2, 4, 8, 16, 32)], 1),
        "causal": np.concatenate([-1e30 * (c > row), np.zeros((P, P)), -1e30 * (c > row)], 1),
        "last": np.stack([i == CH - 1, i == 2 * CH - 1], 1),
        "freq": np.broadcast_to(f(500000.0) ** (-np.arange(0, ROPE, 2, dtype=f) / f(ROPE)), (P, 8)),
    }
    return np.ascontiguousarray(np.concatenate([np.asarray(part[n], f).reshape(P, w) for n, (_, w) in CST.items()], 1))


def kernel(**inputs):
    import numpy as np
    import concourse.bacc as bacc
    from concourse import mybir as mb
    from concourse.bass_utils import run_bass_kernel_spmd

    a = {k: np.ascontiguousarray(v) for k, v in inputs.items()}
    L = DEPTH
    last = lambda n: np.broadcast_to(a[n][-1], (L, *a[n].shape[1:]))
    src = {"mu": a["shift_mu"], "vmu": last("vres_shift_mu"), "decay_b": a["decay_bias"], "iclr_b": a["iclr_bias"],
           "kk_s": a["key_kk_scale"], "ka_s": a["key_iclr_scale"], "bonus": a["bonus_rk"].reshape(L, -1), "gn_w": a["rwkv_gn_w"],
           "gn_b": a["rwkv_gn_b"], "vres_b": last("vres_bias"), "q_norm": a["q_norm"], "k_norm": a["k_norm"],
           "lq1": a["lambda_q1"], "lq2": a["lambda_q2"], "lk1": a["lambda_k1"], "lk2": a["lambda_k2"], "subln": a["diff_subln"]}
    vecs = np.ascontiguousarray(np.concatenate([src[n] for n in VEC], 1))
    fold = lambda v: v.reshape(L, -1, P).transpose(0, 2, 1)
    cols = np.ascontiguousarray(np.concatenate(
        [fold(a[n]) for n in ("mix_norm", "xattn_norm", "mem_norm", "ffn_norm")]
        + [np.tile(fold(a[n]), (1, 1, XH)) for n in ("xattn_q_norm", "xattn_k_norm")], 2))
    feeds = {"x": a["x"], "mem": a["mem"], "positions": np.ascontiguousarray(a["positions"].reshape(TT, P).T), "vecs": vecs, "cols": cols, "consts": constants()}
    for n in ("in_proj", "decay_up", "iclr_up", "gate_up", "vres_down", "vres_up", "out_proj", "xattn_wq", "xattn_wkv", "xattn_wo",
              "dense_w_gu", "dense_w_down", "router", "expert_w_gu", "expert_w_down"):
        feeds[n] = a[n]
    nc = bacc.Bacc("TRN2", target_bir_lowering=False, num_devices=1)
    args = [nc.dram_tensor(f"in_{n}", v.shape, mb.dt.from_np(v.dtype), kind="ExternalInput").ap() for n, v in feeds.items()]
    args.append(nc.dram_tensor("out_0", (1, SEQ, D), mb.dt.float32, kind="ExternalOutput").ap())
    decoder_trunk(nc, *args)
    r = run_bass_kernel_spmd(nc, [{f"in_{n}": v for n, v in feeds.items()}], core_ids=[0])
    return r.results[0]["out_0"]
```

```python
import concourse.bass as bass
from concourse import mybir
from contextlib import ExitStack
import math

P = 128
D = 1024
SEQ = 256
TT = SEQ // P
KD = D // P
DEPTH = 2
EPS = 1e-6
RW, RH, HD = 512, 8, 64
GN_EPS = 64e-5
LORA = 256
RC = 3 * RW + LORA
VR = 32
DH, DV, DQ = 4, 128, 64
ROPE = 16
XH, XD = 4, 256
FD, FE, NE = 2816, 3584, 8
CH = 64
NOVER = 3
NITEM = NE + NOVER
RING, BLK = 4, 1024
NS = 3
DVE_STEPS = 1
FC = 256
DEC = -math.exp(-0.5)

VEC = {}
_at = 0
for _n, _w in (("decay_b", RW), ("iclr_b", RW), ("kk_s", RW), ("ka_s", RW), ("bonus", RW),
               ("gn_w", RW), ("gn_b", RW), ("vres_b", RW), ("q_norm", DQ), ("k_norm", DQ), ("lq1", DQ), ("lq2", DQ),
               ("lk1", DQ), ("lk2", DQ), ("subln", DV)):
    VEC[_n] = (_at, _w)
    _at += _w
NV = _at
NMU = RC + VR
COL = {"mix": 0, "xattn": 8, "mem": 16, "ffn": 24, "xq": 32, "xk": 40}
NCOL = 48
CST = {}
_at = 0
for _n, _w in (("ident", P), ("mask_in", 256), ("lvl", 5 * P), ("neg1", P), ("neg1T", P), ("tri", P), ("tri_s", P),
               ("causal", 384), ("bd", P), ("last", 2), ("ones", P), ("utri", P), ("iota", P), ("freq", 8)):
    CST[_n] = (_at, _w)
    _at += _w
NCST = _at


class Banks:

    def __init__(self, psum, ready, evacuated):
        self.psum, self.ready, self.evacuated = psum, ready, evacuated
        self.n, self.use = [0] * 8, {}
        self.taken = [0]
        self.before = {}

    def open(self, pe, name, bank, more=0):
        self.use[name] = (bank, self.n[bank])
        if self.n[bank]:
            pe.wait_ge(self.evacuated[bank], self.n[bank] + more)
        self.n[bank] += 1
        return self.psum[bank]

    def filled(self, last, name):
        last.then_inc(self.ready[self.use[name][0]], 1)
        self.before[name] = self.taken[0]

    def wait_filled(self, eng, name, more=0):
        bank, nth = self.use[name]
        eng.wait_ge(self.ready[bank], nth + 1 + more)
        return self.psum[bank]

    def wait_evacuated(self, eng, name, more=0):
        bank, nth = self.use[name]
        eng.wait_ge(self.evacuated[bank], nth + 1 + more)

    def release(self, ins, name):
        ins.then_inc(self.evacuated[self.use[name][0]], 1)


def decoder_trunk(nc, x_in, mem_in, pos_in, mus, vecs, cols, consts, in_proj, decay_up, iclr_up, gate_up, vres_down, vres_up,
                  out_proj, wq, wkv, wo, dense_gu, dense_down, router, expert_gu, expert_down, out):
    F32, I32, U32 = mybir.dt.float32, mybir.dt.int32, mybir.dt.uint32
    ACT, ALU, AX = mybir.ActivationFunctionType, mybir.AluOpType, mybir.AxisListType
    MUL, ADD, SUB = ALU.mult, ALU.add, ALU.subtract

    ctx = ExitStack()
    with ctx:
        def sb(name, shape, dt=F32):
            return ctx.enter_context(nc.sbuf_tensor(name, shape, dt))

        def sem(name):
            return ctx.enter_context(nc.semaphore(name))

        F32R = mybir.dt.float32r
        ring = sb("ring", [P, RING, BLK])
        w_hi = sb("w_hi", [P, NS, BLK], F32R)
        w_lo = sb("w_lo", [P, NS, BLK], F32R)
        h_hi = sb("h_hi", [P, 2560], F32R)
        h_lo = sb("h_lo", [P, 2560], F32R)
        x = sb("x", [P, TT, D])
        v_first = sb("v_first", [P, TT, RW])
        vec = sb("vec", [P, NV])
        col = sb("col", [P, DEPTH, NCOL])
        vresd_w = sb("vresd_w", [P, KD, VR])
        router_w = sb("router_w", [P, KD, NE])
        cst = sb("cst", [P, NCST])
        proj = sb("proj", [P, TT * (RC + VR)])
        dproj = sb("dproj", [P, TT, 3 * RW])
        NB = sb("NB", [P, 9, 1024])
        SH = sb("SH", [P, 4096])
        hN = sb("hN", [P, 2048])
        hT = sb("hT", [P, 2048])
        W1 = sb("W1", [P, 1024])
        state = sb("state", [P, 4, P])
        keep = sb("keep", [P, 4, P])
        rope = sb("rope", [P, 4, TT * 8])
        posi = sb("posi", [P, TT], I32)
        st = sb("st", [P, 192])
        psum = [ctx.enter_context(nc.psum_tensor(f"psum{b}", [P, 512], F32)) for b in range(8)]

        def C(name):
            a, w = CST[name]
            return cst[:, a:a + w]

        def V(name):
            a, w = VEC[name]
            return vec[:, a:a + w]

        def bc(ap, *shape):
            return ap.to_broadcast([P, *shape])

        def half_cols(m, b, q):
            return m.rearrange("p (n q b) -> p n q b", q=2, b=b)[:, :, q, :]

        def halves(m, b):
            return m.rearrange("p (n b) -> p n b", b=b)

        ident = C("ident")
        pv = proj[:, :].rearrange("p (t c) -> p t c", t=TT)
        prev = SH[:, 0:TT * (RC + VR)].rearrange("p (t c) -> p t c", t=TT)
        nbf = NB[:, :, :].rearrange("p a b -> p (a b)")

        mu = nbf[:, 0:NMU]
        lora_w = NB[:, 6, 0:RW]
        gate_w = NB[:, 7, 0:RW]
        vres_w = NB[0:VR, 7, RW:2 * RW]

        def nb(i):
            return NB[:, i, :].rearrange("p (t c) -> p t c", t=TT)
        A_, G_, EC, ENC, ECP, KK, B_, RHO, TMP = range(9)
        hNv = hN[:, :].rearrange("p (t c) -> p t c", t=TT)
        hTv = hT[:, :].rearrange("p (k t) -> p k t", k=KD)
        arT = hN[:, 0:1024].rearrange("p (b q t) -> p b q t", b=4, q=2)
        bT = hN[:, 1024:1536].rearrange("p (b t) -> p b t", b=4)
        kT = hN[:, 1536:2048].rearrange("p (b t) -> p b t", b=4)
        mats = SH[:, :].rearrange("p (h q t) -> p h q t", h=8, q=4)
        Tm = hT[:, 0:1024].rearrange("p (h t) -> p h t", h=8)
        TTm = hT[:, 1024:2048].rearrange("p (h t) -> p h t", h=8)
        Xm = NB[:, KK, :].rearrange("p (h t) -> p h t", h=8)
        Cm = NB[:, A_, :].rearrange("p (h t) -> p h t", h=8)
        aiT = W1[:, 0:512].rearrange("p (b t) -> p b t", b=4)
        U_ = W1[:, 512:1024]
        SA0 = NB[:, TMP, 0:512]
        SA = NB[:, TMP, 512:1024]
        yraw = nb(EC)
        lT = W1[:, 0:512].rearrange("p (b t) -> p b t", b=2)
        vrT = U_[0:VR, 0:256]
        sb_items = sb("items", [1, 4], I32)
        ss, ss2, rst, rtmp = st[:, 0:32], st[:, 32:64], st[:, 64:96], st[:, 96:128]
        sm = st[:, 128:192]

        ready = [sem(f"psum_ready{b}") for b in range(8)]
        evacuated = [sem(f"psum_evacuated{b}") for b in range(8)]
        B = Banks(psum, ready, evacuated)
        block_in = [sem(f"block_in{s}") for s in range(RING)]
        block_used, hi_done, lo_done = sem("block_used"), sem("weights_hi"), sem("weights_lo")
        h_hi_done, h_split = sem("h_hi_done"), sem("h_lo_done")
        mu_in = sem("mu_in")
        x_in_s, small_in, vec_in, mem_in_s, out_s = sem("x_in"), sem("small_in"), sem("vec_in"), sem("mem_in"), sem("out_s")
        lw_in = sem("layer_weights_in")
        dve_step, act_step, pool_step = sem("dve_step"), sem("act_step"), sem("pool_step")
        sq_done, hn_done = sem("squares_done"), sem("normed")
        msq_done, mn_done = sem("mem_squares_done"), sem("mem_normed")
        shifted_in = [sem(f"shifted_in{g}") for g in range(5)]
        row0_ready, lora_ready, sg_scan, rate_done, vmix_done = (sem("row0_cleared"), sem("lora_shifted"), sem("decay_sigmoid"),
                                                                 sem("rate_sigmoid"), sem("value_mix_sigmoid"))
        v_final, expc, elem, qs_ready = sem("v_final"), sem("exp_cum_done"), sem("recurrence_inputs"), sem("qk_roped")
        c_ready, t_ready, state_ready, sa_ready = sem("C_masked"), sem("T_started"), sem("state_ready"), sem("SA_ready")
        keep_ready, ycat, smx, pexp, attn_ready = sem("keep_ready"), sem("y_cat"), sem("row_max"), sem("p_exp"), sem("attn_ready")
        lam_in, lam_exp, rope_in, rope_sin = sem("lambda_in"), sem("lambda_exp"), sem("rope_in"), sem("rope_sin")
        xq_n, xk_n, xs_mx = sem("xq_normed"), sem("xk_normed"), sem("x_row_max")
        silu_done, w_in, w_sig, rt_sel, items_in = sem("silu_done"), sem("gate_in"), sem("gate_sigmoid"), sem("selected"), sem("items_ready")
        sel_done, final = sem("selection_done"), sem("final")
        act_hi = sem("hidden_hi_done")

        def rows(w, k0, c0, cw):
            return w[k0 * P:(k0 + 2) * P, c0:c0 + cw].rearrange("(k p) n -> p k n", p=P)
        chunks_in = [(0, 512), (512, 512), (1024, 512), (1536, 256), (1792, 512), (2304, 512), (2816, 512)]

        def square_blocks(w, cs):
            return [("w", rows(w, k0, c0, cw), cw) for c0, cw in cs for k0 in range(0, KD, 2)]

        def half_chunks(n):
            return [(c * 512, 512) for c in range(n)]

        GU = [(0, 0), (0, 1), (1, 0), (1, 1)]

        def gu_block(w, c, g, half):
            c0 = g * (w.shape[-1] // 2) + c * FC
            return w[half * 512:(half + 1) * 512, c0:c0 + FC].rearrange("(k p) f -> p k f", p=P)

        def down_block(w, c, k):
            return w[c * FC + k * P:c * FC + (k + 1) * P, :]

        blocks = []
        for l in range(DEPTH):
            blocks += square_blocks(in_proj[l], chunks_in)
            blocks += square_blocks(out_proj[l], half_chunks(2))
            blocks += square_blocks(wq[l], half_chunks(2))
            blocks += square_blocks(wkv[l], half_chunks(4))
            blocks += square_blocks(wo[l], half_chunks(2))
            if l == 0:
                for c in range(FD // FC + 1):
                    if c < FD // FC:
                        blocks += [("gu", gu_block(dense_gu[0], c, *g), 0) for g in GU]
                    if c:
                        blocks += [("down", down_block(dense_down[0], c - 1, k), 0) for k in range(2)]
        NPRE = len(blocks)
        STEPS = FE // FC
        PER = 6 * STEPS
        assert PER % RING == 0 and PER % NS == 0

        def slot_view(s, kind, cw):
            return shaped(ring[:, s, :], kind, cw)

        def shaped(w, kind, cw):
            if kind == "down":
                return w
            k, cw = (4, FC) if kind == "gu" else (2, cw)
            return w[:, 0:k * cw].rearrange("p (k f) -> p k f", k=k)

        MOE_PER = [STEPS // 2, STEPS // 2, STEPS, 1, 1, 1, 3, 3]
        MOE_USED = 5 * STEPS - 1
        freed = []

        def splitter(eng, one):
            n = [0]

            def to(m):
                while n[0] < min(m, NPRE):
                    one(n[0], n[0], 0)
                    n[0] += 1

            def ahead(name, more=0):
                to(B.before[name] + NS + more)
            return to, ahead

        def hi_of(act, n, m, i):
            act.wait_ge(block_in[n % RING], 16 * (n // RING + 1) + i * (16 * PER // RING))
            if n >= NPRE and m < NS:
                bank, nth = B.use[("ey", 1)]
                act.wait_ge(ready[bank], nth + i * MOE_PER[bank])
            elif n >= NS:
                s_, v_, per = freed[n - NS]
                act.wait_ge(s_, v_ + i * per)
            act.activation(w_hi[:, n % NS, :], ring[:, n % RING, :], ACT.Copy).then_inc(hi_done, 1)

        def lo_of(dve, n, i):
            dve.wait_ge(hi_done, n + 1 + i * PER)
            dve.tensor_tensor(w_lo[:, n % NS, :], ring[:, n % RING, :], w_hi[:, n % NS, :].bitcast(F32), SUB).then_inc(lo_done, 1)

        LO_PARTS = {}
        for l in range(DEPTH):
            for name in (("hT", l, 0), ("hT", l, 1), ("hT", l, 2), ("mT", l), ("oT", l), ("hT", l, 3)):
                LO_PARTS[name] = 4 * (len(LO_PARTS) + 1)

        H_SPLIT0 = 4 * len(LO_PARTS)

        block = ctx.enter_context(nc.Block())

        @block.tensor
        def _(pe):
            at = B.taken
            n_used = [0]
            work = [0]

            def take(kind, cw=512):
                n = at[0]
                at[0] += 1
                pe.wait_ge(lo_done, n + 1)
                return shaped(w_hi[:, n % NS, :], kind, cw), shaped(w_lo[:, n % NS, :], kind, cw)

            def product(o, h, w, start, stop):
                pe.matmul(o, h[0], w[0], start=start, stop=False, skip_group_check=True)
                pe.matmul(o, h[0], w[1], start=False, stop=False, skip_group_check=True)
                return pe.matmul(o, h[1], w[0], start=False, stop=stop, skip_group_check=True)

            def used(last):
                last.then_inc(block_used, 1)
                n_used[0] += 1
                freed.append((block_used, n_used[0], MOE_USED))

            def used_with(name):
                bank, nth = B.use[name]
                freed.append((ready[bank], nth + 1, MOE_PER[bank]))

            def open_work(name):
                work[0] += 1
                return B.open(pe, name, 4 + (work[0] - 1) % 4)
            nproj = [0]

            def transposes(name, srcs, opener=None):
                bank = (opener or open_work)(name)
                for i, s in enumerate(srcs):
                    n = s.shape[0]
                    m = s.shape[1]
                    last = pe.transpose(bank[0:m, i * P:i * P + n], s, ident[0:n, 0:n])
                B.filled(last, name)

            def to_hT(name, src, wait):
                for t in range(TT):
                    wait(t)
                    for g in range(2):
                        transposes((*name, t, g), [src[:, t, (4 * g + i) * P:(4 * g + i + 1) * P] for i in range(4)])

            def project_steps(name, n_cols, src_ready):
                for c, (c0, cw) in enumerate(n_cols):
                    banks = []
                    for t in range(TT):
                        banks.append(B.open(pe, (*name, c, t), nproj[0] % 4))
                        nproj[0] += 1
                    if c == 0:
                        src_ready()
                    for kb in range(0, KD, 2):
                        wh, wl = take("w", cw)
                        for t in range(TT):
                            for k in range(2):
                                last = product(banks[t][:, 0:cw], lhs_h(kb + k, t), (wh[:, k, :], wl[:, k, :]), kb + k == 0, kb + k == 7)
                            if kb == KD - 2:
                                B.filled(last, (*name, c, t))
                        if kb == KD - 2:
                            used_with((*name, c, TT - 1))
                        else:
                            used(last)
                        yield

            def project(name, n_cols, src_ready):
                for _ in project_steps(name, n_cols, src_ready):
                    pass

            pe.wait_ge(small_in, 48)

            def lhs_h(kk, t):
                a = kk * SEQ + t * P
                return h_hi[:, a:a + P], h_lo[:, a:a + P]

            def h_ready(name):
                def wait():
                    for t in range(TT):
                        for g in range(2):
                            B.wait_evacuated(pe, (*name, t, g))
                    pe.wait_ge(h_split, LO_PARTS[name])
                return wait

            for l in range(DEPTH):
                to_hT(("hT", l, 0), hNv, lambda t: pe.wait_ge(hn_done, 2 * 3 * l + t + 1))
                project(("in", l), chunks_in[0:4], h_ready(("hT", l, 0)))
                if l:
                    pe.wait_ge(lw_in, 80)
                    for t in range(TT):
                        bank = B.open(pe, ("vr", l, t), nproj[0] % 4)
                        nproj[0] += 1
                        for k in range(KD):
                            last = pe.matmul(bank[:, 0:VR], hTv[:, k, t * P:(t + 1) * P], vresd_w[:, k, :], start=(k == 0), stop=(k == 7))
                        B.filled(last, ("vr", l, t))
                rest = project_steps(("inb", l), chunks_in[4:], lambda: None)

                def fill(n):
                    for _ in range(n):
                        next(rest, None)
                fill(2)
                pe.wait_ge(lora_ready, l + 1)
                transposes(("lt", l), [pv[:, t, 1536 + b * P:1536 + (b + 1) * P] for b in range(2) for t in range(TT)])
                if l:
                    pe.wait_ge(lora_ready, l + 2)
                    transposes(("vt", l), [pv[:, t, RC:RC + VR] for t in range(TT)])
                fill(1)
                pe.wait_ge(lw_in, 80 + 64 * l)
                B.wait_evacuated(pe, ("lt", l))
                for t in range(TT):
                    ts = slice(t * P, (t + 1) * P)
                    for name, lhs, rhs in (("wup", lT[0:64, 0, ts], lora_w[0:64, :]), ("aup", lT[64:128, 0, ts], lora_w[64:128, :]),
                                           ("gup", lT[:, 1, ts], gate_w[:, :])):
                        bank = open_work((name, l, t))
                        B.filled(pe.matmul(bank[:, :], lhs, rhs, start=True, stop=True), (name, l, t))
                    if l:
                        if t == 0:
                            B.wait_evacuated(pe, ("vt", l))
                        bank = open_work(("vup", l, t))
                        B.filled(pe.matmul(bank[:, :], vrT[:, ts], vres_w[:, :], start=True, stop=True), ("vup", l, t))
                for t in range(TT):
                    if t == 0:
                        fill(1)
                    pe.wait_ge(sg_scan, TT * l + t + 1)
                    for name, m in (("cum", C("tri")), ("cums", C("tri_s"))):
                        bank = open_work((name, l, t))
                        B.filled(pe.matmul(bank[:, :], m, nb(TMP)[:, t, :], start=True, stop=True), (name, l, t))
                fill(1)
                pe.wait_ge(expc, 2 * l + 2)
                bank = open_work(("wt", l))
                for t in range(TT):
                    for b in range(4):
                        last = pe.matmul(bank[:, (t * 4 + b) * 2:(t * 4 + b) * 2 + 2], nb(EC)[:, t, b * P:(b + 1) * P], C("last"),
                                         start=True, stop=True)
                B.filled(last, ("wt", l))

                fill(5)
                for t in range(TT):
                    pe.wait_ge(elem, l + 1)
                    for name, q in (("aT", ECP), ("rT", RHO), ("bT", B_), ("kT", ENC)):
                        transposes((name, l, t), [nb(q)[:, t, b * P:(b + 1) * P] for b in range(4)])
                    for name in ("aT", "rT", "bT", "kT"):
                        B.wait_evacuated(pe, (name, l, t))
                    for h in (0, 2, 4, 6, 1, 3, 5, 7):
                        b, r = h // 2, slice(64 * (h % 2), 64 * (h % 2) + 64)
                        bank = open_work(("m12", l, t, h))
                        pe.matmul(bank[:, 0:256], bT[r, b, :], arT[r, b, :, :].rearrange("p q t -> p (q t)"), start=True, stop=True)
                        B.filled(pe.matmul(bank[:, 256:512], kT[r, b, :], arT[r, b, :, :].rearrange("p q t -> p (q t)"),
                                           start=True, stop=True), ("m12", l, t, h))
                    for par in range(2):
                        r = slice(64 * par, 64 * par + 64)
                        bank = open_work(("m3", l, t, par))
                        for b in range(4):
                            last = pe.matmul(bank[:, b * P:(b + 1) * P], arT[r, b, 0, :], bT[r, b, :], start=True, stop=True)
                        B.filled(last, ("m3", l, t, par))
                    for par in range(2):
                        for h in range(par, 8, 2):
                            B.wait_evacuated(pe, ("m12", l, t, h))
                    bank = open_work(("U", l, t))
                    for h in range(8):
                        last = pe.matmul(bank[:, h * HD:(h + 1) * HD], mats[:, h, 2, :], pv[:, t, 2 * RW + h * HD:2 * RW + (h + 1) * HD],
                                         start=True, stop=True)
                    B.filled(last, ("U", l, t))
                    for lv in range(5):
                        for g in range(2):
                            pe.wait_ge(c_ready, 10 * (TT * l + t) + lv * 2 + g + 1)
                            if lv == 0:
                                pe.wait_ge(t_ready, TT * l + t + 1)
                            else:
                                B.wait_evacuated(pe, ("Z", l, t, lv - 1, g))
                                B.wait_evacuated(pe, ("ZT", l, t, lv - 1, g))
                            bank = open_work(("X", l, t, lv, g))
                            for h in range(4 * g, 4 * g + 4):
                                last = pe.matmul(bank[:, (h % 4) * P:(h % 4 + 1) * P], Cm[:, h, :], Tm[:, h, :], start=True, stop=True)
                            B.filled(last, ("X", l, t, lv, g))
                        fill(t == 0 and lv % 2 == 0)
                        b2 = 2 << lv
                        for g in range(2):
                            B.wait_evacuated(pe, ("X", l, t, lv, g))
                            if lv < 4:
                                bank = open_work(("Z", l, t, lv, g))
                                for h in range(4 * g, 4 * g + 4):
                                    last = pe.matmul(halves(bank[:, (h % 4) * 64:(h % 4 + 1) * 64], b2), TTm[:, h, :], half_cols(Xm[:, h, :], b2, 0),
                                                     start=True, stop=True)
                                B.filled(last, ("Z", l, t, lv, g))
                            bank = open_work(("ZT", l, t, lv, g))
                            for h in range(4 * g, 4 * g + 4):
                                last = pe.matmul(halves(bank[:, (h % 4) * 64:(h % 4 + 1) * 64], b2), Xm[:, h, :], half_cols(TTm[:, h, :], b2, 1),
                                                 start=True, stop=True)
                            B.filled(last, ("ZT", l, t, lv, g))
                    for g in range(2):
                        B.wait_evacuated(pe, ("ZT", l, t, 4, g))
                    for par in range(2):
                        bank = open_work(("ai", l, t, par))
                        for h in range(par, 8, 2):
                            last = pe.matmul(bank[64 * par:64 * par + 64, (h // 2) * P:(h // 2 + 1) * P],
                                             nb(ECP)[:, t, h * HD:(h + 1) * HD], TTm[:, h, :], start=True, stop=True)
                        B.filled(last, ("ai", l, t, par))
                    B.wait_evacuated(pe, ("U", l, t))
                    bank = open_work(("SA0", l, t))
                    for h in range(8):
                        last = pe.matmul(bank[:, h * HD:(h + 1) * HD], TTm[:, h, :], U_[:, h * HD:(h + 1) * HD], start=True, stop=True)
                    B.filled(last, ("SA0", l, t))
                    for par in range(2):
                        B.wait_evacuated(pe, ("ai", l, t, par))
                    ybank = None
                    for p in range(2):
                        tk = slice(64 * p, 64 * p + 64)
                        n = 2 * (TT * l + t) + p
                        pe.wait_ge(state_ready, n + l + 1)
                        bank = open_work(("sa", l, t, p))
                        for b in range(4):
                            last = pe.matmul(bank[tk, b * P:(b + 1) * P], aiT[:, b, tk], state[:, b, :], start=True, stop=True)
                        B.filled(last, ("sa", l, t, p))
                        bank = open_work(("y1", l, t, p))
                        for b in range(4):
                            last = pe.matmul(bank[tk, b * P:(b + 1) * P], arT[:, b, 1, tk], state[:, b, :], start=True, stop=True)
                        B.filled(last, ("y1", l, t, p))
                        bank = open_work(("s", l, t, p))
                        pe.wait_ge(sa_ready, n + 1)
                        for b in range(4):
                            cs = slice(b * P, (b + 1) * P)
                            pe.matmul(bank[:, cs], nb(ENC)[tk, t, cs], pv[tk, t, 2 * RW + b * P:2 * RW + (b + 1) * P], start=True, stop=False)
                            last = pe.matmul(bank[:, cs], nb(B_)[tk, t, cs], SA[tk, cs], start=False, stop=True)
                        B.filled(last, ("s", l, t, p))
                    bank = open_work(("y2", l, t))
                    for h in range(8):
                        hs = slice(h * HD, (h + 1) * HD)
                        pe.matmul(bank[:, hs], mats[:, h, 1, :], SA[:, hs], start=True, stop=False)
                        last = pe.matmul(bank[:, hs], mats[:, h, 3, :], pv[:, t, 2 * RW + h * HD:2 * RW + (h + 1) * HD],
                                         start=False, stop=True)
                    B.filled(last, ("y2", l, t))

                qT = hT[:, 0:1024].rearrange("p (h t) -> p h t", h=4)
                kTd = hT[:, 1024:2048].rearrange("p (h t) -> p h t", h=4)
                pe.wait_ge(qs_ready, l + 1)
                for which in range(2):
                    for t in range(TT):
                        transposes(("qkT", l, which, t), [dproj[:, t, which * RW + h * P:which * RW + (h + 1) * P] for h in range(4)])
                for which in range(2):
                    for t in range(TT):
                        B.wait_evacuated(pe, ("qkT", l, which, t))
                aT = W1[:, :].rearrange("p (s n) -> p s n", s=2)

                def diff_scores(h):
                    for m in range(2):
                        r = slice(64 * m, 64 * m + 64)
                        bank = open_work(("ds", l, h, m))
                        pe.matmul(bank[:, 0:128], qT[r, h, 0:128], kTd[r, h, 0:128], start=True, stop=True)
                        B.filled(pe.matmul(bank[:, 128:384], qT[r, h, 128:256], kTd[r, h, :], start=True, stop=True), ("ds", l, h, m))
                diff_scores(0)
                for h in range(4):
                    if h < 3:
                        diff_scores(h + 1)
                    pe.wait_ge(attn_ready, 4 * l + h + 1)
                    bank = open_work(("atT", l, h))
                    att = SH[:, 2304 + 384 * (h % 2):2304 + 384 * (h % 2) + 384]
                    for i in range(3):
                        last = pe.transpose(bank[:, i * P:(i + 1) * P], att[:, i * P:(i + 1) * P], ident)
                    B.filled(last, ("atT", l, h))
                    B.wait_evacuated(pe, ("atT", l, h))
                    bank = open_work(("pv", l, h))
                    vv = [dproj[:, t, 2 * RW + h * DV:2 * RW + (h + 1) * DV] for t in range(TT)]
                    pe.matmul(bank[:, 0:128], aT[:, h % 2, 0:128], vv[0], start=True, stop=True)
                    pe.matmul(bank[:, 128:256], aT[:, h % 2, 128:256], vv[0], start=True, stop=False)
                    B.filled(pe.matmul(bank[:, 128:256], aT[:, h % 2, 256:384], vv[1], start=False, stop=True), ("pv", l, h))
                to_hT(("hT", l, 1), hNv, lambda t: pe.wait_ge(ycat, 2 * l + 2))
                project(("op", l), half_chunks(2), h_ready(("hT", l, 1)))

                to_hT(("hT", l, 2), hNv, lambda t: pe.wait_ge(hn_done, 2 * (3 * l + 1) + t + 1))
                project(("xq", l), half_chunks(2), h_ready(("hT", l, 2)))
                memn = nbf[:, 4096:6144].rearrange("p (t c) -> p t c", t=TT)
                to_hT(("mT", l), memn, lambda t: pe.wait_ge(mn_done, 2 * l + t + 1))
                project(("kv", l), half_chunks(4), h_ready(("mT", l)))
                qn = proj[:, 0:2048].rearrange("p (t c) -> p t c", t=TT)
                kn = dproj[:, :, :].rearrange("p t c -> p (t c)")[:, 0:2048].rearrange("p (t c) -> p t c", t=TT)
                vx = SH[:, 0:2048].rearrange("p (t c) -> p t c", t=TT)
                kTx = nbf[:, 0:2048].rearrange("p (k t) -> p k t", k=KD)
                qTx = nbf[:, 2048:4096].rearrange("p (k t) -> p k t", k=KD)
                to_hT(("xqT", l), qn, lambda t: pe.wait_ge(xq_n, l + 1))
                to_hT(("xkT", l), kn, lambda t: pe.wait_ge(xk_n, l + 1))
                for nm in ("xqT", "xkT"):
                    for t in range(TT):
                        for g in range(2):
                            B.wait_evacuated(pe, (nm, l, t, g))
                PT = nbf[:, 8192:9216].rearrange("p (s n) -> p s n", s=2)
                px = SH[:, 2048:3072].rearrange("p (s q k) -> p s q k", s=2, q=2)

                def x_scores(h):
                    bank = open_work(("xs", l, h))
                    for t in range(TT):
                        for kb in range(2):
                            last = pe.matmul(bank[:, t * 256:(t + 1) * 256], qTx[:, 2 * h + kb, t * P:(t + 1) * P], kTx[:, 2 * h + kb, :],
                                             start=(kb == 0), stop=(kb == 1))
                    B.filled(last, ("xs", l, h))
                x_scores(0)
                for h in range(XH):
                    if h < XH - 1:
                        x_scores(h + 1)
                    B.wait_evacuated(pe, ("xs", l, h))
                    transposes(("xpT", l, h), [px[:, h % 2, q, m * P:(m + 1) * P] for m in range(2) for q in range(2)])
                    B.wait_evacuated(pe, ("xpT", l, h))
                    bank = open_work(("xo", l, h))
                    for q in range(TT):
                        for m in range(2):
                            last = pe.matmul(bank[:, q * 256:(q + 1) * 256], PT[:, h % 2, (m * 2 + q) * P:(m * 2 + q + 1) * P],
                                             vx[:, m, h * XD:(h + 1) * XD], start=(m == 0), stop=(m == 1))
                    B.filled(last, ("xo", l, h))
                on = memn
                to_hT(("oT", l), on, lambda t: [B.wait_evacuated(pe, ("xo", l, h)) for h in range(XH)])
                project(("wo", l), half_chunks(2), h_ready(("oT", l)))

                to_hT(("hT", l, 3), hNv, lambda t: pe.wait_ge(hn_done, 2 * (3 * l + 2) + t + 1))
                if l == 0:
                    h_ready(("hT", l, 3))()
                    nch = FD // FC
                    ybanks = []
                    act = nbf[:, 0:1024].rearrange("p (s t n) -> p s t n", s=2, t=2)

                    def hidden_T(c):
                        bank = B.open(pe, ("fT", c), 2 + c % 2)
                        for k in range(2):
                            for t in range(TT):
                                if k == 0:
                                    B.wait_evacuated(pe, ("gu", c, t))
                                last = pe.transpose(bank[:, (k * 2 + t) * P:(k * 2 + t + 1) * P], act[:, c % 2, t, k * P:(k + 1) * P], ident)
                        B.filled(last, ("fT", c))

                    def down(c):
                        B.wait_evacuated(pe, ("fT", c))
                        if c == 0:
                            ybanks.extend(B.open(pe, ("fy", i), 4 + i) for i in range(4))
                        for k in range(2):
                            wh, wl = take("down")
                            for t in range(TT):
                                a = 2048 + k * SEQ + t * P
                                for n in range(2):
                                    ns = slice(n * 512, (n + 1) * 512)
                                    last = product(ybanks[t * 2 + n][:, :], (h_hi[:, a:a + P], h_lo[:, a:a + P]), (wh[:, ns], wl[:, ns]),
                                                   c == 0 and k == 0, c == nch - 1 and k == 1)
                                    if c == nch - 1 and k == 1:
                                        B.filled(last, ("fy", t * 2 + n))
                            if c == nch - 1 and k == 1:
                                used_with(("fy", 3))
                            else:
                                used(last)
                    for c in range(nch):
                        banks = [B.open(pe, ("gu", c, t), t) for t in range(TT)]
                        for j, (g, half) in enumerate(GU):
                            wh, wl = take("gu")
                            for t in range(TT):
                                for k in range(4):
                                    last = product(banks[t][:, g * FC:(g + 1) * FC], lhs_h(half * 4 + k, t), (wh[:, k, :], wl[:, k, :]),
                                                   half == 0 and k == 0, half == 1 and k == 3)
                                if j == 3:
                                    B.filled(last, ("gu", c, t))
                            if j == 3:
                                used_with(("gu", c, TT - 1))
                            else:
                                used(last)
                            if j == 1 and c:
                                hidden_T(c - 1)
                        if c:
                            down(c - 1)
                    hidden_T(nch - 1)
                    down(nch - 1)

            assert at[0] == NPRE == len(freed)
            l = 1
            h_ready(("hT", l, 3))()
            pe.wait_ge(lw_in, 80)
            bank = B.open(pe, ("logit",), 6)
            for t in range(TT):
                for k in range(KD):
                    last = pe.matmul(bank[:, t * NE:(t + 1) * NE], hTv[:, k, t * P:(t + 1) * P], router_w[:, k, :], start=(k == 0), stop=(k == KD - 1))
            B.filled(last, ("logit",))
            sel = nbf[:, 8192:8192 + 2 * NE].rearrange("p (t e) -> p t e", t=TT)
            pe.wait_ge(rt_sel, 1)
            bank = B.open(pe, ("pos",), 7)
            pe.matmul(bank[:, 0:8], C("utri"), sel[:, 0, :], start=True, stop=True)
            pe.matmul(bank[:, 8:16], C("ones"), sel[:, 0, :], start=True, stop=False)
            pe.matmul(bank[:, 8:16], C("utri"), sel[:, 1, :], start=False, stop=True)
            pe.matmul(bank[:, 16:24], C("ones"), sel[:, 0, :], start=True, stop=False)
            B.filled(pe.matmul(bank[:, 16:24], C("ones"), sel[:, 1, :], start=False, stop=True), ("pos",))

            start, start_used = list(B.n), n_used[0]

            def expert(i):
                B.n = list(start)
                n_used[0] = start_used
                del freed[NPRE:]

                def more(bank):
                    return i * MOE_PER[bank]

                def open_(name, bank):
                    return B.open(pe, name, bank, more(bank))

                def take_e(j, kind):
                    n = NPRE + j
                    pe.wait_ge(lo_done, n + 1 + i * PER)
                    return shaped(w_hi[:, n % NS, :], kind, 512), shaped(w_lo[:, n % NS, :], kind, 512)
                pe.wait_ge(sel_done, i * 2 + 1)
                Psel = nbf[:, 2048:2304].rearrange("p (t j) -> p t j", t=TT)
                Pg = nbf[:, 2304:2560].rearrange("p (t j) -> p t j", t=TT)
                PgT = nbf[:, 2560:2816]
                for g in range(2):
                    bank = open_(("he", g), 6 + g)
                    for k in range(4):
                        for t in range(TT):
                            last = pe.matmul(bank[:, k * P:(k + 1) * P], hNv[:, t, (4 * g + k) * P:(4 * g + k + 1) * P], Psel[:, t, :],
                                             start=(t == 0), stop=(t == 1))
                    B.filled(last, ("he", g))
                pe.wait_ge(sel_done, i * 2 + 2)
                bank = open_(("pgT",), 3)
                for t in range(TT):
                    last = pe.transpose(bank[:, t * P:(t + 1) * P], Pg[:, t, :], ident)
                B.filled(last, ("pgT",))
                pe.wait_ge(h_split, H_SPLIT0 + 1 + i)
                act = nbf[:, 0:512].rearrange("p (s n) -> p s n", s=2)
                ybanks = []

                def hidden_T(c):
                    bank = open_(("eT", c), 2)
                    B.wait_evacuated(pe, ("egu", c), more(c % 2))
                    for k in range(2):
                        last = pe.transpose(bank[:, k * P:(k + 1) * P], act[:, c % 2, k * P:(k + 1) * P], ident)
                    B.filled(last, ("eT", c))

                def down(c):
                    B.wait_evacuated(pe, ("eT", c), more(2))
                    if c == 0:
                        ybanks.extend(open_(("ey", n), 4 + n) for n in range(2))
                    for k in range(2):
                        wh, wl = take_e(6 * c + 8 + k if c < STEPS - 1 else 6 * c + 4 + k, "down")
                        a = 2048 + k * P
                        for n in range(2):
                            ns = slice(n * 512, (n + 1) * 512)
                            last = product(ybanks[n][:, :], (h_hi[:, a:a + P], h_lo[:, a:a + P]), (wh[:, ns], wl[:, ns]),
                                           c == 0 and k == 0, c == STEPS - 1 and k == 1)
                            if c == STEPS - 1 and k == 1:
                                B.filled(last, ("ey", n))
                        if c == STEPS - 1 and k == 1:
                            used_with(("ey", 1))
                        else:
                            used(last)
                for c in range(STEPS):
                    bank = open_(("egu", c), c % 2)
                    for j, (g, half) in enumerate(GU):
                        wh, wl = take_e((6 * c - 2 if c else 0) + j, "gu")
                        for k in range(4):
                            a = (half * 4 + k) * P
                            last = product(bank[:, g * FC:(g + 1) * FC], (h_hi[:, a:a + P], h_lo[:, a:a + P]), (wh[:, k, :], wl[:, k, :]),
                                           half == 0 and k == 0, half == 1 and k == 3)
                        if j < 3:
                            used(last)
                        else:
                            B.filled(last, ("egu", c))
                            used_with(("egu", c))
                        if j == 1 and c:
                            hidden_T(c - 1)
                    if c:
                        down(c - 1)
                hidden_T(STEPS - 1)
                down(STEPS - 1)
                B.wait_evacuated(pe, ("pgT",), more(3))
                for n in range(2):
                    B.wait_evacuated(pe, ("ey", n), more(4 + n))
                Ysb = nbf[:, 4096:5120]
                for t in range(TT):
                    for n in range(2):
                        name = ("sc", t, n)
                        bank = open_(name, 6 + n)
                        B.filled(pe.matmul(bank[:, :], PgT[:, t * P:(t + 1) * P], Ysb[:, n * 512:(n + 1) * 512], start=True, stop=True), name)

            with pe.Fori(0, NE) as i:
                expert(i)
            pe.wait_ge(items_in, 1)
            n_over = pe.value_load(sb_items[0:1, 0:1], min_val=0, max_val=NOVER)
            with pe.If(n_over > 0):
                with pe.Fori(NE, n_over + NE) as i:
                    expert(i)

        @block.sync
        def _(sp):
            sp.dma_start(cst[:, :], consts).then_inc(small_in, 16)
            for n, (kind, src, cw) in enumerate(blocks):
                if n >= RING:
                    sp.wait_ge(lo_done, n - RING + 1)
                sp.dma_start(slot_view(n % RING, kind, cw), src).then_inc(block_in[n % RING], 16)

            def expert_blocks(e, i):
                j = 0
                for c in range(STEPS + 1):
                    todo = [gu(e, c, *g) for g in GU] if c < STEPS else []
                    todo += [down(e, c - 1, k) for k in range(2)] if c else []
                    for kind, src in todo:
                        sp.wait_ge(lo_done, NPRE + j - RING + 1 + i * PER)
                        s = (NPRE + j) % RING
                        sp.dma_start(slot_view(s, kind, 0), src).then_inc(block_in[s], 16)
                        j += 1

            def gu(e, c, g, half):
                c0 = g * FE + c * FC
                return "gu", expert_gu[0, bass.ds(e, 1), half * 512:(half + 1) * 512, c0:c0 + FC].rearrange("a (k p) f -> p (a k) f", p=P)

            def down(e, c, k):
                return "down", expert_down[0, bass.ds(e, 1), c * FC + k * P:c * FC + (k + 1) * P, :].rearrange("a p n -> p (a n)")
            with sp.Fori(0, NE) as i:
                expert_blocks(i, i)
            sp.wait_ge(items_in, 1)
            n_over = sp.value_load(sb_items[0:1, 0:1], min_val=0, max_val=NOVER)
            with sp.If(n_over > 0):
                with sp.Fori(NE, n_over + NE) as i:
                    e = sp.value_load(sb_items[0:1, bass.ds(i - (NE - 1), 1)], min_val=0, max_val=NE - 1)
                    expert_blocks(e, i)
            sp.wait_ge(final, 1)
            sp.dma_start(out[0].rearrange("(t p) d -> p t d", p=P), x[:, :, :]).then_inc(out_s, 16)
            sp.wait_ge(out_s, 16)

        @block.gpsimd
        def _(pool):
            n = [0]

            def step(ins):
                n[0] += 1
                ins.then_inc(pool_step, 1)
                pool.wait_ge(pool_step, n[0])
            for w, s in ((vresd_w[:, :, :], vres_down[0].rearrange("(k p) n -> p k n", p=P)),
                         (router_w[:, :, :], router[0].rearrange("(k p) n -> p k n", p=P))):
                pool.dma_start(w, s).then_inc(lw_in, 16)
            pool.dma_start(vec[:, :], vecs[0].partition_broadcast(P)).then_inc(vec_in, 16)
            for l in range(DEPTH):
                if l:
                    pool.wait_ge(ycat, 2 * l)
                    pool.dma_start(vec[:, :], vecs[l].partition_broadcast(P)).then_inc(vec_in, 16)
                    B.wait_evacuated(pool, ("wo", l - 1, 1, 1))
                pool.dma_start(lora_w[0:64, :], decay_up[l]).then_inc(lw_in, 16)
                pool.dma_start(lora_w[64:128, :], iclr_up[l]).then_inc(lw_in, 16)
                pool.dma_start(gate_w, gate_up[l]).then_inc(lw_in, 16)
                if l:
                    pool.dma_start(vres_w, vres_up[l - 1]).then_inc(lw_in, 16)
                    B.wait_evacuated(pool, ("fy", 3))
                pool.dma_start(mu, mus[l].partition_broadcast(P)).then_inc(mu_in, 16)
                pool.memset(prev[0:1, 0, :], 0.0).then_inc(row0_ready, 1)
                for t in range(TT):
                    for lv in range(5):
                        for g in range(2):
                            if lv == 0:
                                for h in range(4 * g, 4 * g + 4):
                                    B.wait_evacuated(pool, ("m12", l, t, h))
                                if t:
                                    B.wait_filled(pool, ("X", l, t - 1, 4, g))
                            else:
                                B.wait_filled(pool, ("X", l, t, lv - 1, g))
                            m = C("lvl")[:, lv * P:(lv + 1) * P].unsqueeze(1)
                            pool.tensor_tensor(Cm[:, 4 * g:4 * g + 4, :], mats[:, 4 * g:4 * g + 4, 0, :], bc(m, 4, P), MUL)\
                                .then_inc(c_ready, 1)
                    for p in range(2):
                        c = TT * t + p
                        if c:
                            pool.wait_ge(state_ready, 5 * l + c + 1)
                        else:
                            B.wait_evacuated(pool, ("wt", l))
                        wts = sm[:, 0:16].rearrange("p (t b c) -> p t b c", t=TT, b=4)[:, t, :, p:p + 1]
                        pool.tensor_tensor(keep[:, :, :], bc(C("bd").unsqueeze(1), 4, P), bc(wts, 4, P), MUL).then_inc(keep_ready, 1)
                pool.wait_ge(ycat, 2 * l + 1)
                pool.dma_start(nbf[:, 4096:6144].rearrange("p (t c) -> p t c", t=TT), mem_in[0].rearrange("(t p) d -> p t d", p=P))\
                    .then_inc(mem_in_s, 16)

        @block.scalar
        def _(act):
            act.dma_start(x[:, :, :], x_in[0].rearrange("(t p) d -> p t d", p=P)).then_inc(x_in_s, 16)
            act.dma_start(col[:, :, :], cols.rearrange("l p c -> p l c")).then_inc(small_in, 16)
            act.dma_start(posi[:, :], pos_in).then_inc(small_in, 16)

            split_to, ahead = splitter(act, lambda n, m, i: hi_of(act, n, m, i))

            def copy(dst, name, src=None, scale=1.0, func=ACT.Copy):
                ahead(name)
                bank = B.wait_filled(act, name)
                B.release(act.activation(dst, bank[:, :] if src is None else src(bank), func, scale=scale), name)

            def squares(srcs, junk, cols_, done):
                for t in range(TT):
                    act.activation(junk[:, t, :], srcs[:, t, :], ACT.Square, accum_out=cols_[:, t:t + 1]).then_inc(done, 1)
            def h_parts(name):
                for t in range(TT):
                    for g in range(2):
                        ahead((*name, t, g))
                        B.wait_evacuated(act, (*name, t, g))
                        act.activation(h_hi[:, 0:2048].rearrange("p (k t) -> p k t", k=KD)[:, 4 * g:4 * g + 4, t * P:(t + 1) * P],
                                       hTv[:, 4 * g:4 * g + 4, t * P:(t + 1) * P], ACT.Copy).then_inc(h_hi_done, 1)

            act.wait_ge(x_in_s, 16)
            squares(x, hNv, sm[:, 32:34], sq_done)
            act.wait_ge(rope_in, 1)
            act.activation(rope[:, 0:2, :], rope[:, 2:4, :], ACT.Sin).then_inc(rope_sin, 1)
            for l in range(DEPTH):
                h_parts(("hT", l, 0))
                for g, (c0, cw) in enumerate(chunks_in[0:4] + ([(RC, VR)] if l else [])):
                    names = [("in", l, g, t) if g < 4 else ("vr", l, t) for t in range(TT)]
                    for t in range(TT):
                        copy(pv[:, t, c0:c0 + cw], names[t], lambda b, cw=cw: b[:, 0:cw])
                    if True:
                        for t in range(TT):
                            B.wait_evacuated(act, names[t])
                        if g == 0:
                            act.wait_ge(row0_ready, l + 1)
                        cs = slice(c0, c0 + cw)
                        act.dma_start(prev[1:113, :, cs], pv[0:112, :, cs]).then_inc(shifted_in[g], 16)
                        act.dma_start(prev[113:128, :, cs], pv[112:127, :, cs]).then_inc(shifted_in[g], 16)
                        act.dma_start(prev[0:1, 1, cs], pv[127:128, 0, cs]).then_inc(shifted_in[g], 16)
                ahead(("lt", l))
                bank = B.wait_filled(act, ("lt", l))
                act.activation(lT[0:64, 0, :], bank[0:64, 0:256], ACT.Tanh)
                act.activation(lT[64:128, 0, :], bank[64:128, 0:256], ACT.Copy)
                B.release(act.activation(lT[:, 1, :], bank[:, 256:512], ACT.Sigmoid), ("lt", l))
                if l:
                    copy(vrT, ("vt", l), lambda b: b[0:VR, 0:256])
                for t in range(TT):
                    ahead(("wup", l, t))
                    B.wait_evacuated(act, ("wup", l, t))
                    act.activation(nb(TMP)[:, t, :], nb(TMP)[:, t, :], ACT.Sigmoid).then_inc(sg_scan, 1)
                    ahead(("aup", l, t))
                    B.wait_evacuated(act, ("aup", l, t))
                    act.activation(nb(A_)[:, t, :], nb(A_)[:, t, :], ACT.Sigmoid).then_inc(rate_done, 1)
                    if l:
                        ahead(("vup", l, t))
                        B.wait_evacuated(act, ("vup", l, t))
                        act.activation(nb(KK)[:, t, :], nb(KK)[:, t, :], ACT.Sigmoid).then_inc(vmix_done, 1)
                    copy(nb(G_)[:, t, :], ("gup", l, t))
                diff_in = [(c, t) for c in range(3) for t in range(TT)]

                def diff_proj(before):
                    while diff_in and B.before[("inb", l, *diff_in[0])] <= B.before[before]:
                        c, t = diff_in.pop(0)
                        copy(dproj[:, t, c * RW:(c + 1) * RW], ("inb", l, c, t))
                for t in range(TT):
                    diff_proj(("cum", l, t))
                    ahead(("cum", l, t))
                    bank = B.wait_filled(act, ("cum", l, t))
                    act.activation(nb(EC)[:, t, :], bank[:, :], ACT.Exp).then_inc(expc, 1)
                    copy(nb(ENC)[:, t, :], ("cum", l, t), scale=-1.0, func=ACT.Exp)
                    copy(nb(ECP)[:, t, :], ("cums", l, t), func=ACT.Exp)
                diff_proj(("wt", l))
                copy(sm[:, 0:16], ("wt", l), lambda b: b[:, 0:16])
                diff_proj(("aT", l, 0))
                for t in range(TT):
                    copy(arT[:, :, 0, :], ("aT", l, t))
                    copy(arT[:, :, 1, :], ("rT", l, t))
                    copy(bT, ("bT", l, t))
                    copy(kT, ("kT", l, t))
                    copy(U_, ("U", l, t), scale=-1.0)
                    for lv in range(5):
                        for g in range(2):
                            copy(Xm[:, 4 * g:4 * g + 4, :], ("X", l, t, lv, g))
                        if t == 0:
                            diff_proj(("ZT", l, t, lv, 0))
                    for par in range(2):
                        r = slice(64 * par, 64 * par + 64)
                        copy(aiT[r, :, :], ("ai", l, t, par), lambda b, r=r: b[r, :])
                    copy(SA0, ("SA0", l, t))
                    for p in range(2):
                        r = slice(64 * p, 64 * p + 64)
                        copy(yraw[r, t, :], ("y1", l, t, p), lambda b, r=r: b[r, :])
                assert not diff_in
                act.wait_ge(lam_in, l + 1)
                act.activation(sm[:, 38:40], sm[:, 36:38], ACT.Exp).then_inc(lam_exp, 1)
                qk = hT[:, :].rearrange("p (w h t) -> p w h t", w=2, h=4)
                for which in range(2):
                    for t in range(TT):
                        copy(qk[:, which, :, t * P:(t + 1) * P], ("qkT", l, which, t))

                def diff_out(h):
                    copy(W1[:, 512 * (h % 2):512 * (h % 2) + 384], ("atT", l, h), lambda b: b[:, 0:384])
                    copy(hNv[:, :, RW + h * DV:RW + (h + 1) * DV], ("pv", l, h), lambda b: b[:, 0:256].rearrange("p (t c) -> p t c", t=TT))
                for h in range(DH):
                    for m in range(2):
                        ahead(("ds", l, h, m))
                        act.wait_ge(smx, 8 * l + 2 * h + m + 1)
                        if h >= 2:
                            act.wait_ge(attn_ready, 4 * l + h - 1)
                        s_, p_ = 384 * m, 768 + 384 * (2 * (h % 2) + m)
                        for q, (a, b) in enumerate(((0, 128), (128, 384))):
                            j = 4 * h + 2 * m + q
                            ins = act.activation(SH[:, p_ + a:p_ + b], SH[:, s_ + a:s_ + b], ACT.Exp, bias=ss[:, j:j + 1],
                                                 scale=DQ ** -0.5, accum_out=ss2[:, j:j + 1])
                        ins.then_inc(pexp, 1)
                    if h:
                        diff_out(h - 1)
                diff_out(DH - 1)
                act.wait_ge(mem_in_s, 16 * (l + 1))
                memn = nbf[:, 4096:6144].rearrange("p (t c) -> p t c", t=TT)
                squares(memn, nbf[:, 6144:8192].rearrange("p (t c) -> p t c", t=TT), sm[:, 34:36], msq_done)

                def x_squares(name):
                    for t in range(TT):
                        for c in range(2):
                            ahead((*name, c, t))
                            B.wait_evacuated(act, (*name, c, t))
                    squares(x, hNv, sm[:, 32:34], sq_done)
                h_parts(("hT", l, 1))
                x_squares(("op", l))
                h_parts(("hT", l, 2))
                qn = proj[:, 0:2048].rearrange("p (t c) -> p t c", t=TT)
                kn = dproj[:, :, :].rearrange("p t c -> p (t c)")[:, 0:2048].rearrange("p (t c) -> p t c", t=TT)
                vx = SH[:, 0:2048].rearrange("p (t c) -> p t c", t=TT)
                for c in range(2):
                    for t in range(TT):
                        copy(qn[:, t, c * 512:(c + 1) * 512], ("xq", l, c, t))
                h_parts(("mT", l))
                for c in range(4):
                    for t in range(TT):
                        copy((kn if c < 2 else vx)[:, t, (c % 2) * 512:(c % 2 + 1) * 512], ("kv", l, c, t))
                px = SH[:, 2048:3072].rearrange("p (s q k) -> p s q k", s=2, q=2)
                for h in range(XH):
                    ahead(("xs", l, h))
                    bank = B.wait_filled(act, ("xs", l, h))
                    act.wait_ge(xs_mx, XH * l + h + 1)
                    if h >= 2:
                        B.wait_filled(act, ("xpT", l, h - 2))
                    for q in range(TT):
                        ins = act.activation(px[:, h % 2, q, :], bank[:, q * 256:(q + 1) * 256], ACT.Exp, bias=ss[:, 16 + 2 * h + q:17 + 2 * h + q],
                                             scale=XD ** -0.5, accum_out=ss2[:, 16 + 2 * h + q:17 + 2 * h + q])
                    B.release(ins, ("xs", l, h))
                h_parts(("oT", l))
                x_squares(("wo", l))
                h_parts(("hT", l, 3))
                if l == 0:
                    sil = nbf[:, 1536:2048].rearrange("p (t n) -> p t n", t=TT)
                    for c in range(FD // FC):
                        for t in range(TT):
                            ahead(("gu", c, t))
                            bank = B.wait_filled(act, ("gu", c, t))
                            act.activation(sil[:, t, :], bank[:, 0:FC], ACT.Silu).then_inc(silu_done, 1)
                        ahead(("fT", c))
                        bank = B.wait_filled(act, ("fT", c))
                        act.activation(h_hi[:, 2048:2560], bank[:, :], ACT.Copy).then_inc(act_hi, 1)
                    for t in range(TT):
                        for n in range(2):
                            ahead(("fy", 2 * t + n))
                            B.wait_evacuated(act, ("fy", 2 * t + n))
                    squares(x, hNv, sm[:, 32:34], sq_done)
            wt = nbf[:, 8256:8260]
            act.wait_ge(w_in, 1)
            act.activation(wt, wt, ACT.Sigmoid).then_inc(w_sig, 1)

            def expert(i):
                done = [0]

                def split_to(m):
                    while done[0] < min(m, PER):
                        hi_of(act, NPRE + done[0], done[0], i)
                        done[0] += 1

                def copy_e(dst, name, bank_no, src):
                    bank = B.wait_filled(act, name, i * MOE_PER[bank_no])
                    B.release(act.activation(dst, src(bank), ACT.Copy), name)
                split_to(NS)
                copy_e(nbf[:, 2560:2816], ("pgT",), 3, lambda b: b[:, 0:256])
                heT = hT[:, 0:1024]
                for g in range(2):
                    B.wait_evacuated(act, ("he", g), i * MOE_PER[6 + g])
                act.activation(h_hi[:, 0:1024], heT, ACT.Copy).then_inc(h_hi_done, 1)
                sil = nbf[:, 1536:2048].rearrange("p (s n) -> p s n", s=2)
                for c in range(STEPS):
                    g_last = 6 * c + 1 if c else 3
                    split_to(g_last + 1 + NS)
                    bank = B.wait_filled(act, ("egu", c), i * MOE_PER[c % 2])
                    act.activation(sil[:, c % 2, :], bank[:, 0:FC], ACT.Silu).then_inc(silu_done, 1)
                    split_to((6 * c + 6 if c < STEPS - 1 else PER) + NS)
                    bank = B.wait_filled(act, ("eT", c), i * MOE_PER[2])
                    act.activation(h_hi[:, 2048:2304], bank[:, 0:256], ACT.Copy).then_inc(act_hi, 1)
                copy_e(nbf[:, 4096:4608], ("ey", 0), 4, lambda b: b[:, :])
            B.wait_filled(act, ("logit",))
            with act.Fori(0, NE) as i:
                expert(i)
            act.wait_ge(items_in, 1)
            n_over = act.value_load(sb_items[0:1, 0:1], min_val=0, max_val=NOVER)
            with act.If(n_over > 0):
                with act.Fori(NE, n_over + NE) as i:
                    expert(i)

        @block.vector
        def _(dve):
            n = [0]

            def step(ins, more=0):
                n[0] += 1
                ins.then_inc(dve_step, 1)
                dve.wait_ge(dve_step, n[0] + more)

            def tt(o, a, b, op, more=0):
                step(dve.tensor_tensor(o, a, b, op), more)

            def ts(o, a, s1, s2, op0, op1=None, more=0):
                step(dve.tensor_scalar(o, a, s1, s2, op0, op1) if op1 is not None else dve.tensor_scalar(o, a, s1, None, op0), more)

            def stt(o, a, s, b, op0, op1):
                step(dve.scalar_tensor_tensor(o, a, s, b, op0, op1))

            def total(o, a):
                step(dve.tensor_reduce(o, a, AX.X, ADD))

            def rsqrt(v, w, scale, eps):
                y, t, z = rst[:, 0:w], rtmp[:, 0:w], v[:, 0:w]
                ts(z, z, scale, eps, MUL, ADD)
                ts(y.bitcast(I32), z.bitcast(I32), 1, None, ALU.logical_shift_right)
                ts(y.bitcast(I32), y.bitcast(I32), -1.0, 1597463007.0, MUL, ADD)
                for _ in range(3):
                    tt(t, y, y, MUL)
                    stt(t, t, -0.5, z, MUL, MUL)
                    stt(y, t, 1.5, y, ADD, MUL)
                return y

            split_to, ahead = splitter(dve, lambda n, m, i: lo_of(dve, n, i))

            def evac(dst, name, src, other, op):
                ahead(name)
                bank = B.wait_filled(dve, name)
                B.release(dve.tensor_tensor(dst, src(bank), other, op), name)
                B.wait_evacuated(dve, name)

            def four(b):
                return b[:, :].rearrange("p (b t) -> p b t", b=4)

            def gain_hT(name, dst, gains):
                for t in range(TT):
                    for g in range(2):
                        evac(dst[:, 4 * g:4 * g + 4, t * P:(t + 1) * P], (*name, t, g), four, bc(gains[:, 4 * g:4 * g + 4].unsqueeze(2), 4, P), MUL)

            n_lo = [0]

            def h_lo_parts(name):
                for t in range(TT):
                    for g in range(2):
                        n_lo[0] += 1
                        dve.wait_ge(h_hi_done, n_lo[0])
                        a = lambda z: z.rearrange("p (k t) -> p k t", k=KD)[:, 4 * g:4 * g + 4, t * P:(t + 1) * P]
                        dve.tensor_tensor(a(h_lo[:, 0:2048]), a(hT[:, :]), a(h_hi[:, 0:2048]).bitcast(F32), SUB).then_inc(h_split, 1)
                assert n_lo[0] == LO_PARTS[name]

            def plain_hT(name):
                for t in range(TT):
                    for g in range(2):
                        ahead((*name, t, g))
                        bank = B.wait_filled(dve, (*name, t, g))
                        B.release(dve.tensor_copy(hTv[:, 4 * g:4 * g + 4, t * P:(t + 1) * P], bank[:, :]), (*name, t, g))
                h_lo_parts(name)

            def gains(l, name, w=8):
                return col[:, l, COL[name]:COL[name] + w]

            def normalize(l, s, gain, name):
                for t in range(TT):
                    dve.wait_ge(sq_done, 2 * (3 * l + s) + t + 1)
                r = rsqrt(sm[:, 32:34], TT, 1.0 / D, EPS)
                for t in range(TT):
                    dve.tensor_scalar(hNv[:, t, :], x[:, t, :], r[:, t:t + 1], None, MUL).then_inc(hn_done, 1)
                gain_hT(name, hTv, gains(l, gain))
                h_lo_parts(name)

            def add_x(name):
                for c in range(2):
                    for t in range(TT):
                        xs = x[:, t, c * 512:(c + 1) * 512]
                        evac(xs, (*name, c, t), lambda b: b[:, :], xs, ADD)

            dve.wait_ge(small_in, 48)
            posf = sm[:, 40:42]
            step(dve.tensor_copy(posf, posi[:, :]))
            ang, k_, r_ = rope[:, 0, :], rope[:, 1, :], rope[:, 2, :]
            tt(ang.rearrange("p (t f) -> p t f", t=TT), bc(posf.unsqueeze(2), TT, 8), bc(C("freq").unsqueeze(1), TT, 8), MUL)
            ts(k_, ang, 1.0 / (2 * math.pi), 12582912.0, MUL, ADD)
            ts(k_, k_, -12582912.0, None, ADD)
            stt(r_, k_, -6.28125, ang, MUL, ADD)
            stt(r_, k_, -(2 * math.pi - 6.28125), r_, MUL, ADD)
            ts(r_, r_, -3.1415925, 3.1415925, ALU.max, ALU.min)
            ts(rope[:, 3, :], r_, 0.5, None, MUL)
            step(dve.tensor_copy(rope[:, 0, :], r_))
            dve.tensor_copy(rope[:, 1, :], r_).then_inc(rope_in, 1)
            dve.wait_ge(rope_sin, 1)
            tt(rope[:, 1, :], rope[:, 1, :], rope[:, 1, :], MUL)
            ts(rope[:, 1, :], rope[:, 1, :], -2.0, 1.0, MUL, ADD)
            sin = rope[:, 0, :].rearrange("p (t f) -> p t f", t=TT)
            cos = rope[:, 1, :].rearrange("p (t f) -> p t f", t=TT)

            for l in range(DEPTH):
                lam_init = 0.8 - 0.6 * math.exp(-0.3 * l)
                normalize(l, 0, "mix", ("hT", l, 0))
                dve.wait_ge(vec_in, 16 * (l + 1))
                dve.wait_ge(mu_in, 16 * (l + 1))
                for g, (c0, cw) in enumerate(chunks_in[0:4] + ([(RC, VR)] if l else [])):
                    ahead(("in", l, g, 1) if g < 4 else ("vr", l, 1))
                    dve.wait_ge(shifted_in[g], 48 * (l + 1) if g < 4 else 48)
                    p_, q_ = pv[:, :, c0:c0 + cw], prev[:, :, c0:c0 + cw]
                    mu_ = mu[:, c0:c0 + cw].unsqueeze(1)
                    tt(q_, q_, p_, SUB)
                    tt(q_, q_, bc(mu_, TT, cw), MUL)
                    if g < 3:
                        tt(p_, p_, q_, ADD)
                    else:
                        dve.tensor_tensor(p_, p_, q_, ADD).then_inc(lora_ready, 1)
                r_, k_, v_ = (pv[:, :, i * RW:(i + 1) * RW] for i in range(3))
                for t in range(TT):
                    evac(nb(TMP)[:, t, :], ("wup", l, t), lambda b: b[:, :], V("decay_b"), ADD)
                    evac(nb(A_)[:, t, :], ("aup", l, t), lambda b: b[:, :], V("iclr_b"), ADD)
                    if l:
                        evac(nb(KK)[:, t, :], ("vup", l, t), lambda b: b[:, :], V("vres_b"), ADD)
                if l:
                    tt(nb(B_), v_first[:, :, :], v_, SUB)
                    dve.wait_ge(vmix_done, TT)
                    tt(nb(B_), nb(B_), nb(KK), MUL)
                    tt(v_, v_, nb(B_), ADD)
                else:
                    step(dve.tensor_copy(v_first[:, :, :], v_))
                heads = lambda a: a.rearrange("p (n c) -> p n c", c=HD)
                kkf, bf = NB[:, KK, :], NB[:, B_, :]
                tt(nb(KK), k_, bc(V("kk_s").unsqueeze(1), TT, RW), MUL)
                tt(bf, kkf, kkf, MUL)
                total(ss[:, 0:16], heads(bf))
                ts(ss[:, 0:16], ss[:, 0:16], 1e-24, None, ALU.max)
                rs = rsqrt(ss, 16, 1.0, 0.0)
                tt(heads(kkf), heads(kkf), bc(rs.unsqueeze(2), 16, HD), MUL)
                dve.wait_ge(rate_done, TT * (l + 1))
                stt(nb(B_), nb(A_), -1.0, bc(V("ka_s").unsqueeze(1), TT, RW), ADD, MUL)
                stt(k_, nb(B_), 1.0, k_, ADD, MUL)
                tt(bf, kkf, NB[:, A_, :], MUL)
                for t in range(TT):
                    ahead(("cums", l, t))
                    B.wait_evacuated(dve, ("cum", l, t))
                    B.wait_evacuated(dve, ("cums", l, t))
                tt(NB[:, ECP, :], kkf, NB[:, ECP, :], MUL)
                tt(bf, bf, NB[:, ENC, :], MUL)
                tt(nb(ENC), k_, nb(ENC), MUL)
                tt(nb(RHO), r_, nb(EC), MUL)
                if l:
                    dve.wait_ge(state_ready, 5 * l)
                dve.memset(state[:, :, :], 0.0).then_inc(state_ready, 1)
                tt(nb(KK), r_, k_, MUL)
                dve.engine_nop().then_inc(elem, 1)
                ahead(("aT", l, 0))
                tt(nb(KK), nb(KK), bc(V("bonus").unsqueeze(1), TT, RW), MUL)
                total(sm[:, 16:32], heads(kkf))
                for t in range(TT):
                    for h in (0, 2, 4, 6, 1, 3, 5, 7):
                        evac(mats[:, h, :, :].rearrange("p (a q) t -> p a (q t)", a=2), ("m12", l, t, h),
                             lambda b: b[:, :].rearrange("p (a q) -> p a q", a=2), bc(C("mask_in").unsqueeze(1), 2, 256), MUL)
                    for par in range(2):
                        tp = Tm.rearrange("p (b q) t -> p b q t", q=2)[:, :, par, :]
                        evac(tp, ("m3", l, t, par), four, bc(C("neg1").unsqueeze(1), 4, P), MUL)
                    tt(Tm, Tm, bc(ident.unsqueeze(1), 8, P), ADD)
                    tt(TTm, mats[:, :, 0, :], bc(C("neg1T").unsqueeze(1), 8, P), MUL)
                    dve.tensor_tensor(TTm, TTm, bc(ident.unsqueeze(1), 8, P), ADD).then_inc(t_ready, 1)
                    dve.wait_ge(t_ready, TT * l + t + 1)
                    for lv in range(5):
                        b2 = 2 << lv

                        def sub(m, name, q):
                            bank = B.wait_filled(dve, name)
                            mc = m.rearrange("p h (n q b) -> p h n q b", q=2, b=b2)[:, :, :, q, :]
                            B.release(dve.tensor_tensor(mc, mc, bank[:, 0:256].rearrange("p (h n b) -> p h n b", h=4, b=b2), SUB), name)
                        ahead(("ZT", l, t, lv, 0))
                        for g in range(2):
                            hs = slice(4 * g, 4 * g + 4)
                            if lv < 4:
                                sub(Tm[:, hs, :], ("Z", l, t, lv, g), 0)
                            sub(TTm[:, hs, :], ("ZT", l, t, lv, g), 1)
                            if lv < 4:
                                B.wait_evacuated(dve, ("Z", l, t, lv, g))
                            B.wait_evacuated(dve, ("ZT", l, t, lv, g))
                    B.wait_evacuated(dve, ("SA0", l, t))
                    for p in range(2):
                        c = 2 * (TT * l + t) + p
                        r = slice(64 * p, 64 * p + 64)
                        bank = B.wait_filled(dve, ("sa", l, t, p))
                        step(dve.tensor_tensor(SA[r, :], SA0[r, :], bank[r, :], SUB))
                        B.release(dve.engine_nop(), ("sa", l, t, p))
                        dve.engine_nop().then_inc(sa_ready, 1)
                        evac(state[:, :, :], ("s", l, t, p), four, state[:, :, :], ADD)
                        dve.wait_ge(keep_ready, c + 1)
                        dve.tensor_tensor(state[:, :, :], state[:, :, :], keep[:, :, :], MUL).then_inc(state_ready, 1)
                        dve.wait_ge(state_ready, c + l + 2)
                    for p in range(2):
                        B.wait_evacuated(dve, ("y1", l, t, p))
                    evac(yraw[:, t, :], ("y2", l, t), lambda b: b[:, :], yraw[:, t, :], ADD)
                y, yf, rho = NB[:, EC, :], heads(NB[:, EC, :]), NB[:, RHO, :]
                total(ss[:, 0:16], yf)
                ts(ss[:, 0:16], ss[:, 0:16], 1.0 / HD, None, MUL)
                tt(yf, yf, bc(ss[:, 0:16].unsqueeze(2), 16, HD), SUB)
                tt(rho, y, y, MUL)
                total(ss[:, 0:16], heads(rho))
                rs = rsqrt(ss, 16, 1.0 / HD, GN_EPS)
                tt(yf, yf, bc(rs.unsqueeze(2), 16, HD), MUL)
                tt(nb(EC), nb(EC), bc(V("gn_w").unsqueeze(1), TT, RW), MUL)
                tt(nb(EC), nb(EC), bc(V("gn_b").unsqueeze(1), TT, RW), ADD)
                vh = v_.rearrange("p t (n c) -> p t n c", c=HD)
                bon = sm[:, 16:32].rearrange("p (t n) -> p t n", t=TT).unsqueeze(3)
                tt(nb(RHO).rearrange("p t (n c) -> p t n c", c=HD), vh, bc(bon, TT, 8, HD), MUL)
                tt(y, y, rho, ADD)
                dve.tensor_tensor(hNv[:, :, 0:RW], nb(EC), nb(G_), MUL).then_inc(ycat, 1)
                dve.wait_ge(ycat, 2 * l + 1)

                lp = SH[:, 3072:3200]
                tt(lp, vec[:, VEC["lq1"][0]:VEC["lq1"][0] + 128], vec[:, VEC["lk1"][0]:VEC["lk1"][0] + 128], MUL)
                step(dve.tensor_reduce(sm[:, 36:38], lp.rearrange("p (a c) -> p a c", a=2), AX.X, ADD))
                dve.engine_nop().then_inc(lam_in, 1)
                qk = dproj[:, :, 0:1024].rearrange("p t (n c) -> p t n c", c=DQ)
                sq = SH[:, 0:2048].rearrange("p (t n c) -> p t n c", t=TT, c=DQ)
                for c in range(3):
                    for t in range(TT):
                        B.wait_evacuated(dve, ("inb", l, c, t))
                tt(sq, qk, qk, MUL)
                total(ss[:, 0:32], SH[:, 0:2048].rearrange("p (n c) -> p n c", c=DQ))
                rs = rsqrt(ss, 32, 1.0 / DQ, EPS).rearrange("p (t n) -> p t n", t=TT).unsqueeze(3)
                tt(qk, qk, bc(rs, TT, 16, DQ), MUL)
                for w, nm in ((0, "q_norm"), (1, "k_norm")):
                    part = qk[:, :, 8 * w:8 * w + 8, :]
                    tt(part, part, bc(V(nm).unsqueeze(1).unsqueeze(1), TT, 8, DQ), MUL)
                x1, x2 = qk[:, :, :, 0:8], qk[:, :, :, 8:16]
                t1 = SH[:, 2048:2304].rearrange("p (t n c) -> p t n c", t=TT, c=8)
                t2 = SH[:, 2304:2560].rearrange("p (t n c) -> p t n c", t=TT, c=8)
                sn, cs = bc(sin.unsqueeze(2), TT, 16, 8), bc(cos.unsqueeze(2), TT, 16, 8)
                tt(t1, x1, sn, MUL)
                tt(t2, x2, sn, MUL)
                tt(x1, x1, cs, MUL)
                tt(x2, x2, cs, MUL)
                tt(x1, x1, t2, SUB)
                dve.tensor_tensor(x2, x2, t1, ADD).then_inc(qs_ready, 1)
                dve.wait_ge(lam_exp, l + 1)
                nlam = sm[:, 42:43]
                tt(nlam, sm[:, 39:40], sm[:, 38:39], SUB)
                ts(nlam, nlam, -lam_init, None, ADD)

                def row_max(h):
                    for m in range(2):
                        S = SH[:, 384 * m:384 * m + 384]
                        if h:
                            dve.wait_ge(pexp, 8 * l + 2 * (h - 1) + m + 1)
                        evac(S, ("ds", l, h, m), lambda b: b[:, 0:384], C("causal"), ADD)
                        j = 4 * h + 2 * m
                        step(dve.tensor_reduce(ss[:, j:j + 1], S[:, 0:128], AX.X, ALU.max))
                        step(dve.tensor_reduce(ss[:, j + 1:j + 2], S[:, 128:384], AX.X, ALU.max))
                        dve.tensor_scalar(ss[:, j:j + 2], ss[:, j:j + 2], -DQ ** -0.5, None, MUL).then_inc(smx, 1)

                def attend(h):
                    dve.wait_ge(pexp, 8 * l + 2 * h + 2)
                    j = 4 * h
                    step(dve.reciprocal(ss2[:, j:j + 4], ss2[:, j:j + 4]))
                    ts(ss2[:, j + 2:j + 4], ss2[:, j + 2:j + 4], nlam, None, MUL)
                    if h >= 2:
                        B.wait_filled(dve, ("atT", l, h - 2))
                    o, p0, p1 = 2304 + 384 * (h % 2), 768 + 768 * (h % 2), 768 + 768 * (h % 2) + 384
                    for q, (a, b) in enumerate(((0, 128), (128, 384))):
                        ts(SH[:, o + a:o + b], SH[:, p0 + a:p0 + b], ss2[:, j + q:j + q + 1], None, MUL)
                        stt(SH[:, o + a:o + b], SH[:, p1 + a:p1 + b], ss2[:, j + 2 + q:j + 3 + q], SH[:, o + a:o + b], MUL, ADD)
                    dve.engine_nop().then_inc(attn_ready, 1)
                for h in range(DH + 1):
                    if h < DH:
                        row_max(h)
                    if h:
                        attend(h - 1)
                for h in range(DH):
                    B.wait_evacuated(dve, ("pv", l, h))
                o4 = hNv[:, :, RW:].rearrange("p t (h c) -> p t h c", h=DH)
                tt(SH[:, 0:1024].rearrange("p (t h c) -> p t h c", t=TT, h=DH), o4, o4, MUL)
                total(ss[:, 0:8], SH[:, 0:1024].rearrange("p (n c) -> p n c", c=DV))
                rs = rsqrt(ss, 8, 1.0 / DV, EPS)
                ts(rs, rs, 1.0 - lam_init, None, MUL)
                tt(o4, o4, bc(rs.rearrange("p (t h) -> p t h", t=TT).unsqueeze(3), TT, DH, DV), MUL)
                dve.tensor_tensor(o4, o4, bc(V("subln").unsqueeze(1).unsqueeze(1), TT, DH, DV), MUL).then_inc(ycat, 1)
                dve.wait_ge(ycat, 2 * l + 2)
                memn = nbf[:, 4096:6144].rearrange("p (t c) -> p t c", t=TT)
                dve.wait_ge(msq_done, 2 * l + 2)
                r = rsqrt(sm[:, 34:36], TT, 1.0 / D, EPS)
                for t in range(TT):
                    dve.tensor_scalar(memn[:, t, :], memn[:, t, :], r[:, t:t + 1], None, MUL).then_inc(mn_done, 1)
                dve.wait_ge(mn_done, 2 * l + 2)
                plain_hT(("hT", l, 1))
                add_x(("op", l))
                normalize(l, 1, "xattn", ("hT", l, 2))

                def head_norm(src, scratch, done):
                    tt(scratch, src, src, MUL)
                    total(ss[:, 0:8], scratch.rearrange("p (n c) -> p n c", c=XD))
                    rs = rsqrt(ss, 8, 1.0 / XD, EPS)
                    s8 = src.rearrange("p (n c) -> p n c", c=XD)
                    dve.tensor_tensor(s8, s8, bc(rs.unsqueeze(2), 8, XD), MUL).then_inc(done, 1)
                    dve.wait_ge(done, l + 1)
                gain_hT(("mT", l), hTv, gains(l, "mem"))
                h_lo_parts(("mT", l))
                for c in range(2):
                    for t in range(TT):
                        B.wait_evacuated(dve, ("xq", l, c, t))
                head_norm(proj[:, 0:2048], nbf[:, 2048:4096], xq_n)
                for c in range(2):
                    for t in range(TT):
                        ahead(("kv", l, c, t))
                        B.wait_evacuated(dve, ("kv", l, c, t))
                head_norm(dproj[:, :, :].rearrange("p t c -> p (t c)")[:, 0:2048], nbf[:, 0:2048], xk_n)
                gain_hT(("xqT", l), nbf[:, 2048:4096].rearrange("p (k t) -> p k t", k=KD), gains(l, "xq"))
                gain_hT(("xkT", l), nbf[:, 0:2048].rearrange("p (k t) -> p k t", k=KD), gains(l, "xk"))
                PT = nbf[:, 8192:9216].rearrange("p (s n) -> p s n", s=2)
                ahead(("kv", l, 3, 1))
                for h in range(XH + 1):
                    if h < XH:
                        ahead(("xs", l, h))
                        bank = B.wait_filled(dve, ("xs", l, h))
                        j = 16 + 2 * h
                        step(dve.tensor_reduce(ss[:, j:j + 2], bank[:, :].rearrange("p (q k) -> p q k", q=2), AX.X, ALU.max))
                        dve.tensor_scalar(ss[:, j:j + 2], ss[:, j:j + 2], -XD ** -0.5, None, MUL).then_inc(xs_mx, 1)
                    if h:
                        bank = B.wait_filled(dve, ("xpT", l, h - 1))
                        B.release(dve.tensor_copy(PT[:, (h - 1) % 2, :], bank[:, :]), ("xpT", l, h - 1))
                        j = 16 + 2 * (h - 1)
                        B.wait_evacuated(dve, ("xs", l, h - 1))
                        step(dve.reciprocal(ss2[:, j:j + 2], ss2[:, j:j + 2]))
                        bank = B.wait_filled(dve, ("xo", l, h - 1))
                        for q in range(TT):
                            ins = dve.tensor_scalar(memn[:, q, (h - 1) * XD:h * XD], bank[:, q * 256:(q + 1) * 256], ss2[:, j + q:j + q + 1], None, MUL)
                        B.release(ins, ("xo", l, h - 1))
                plain_hT(("oT", l))
                add_x(("wo", l))
                normalize(l, 2, "ffn", ("hT", l, 3))
                if l == 0:
                    sil = nbf[:, 1536:2048].rearrange("p (t n) -> p t n", t=TT)
                    actv = nbf[:, 0:1024].rearrange("p (s t n) -> p s t n", s=2, t=2)
                    for c in range(FD // FC):
                        for t in range(TT):
                            ahead(("gu", c, t))
                            bank = B.wait_filled(dve, ("gu", c, t))
                            dve.wait_ge(silu_done, TT * c + t + 1)
                            B.release(dve.tensor_tensor(actv[:, c % 2, t, :], sil[:, t, :], bank[:, FC:2 * FC], MUL), ("gu", c, t))
                        ahead(("fT", c))
                        bank = B.wait_filled(dve, ("fT", c))
                        dve.wait_ge(act_hi, c + 1)
                        B.release(dve.tensor_tensor(h_lo[:, 2048:2560], bank[:, :], h_hi[:, 2048:2560].bitcast(F32), SUB), ("fT", c))
                    for t in range(TT):
                        for nn in range(2):
                            xs = x[:, t, nn * 512:(nn + 1) * 512]
                            evac(xs, ("fy", t * 2 + nn), lambda b: b[:, :], xs, ADD)
            SILU0, HI0 = TT * (FD // FC), FD // FC

            sc = nbf[:, 8192:9216]
            sel, lg = (sc[:, a:a + 16].rearrange("p (t e) -> p t e", t=TT) for a in (0, 16))
            mx8 = sc[:, 32:48].rearrange("p (t e) -> p t e", t=TT)
            w4 = sc[:, 64:68].rearrange("p (t j) -> p t j", t=TT)
            ix = sc[:, 80:96]
            ixf = sc[:, 96:112].rearrange("p (t e) -> p t e", t=TT)
            oh = sc[:, 112:144].rearrange("p (j t e) -> p j t e", j=2, t=TT)
            gate = sc[:, 144:160].rearrange("p (t e) -> p t e", t=TT)
            pos = sc[:, 160:184]
            ov, rank, R, tmp = (sc[:, a:a + 8] for a in (184, 192, 200, 208))
            tmp2 = sc[:, 224:240].rearrange("p (t e) -> p t e", t=TT)
            itf = sc[:, 240:244]
            IT = sc[:, 256:256 + 6 * NITEM].rearrange("p (q t i) -> p q t i", q=3, t=TT)
            iota8 = C("iota")[:, 0:NE]
            bank = B.wait_filled(dve, ("logit",))
            B.release(dve.tensor_copy(sc[:, 16:32], bank[:, 0:16]), ("logit",))
            B.wait_evacuated(dve, ("logit",))
            for t in range(TT):
                step(dve.max(mx8[:, t, :], lg[:, t, :]))
                step(dve.max_index(ix.bitcast(U32)[:, t * 8:(t + 1) * 8], mx8[:, t, :], lg[:, t, :]))
            step(dve.tensor_copy(sc[:, 96:112], ix.bitcast(U32)))
            tt(w4[:, :, 0], mx8[:, :, 0], mx8[:, :, 1], SUB)
            dve.tensor_tensor(w4[:, :, 1], mx8[:, :, 1], mx8[:, :, 0], SUB).then_inc(w_in, 1)
            for j in range(2):
                for t in range(TT):
                    ts(oh[:, j, t, :], iota8, ixf[:, t, j:j + 1], None, ALU.is_equal)
            dve.tensor_tensor(sel, oh[:, 0, :, :], oh[:, 1, :, :], ADD).then_inc(rt_sel, 1)
            dve.wait_ge(rt_sel, 1)
            dve.wait_ge(w_sig, 1)
            for t in range(TT):
                ts(gate[:, t, :], oh[:, 0, t, :], w4[:, t, 0:1], None, MUL)
                stt(gate[:, t, :], oh[:, 1, t, :], w4[:, t, 1:2], gate[:, t, :], MUL, ADD)
            bank = B.wait_filled(dve, ("pos",))
            B.release(dve.tensor_copy(pos, bank[:, 0:24]), ("pos",))
            B.wait_evacuated(dve, ("pos",))
            posv = pos[:, 0:16].rearrange("p (t e) -> p t e", t=TT)
            for q, src in enumerate((posv, sel, gate)):
                step(dve.tensor_copy(IT[:, q, :, 0:NE], src))
            ts(ov, pos[:, 16:24], float(P), None, ALU.is_gt)
            step(dve.tensor_tensor_scan(rank, C("ones")[:, 0:NE], ov, 0.0, MUL, ADD))
            step(dve.tensor_copy(itf[:, 0:1], rank[:, NE - 1:NE]))
            tt(rank, rank, ov, SUB)
            for r in range(NOVER):
                ts(R, rank, float(r), None, ALU.is_equal)
                tt(R, R, ov, MUL)
                for q, src in enumerate((posv, sel, gate)):
                    tt(tmp2, src, bc(R.unsqueeze(1), TT, NE), MUL)
                    step(dve.tensor_reduce(IT[:, q, :, NE + r], tmp2, AX.X, ADD))
                ts(IT[:, 0, :, NE + r], IT[:, 0, :, NE + r], -float(P), None, ADD)
                tt(tmp, R, iota8, MUL)
                step(dve.tensor_reduce(itf[:, r + 1:r + 2], tmp, AX.X, ADD))
            dve.tensor_copy(sb_items[:, :], itf[0:1, :]).then_inc(items_in, 1)

            first_step = n[0]

            def expert(i):
                n[0] = first_step
                more = i * DVE_STEPS

                def evac_e(dst, name, bank_no, src, other, op):
                    bank = B.wait_filled(dve, name, i * MOE_PER[bank_no])
                    B.release(dve.tensor_tensor(dst, src(bank), other, op), name)
                    B.wait_evacuated(dve, name, i * MOE_PER[bank_no])
                cur = sm[:, 44:50]
                step(dve.tensor_copy(cur.rearrange("p (q t) -> p q t", q=3).unsqueeze(3), IT[:, :, :, bass.ds(i, 1)]), more)
                Psel = nbf[:, 2048:2304].rearrange("p (t j) -> p t j", t=TT)
                Pg = nbf[:, 2304:2560].rearrange("p (t j) -> p t j", t=TT)
                for q, dst in ((1, Psel), (2, Pg)):
                    for t in range(TT):
                        ins = dve.tensor_scalar(dst[:, t, :], C("iota"), cur[:, t:t + 1], cur[:, 2 * q + t:2 * q + t + 1], ALU.is_equal, MUL)
                    ins.then_inc(sel_done, 1)
                done = [0]

                def split_to(m):
                    while done[0] < min(m, PER):
                        lo_of(dve, NPRE + done[0], i)
                        done[0] += 1
                heT = hT[:, 0:1024].rearrange("p (k j) -> p k j", k=KD)
                for g in range(2):
                    evac_e(heT[:, 4 * g:4 * g + 4, :], ("he", g), 6 + g, four, bc(gains(1, "ffn")[:, 4 * g:4 * g + 4].unsqueeze(2), 4, P), MUL)
                actv = nbf[:, 0:512].rearrange("p (s n) -> p s n", s=2)
                sil = nbf[:, 1536:2048].rearrange("p (s n) -> p s n", s=2)
                dve.wait_ge(h_hi_done, H_SPLIT0 + 1 + i)
                dve.tensor_tensor(h_lo[:, 0:1024], hT[:, 0:1024], h_hi[:, 0:1024].bitcast(F32), SUB).then_inc(h_split, 1)
                for c in range(STEPS):
                    split_to((6 * c + 1 if c else 3) + 1 + NS)
                    bank = B.wait_filled(dve, ("egu", c), i * MOE_PER[c % 2])
                    dve.wait_ge(silu_done, SILU0 + c + 1 + i * STEPS)
                    B.release(dve.tensor_tensor(actv[:, c % 2, :], sil[:, c % 2, :], bank[:, FC:2 * FC], MUL), ("egu", c))
                    split_to((6 * c + 6 if c < STEPS - 1 else PER) + NS)
                    bank = B.wait_filled(dve, ("eT", c), i * MOE_PER[2])
                    dve.wait_ge(act_hi, HI0 + c + 1 + i * STEPS)
                    B.release(dve.tensor_tensor(h_lo[:, 2048:2304], bank[:, 0:256], h_hi[:, 2048:2304].bitcast(F32), SUB), ("eT", c))
                bank = B.wait_filled(dve, ("ey", 1), i * MOE_PER[5])
                B.release(dve.tensor_copy(nbf[:, 4608:5120], bank[:, :]), ("ey", 1))
                for t in range(TT):
                    for nn in range(2):
                        xs = x[:, t, nn * 512:(nn + 1) * 512]
                        evac_e(xs, ("sc", t, nn), 6 + nn, lambda b: b[:, :], xs, ADD)
                assert n[0] == first_step + DVE_STEPS
            with dve.Fori(0, NE) as i:
                expert(i)
            n_over = dve.value_load(sb_items[0:1, 0:1], min_val=0, max_val=NOVER)
            with dve.If(n_over > 0):
                with dve.Fori(NE, n_over + NE) as i:
                    expert(i)
            dve.engine_nop().then_inc(final, 1)


def constants():
    import numpy as np
    f = np.float32
    i = np.arange(P)
    row, c = i[:, None], i[None, :]
    same = (row // CH) == (c // CH)
    part = {
        "ident": (row == c), "bd": same, "ones": np.ones((P, P)), "utri": row < c, "iota": np.broadcast_to(c, (P, P)),
        "mask_in": np.concatenate([same & (row < c), same & (row <= c)], 1),
        "tri": DEC * (same & (row <= c)), "tri_s": DEC * (same & (row < c)),
        "neg1": -1.0 * ((row == c + 1) & (row % 2 == 1)), "neg1T": -1.0 * ((c == row + 1) & (c % 2 == 1)),
        "lvl": np.concatenate([(row // (2 * b) == c // (2 * b)) & (row % (2 * b) < b) & (c % (2 * b) >= b) for b in (2, 4, 8, 16, 32)], 1),
        "causal": np.concatenate([-1e30 * (c > row), np.zeros((P, P)), -1e30 * (c > row)], 1),
        "last": np.stack([i == CH - 1, i == 2 * CH - 1], 1),
        "freq": np.broadcast_to(f(500000.0) ** (-np.arange(0, ROPE, 2, dtype=f) / f(ROPE)), (P, 8)),
    }
    return np.ascontiguousarray(np.concatenate([np.asarray(part[n], f).reshape(P, w) for n, (_, w) in CST.items()], 1))


def kernel(**inputs):
    import numpy as np
    import concourse.bacc as bacc
    from concourse import mybir as mb
    from concourse.bass_utils import run_bass_kernel_spmd

    a = {k: np.ascontiguousarray(v) for k, v in inputs.items()}
    L = DEPTH
    last = lambda n: np.broadcast_to(a[n][-1], (L, *a[n].shape[1:]))
    mus = np.ascontiguousarray(np.concatenate([a["shift_mu"], last("vres_shift_mu")], 1))
    src = {"decay_b": a["decay_bias"], "iclr_b": a["iclr_bias"],
           "kk_s": a["key_kk_scale"], "ka_s": a["key_iclr_scale"], "bonus": a["bonus_rk"].reshape(L, -1), "gn_w": a["rwkv_gn_w"],
           "gn_b": a["rwkv_gn_b"], "vres_b": last("vres_bias"), "q_norm": a["q_norm"], "k_norm": a["k_norm"],
           "lq1": a["lambda_q1"], "lq2": a["lambda_q2"], "lk1": a["lambda_k1"], "lk2": a["lambda_k2"], "subln": a["diff_subln"]}
    vecs = np.ascontiguousarray(np.concatenate([src[n] for n in VEC], 1))
    fold = lambda v: v.reshape(L, -1, P).transpose(0, 2, 1)
    cols = np.ascontiguousarray(np.concatenate(
        [fold(a[n]) for n in ("mix_norm", "xattn_norm", "mem_norm", "ffn_norm")]
        + [np.tile(fold(a[n]), (1, 1, XH)) for n in ("xattn_q_norm", "xattn_k_norm")], 2))
    feeds = {"x": a["x"], "mem": a["mem"], "positions": np.ascontiguousarray(a["positions"].reshape(TT, P).T), "mus": mus, "vecs": vecs, "cols": cols, "consts": constants()}
    for n in ("in_proj", "decay_up", "iclr_up", "gate_up", "vres_down", "vres_up", "out_proj", "xattn_wq", "xattn_wkv", "xattn_wo",
              "dense_w_gu", "dense_w_down", "router", "expert_w_gu", "expert_w_down"):
        feeds[n] = a[n]
    nc = bacc.Bacc("TRN2", target_bir_lowering=False, num_devices=1)
    args = [nc.dram_tensor(f"in_{n}", v.shape, mb.dt.from_np(v.dtype), kind="ExternalInput").ap() for n, v in feeds.items()]
    args.append(nc.dram_tensor("out_0", (1, SEQ, D), mb.dt.float32, kind="ExternalOutput").ap())
    decoder_trunk(nc, *args)
    r = run_bass_kernel_spmd(nc, [{f"in_{n}": v for n, v in feeds.items()}], core_ids=[0])
    return r.results[0]["out_0"]
```

```python
import concourse.bass as bass
from concourse import mybir
from contextlib import ExitStack
import math

P = 128
D = 1024
SEQ = 256
TT = SEQ // P
KD = D // P
DEPTH = 2
EPS = 1e-6
RW, RH, HD = 512, 8, 64
GN_EPS = 64e-5
LORA = 256
RC = 3 * RW + LORA
VR = 32
DH, DV, DQ = 4, 128, 64
ROPE = 16
XH, XD = 4, 256
FD, FE, NE = 2816, 3584, 8
CH = 64
NOVER = 3
NITEM = NE + NOVER
RING, BLK = 4, 1024
NS = 3
RING_E, NS_E = 14, 4
LOOK = NS_E - 1
DVE_STEPS = 2
GATE_STEP, NEXT_STEP = 3, 8
FC = 256
DEC = -math.exp(-0.5)

VEC = {}
_at = 0
for _n, _w in (("decay_b", RW), ("iclr_b", RW), ("kk_s", RW), ("ka_s", RW), ("bonus", RW),
               ("gn_w", RW), ("gn_b", RW), ("vres_b", RW), ("q_norm", DQ), ("k_norm", DQ), ("lq1", DQ), ("lq2", DQ),
               ("lk1", DQ), ("lk2", DQ), ("subln", DV)):
    VEC[_n] = (_at, _w)
    _at += _w
NV = _at
NMU = RC + VR
COL = {"mix": 0, "xattn": 8, "mem": 16, "ffn": 24, "xq": 32, "xk": 40}
NCOL = 48
CST = {}
_at = 0
for _n, _w in (("ident", P), ("mask_in", 256), ("lvl", 5 * P), ("neg1", P), ("neg1T", P), ("tri", P), ("tri_s", P),
               ("causal", 384), ("bd", P), ("last", 2), ("ones", P), ("utri", P), ("iota", P), ("freq", 8)):
    CST[_n] = (_at, _w)
    _at += _w
NCST = _at


class Banks:

    def __init__(self, psum, ready, evacuated):
        self.psum, self.ready, self.evacuated = psum, ready, evacuated
        self.n, self.use = [0] * 8, {}
        self.taken = [0]
        self.before = {}

    def open(self, pe, name, bank, more=0):
        self.use[name] = (bank, self.n[bank])
        if self.n[bank]:
            pe.wait_ge(self.evacuated[bank], self.n[bank] + more)
        self.n[bank] += 1
        return self.psum[bank]

    def filled(self, last, name):
        last.then_inc(self.ready[self.use[name][0]], 1)
        self.before[name] = self.taken[0]

    def wait_filled(self, eng, name, more=0):
        bank, nth = self.use[name]
        eng.wait_ge(self.ready[bank], nth + 1 + more)
        return self.psum[bank]

    def wait_evacuated(self, eng, name, more=0):
        bank, nth = self.use[name]
        eng.wait_ge(self.evacuated[bank], nth + 1 + more)

    def release(self, ins, name):
        ins.then_inc(self.evacuated[self.use[name][0]], 1)


def decoder_trunk(nc, x_in, mem_in, pos_in, mus, vecs, cols, consts, in_proj, decay_up, iclr_up, gate_up, vres_down, vres_up,
                  out_proj, wq, wkv, wo, dense_gu, dense_down, router, expert_gu, expert_down, out):
    F32, I32, U32 = mybir.dt.float32, mybir.dt.int32, mybir.dt.uint32
    ACT, ALU, AX = mybir.ActivationFunctionType, mybir.AluOpType, mybir.AxisListType
    MUL, ADD, SUB = ALU.mult, ALU.add, ALU.subtract

    ctx = ExitStack()
    with ctx:
        def sb(name, shape, dt=F32):
            return ctx.enter_context(nc.sbuf_tensor(name, shape, dt))

        def sem(name):
            return ctx.enter_context(nc.semaphore(name))

        F32R = mybir.dt.float32r
        ring = sb("ring", [P, RING, BLK])
        w_hi = sb("w_hi", [P, NS, BLK], F32R)
        w_lo = sb("w_lo", [P, NS, BLK], F32R)
        h_hi = sb("h_hi", [P, 2560], F32R)
        h_lo = sb("h_lo", [P, 2560], F32R)
        x = sb("x", [P, TT, D])
        v_first = sb("v_first", [P, TT, RW])
        vec = sb("vec", [P, NV])
        col = sb("col", [P, DEPTH, NCOL])
        vresd_w = sb("vresd_w", [P, KD, VR])
        router_w = sb("router_w", [P, KD, NE])
        cst = sb("cst", [P, NCST])
        proj = sb("proj", [P, TT * (RC + VR)])
        dproj = sb("dproj", [P, TT, 3 * RW])
        NB = sb("NB", [P, 9, 1024])
        SH = sb("SH", [P, 4096])
        hN = sb("hN", [P, 2048])
        hT = sb("hT", [P, 2048])
        W1 = sb("W1", [P, 1024])
        state = sb("state", [P, 4, P])
        keep = sb("keep", [P, 4, P])
        rope = sb("rope", [P, 4, TT * 8])
        posi = sb("posi", [P, TT], I32)
        st = sb("st", [P, 192])
        psum = [ctx.enter_context(nc.psum_tensor(f"psum{b}", [P, 512], F32)) for b in range(8)]

        def C(name):
            a, w = CST[name]
            return cst[:, a:a + w]

        def V(name):
            a, w = VEC[name]
            return vec[:, a:a + w]

        def bc(ap, *shape):
            return ap.to_broadcast([P, *shape])

        def half_cols(m, b, q):
            return m.rearrange("p (n q b) -> p n q b", q=2, b=b)[:, :, q, :]

        def halves(m, b):
            return m.rearrange("p (n b) -> p n b", b=b)

        ident = C("ident")
        pv = proj[:, :].rearrange("p (t c) -> p t c", t=TT)
        prev = SH[:, 0:TT * (RC + VR)].rearrange("p (t c) -> p t c", t=TT)
        nbf = NB[:, :, :].rearrange("p a b -> p (a b)")

        mu = nbf[:, 0:NMU]
        lora_w = NB[:, 6, 0:RW]
        gate_w = NB[:, 7, 0:RW]
        vres_w = NB[0:VR, 7, RW:2 * RW]

        def nb(i):
            return NB[:, i, :].rearrange("p (t c) -> p t c", t=TT)
        A_, G_, EC, ENC, ECP, KK, B_, RHO, TMP = range(9)
        hNv = hN[:, :].rearrange("p (t c) -> p t c", t=TT)
        hTv = hT[:, :].rearrange("p (k t) -> p k t", k=KD)
        arT = hN[:, 0:1024].rearrange("p (b q t) -> p b q t", b=4, q=2)
        bT = hN[:, 1024:1536].rearrange("p (b t) -> p b t", b=4)
        kT = hN[:, 1536:2048].rearrange("p (b t) -> p b t", b=4)
        mats = SH[:, :].rearrange("p (h q t) -> p h q t", h=8, q=4)
        Tm = hT[:, 0:1024].rearrange("p (h t) -> p h t", h=8)
        TTm = hT[:, 1024:2048].rearrange("p (h t) -> p h t", h=8)
        Xm = NB[:, KK, :].rearrange("p (h t) -> p h t", h=8)
        Cm = NB[:, A_, :].rearrange("p (h t) -> p h t", h=8)
        aiT = W1[:, 0:512].rearrange("p (b t) -> p b t", b=4)
        U_ = W1[:, 512:1024]
        SA0 = NB[:, TMP, 0:512]
        SA = NB[:, TMP, 512:1024]
        yraw = nb(EC)
        lT = W1[:, 0:512].rearrange("p (b t) -> p b t", b=2)
        vrT = U_[0:VR, 0:256]
        sb_items = sb("items", [1, 4], I32)
        ss, ss2, rst, rtmp = st[:, 0:32], st[:, 32:64], st[:, 64:96], st[:, 96:128]
        sm = st[:, 128:192]

        ready = [sem(f"psum_ready{b}") for b in range(8)]
        evacuated = [sem(f"psum_evacuated{b}") for b in range(8)]
        B = Banks(psum, ready, evacuated)
        block_in = [sem(f"block_in{s}") for s in range(RING)]
        expert_block_in = [sem(f"expert_block_in{s}") for s in range(RING_E)]
        block_used, hi_done, lo_done = sem("block_used"), sem("weights_hi"), sem("weights_lo")
        h_hi_done, h_split = sem("h_hi_done"), sem("h_lo_done")
        mu_in = sem("mu_in")
        x_in_s, small_in, vec_in, mem_in_s, out_s = sem("x_in"), sem("small_in"), sem("vec_in"), sem("mem_in"), sem("out_s")
        lw_in = sem("layer_weights_in")
        dve_step, act_step, pool_step = sem("dve_step"), sem("act_step"), sem("pool_step")
        sq_done, hn_done = sem("squares_done"), sem("normed")
        msq_done, mn_done = sem("mem_squares_done"), sem("mem_normed")
        shifted_in = [sem(f"shifted_in{g}") for g in range(5)]
        row0_ready, lora_ready, sg_scan, rate_done, vmix_done = (sem("row0_cleared"), sem("lora_shifted"), sem("decay_sigmoid"),
                                                                 sem("rate_sigmoid"), sem("value_mix_sigmoid"))
        v_final, expc, elem, qs_ready = sem("v_final"), sem("exp_cum_done"), sem("recurrence_inputs"), sem("qk_roped")
        c_ready, t_ready, state_ready, sa_ready = sem("C_masked"), sem("T_started"), sem("state_ready"), sem("SA_ready")
        keep_ready, ycat, smx, pexp, attn_ready = sem("keep_ready"), sem("y_cat"), sem("row_max"), sem("p_exp"), sem("attn_ready")
        lam_in, lam_exp, rope_in, rope_sin = sem("lambda_in"), sem("lambda_exp"), sem("rope_in"), sem("rope_sin")
        xq_n, xk_n, xs_mx = sem("xq_normed"), sem("xk_normed"), sem("x_row_max")
        silu_done, w_in, w_sig, rt_sel, items_in = sem("silu_done"), sem("gate_in"), sem("gate_sigmoid"), sem("selected"), sem("items_ready")
        gn_ready = sem("group_normed")
        sel_done, final = sem("selection_done"), sem("final")
        act_hi = sem("hidden_hi_done")

        def rows(w, k0, c0, cw):
            return w[k0 * P:(k0 + 2) * P, c0:c0 + cw].rearrange("(k p) n -> p k n", p=P)
        chunks_in = [(0, 512), (512, 512), (1024, 512), (1536, 256), (1792, 512), (2304, 512), (2816, 512)]

        def square_blocks(w, cs):
            return [("w", rows(w, k0, c0, cw), cw) for c0, cw in cs for k0 in range(0, KD, 2)]

        def half_chunks(n):
            return [(c * 512, 512) for c in range(n)]

        GU = [(0, 0), (0, 1), (1, 0), (1, 1)]

        def gu_block(w, c, g, half):
            c0 = g * (w.shape[-1] // 2) + c * FC
            return w[half * 512:(half + 1) * 512, c0:c0 + FC].rearrange("(k p) f -> p k f", p=P)

        def down_block(w, c, k):
            return w[c * FC + k * P:c * FC + (k + 1) * P, :]

        blocks = []
        for l in range(DEPTH):
            blocks += square_blocks(in_proj[l], chunks_in)
            blocks += square_blocks(out_proj[l], half_chunks(2))
            blocks += square_blocks(wkv[l], half_chunks(4))
            blocks += square_blocks(wq[l], half_chunks(2))
            blocks += square_blocks(wo[l], half_chunks(2))
            if l == 0:
                for c in range(FD // FC + 1):
                    if c < FD // FC:
                        blocks += [("gu", gu_block(dense_gu[0], c, *g), 0) for g in GU]
                    if c:
                        blocks += [("down", down_block(dense_down[0], c - 1, k), 0) for k in range(2)]
        NPRE = len(blocks)
        STEPS = FE // FC
        PER = 6 * STEPS
        assert PER % RING_E == 0 and PER % NS_E == 0
        dpf = dproj[:, :, :].rearrange("p t c -> p (t c)")
        spare = [SH[:, 0:3 * BLK], proj[:, 0:3 * BLK], dpf, W1[:, :]]
        ring_e = [m[:, a:a + BLK] for m in [ring[:, :, :].rearrange("p s n -> p (s n)")] + spare for a in range(0, m.shape[1], BLK)]
        assert len(ring_e) == RING_E
        hi_e, lo_e = ([w[:, s, :] for s in range(NS)] + [h[:, BLK:2 * BLK]] for w, h in ((w_hi, h_hi), (w_lo, h_lo)))

        def shaped(w, kind, cw):
            if kind == "down":
                return w
            k, cw = (4, FC) if kind == "gu" else (2, cw)
            return w[:, 0:k * cw].rearrange("p (k f) -> p k f", k=k)

        MOE_PER = [STEPS // 2, STEPS // 2, STEPS, 1, 1, 1, 3, 3]
        MOE_USED = 5 * STEPS - 1
        freed = []

        def splitter(eng, one):
            n = [0]

            def to(m):
                while n[0] < min(m, NPRE):
                    one(n[0])
                    n[0] += 1

            def ahead(name, more=0):
                to(B.before[name] + NS + more)
            return to, ahead

        def hi_of(act, n):
            act.wait_ge(block_in[n % RING], 16 * (n // RING + 1))
            if n >= NS:
                act.wait_ge(*freed[n - NS][0:2])
            act.activation(w_hi[:, n % NS, :], ring[:, n % RING, :], ACT.Copy).then_inc(hi_done, 1)

        def lo_of(dve, n):
            dve.wait_ge(hi_done, n + 1)
            dve.tensor_tensor(w_lo[:, n % NS, :], ring[:, n % RING, :], w_hi[:, n % NS, :].bitcast(F32), SUB).then_inc(lo_done, 1)

        def expert_hi_of(act, j, i):
            act.wait_ge(expert_block_in[j % RING_E], 16 * (j // RING_E + 1) + i * (16 * PER // RING_E))
            if j < NS_E:
                s_, v_, per = freed[NPRE + PER + j - NS_E]
                act.wait_ge(s_, v_ - per + i * per)
            else:
                s_, v_, per = freed[NPRE + j - NS_E]
                act.wait_ge(s_, v_ + i * per)
            act.activation(hi_e[j % NS_E], ring_e[j % RING_E], ACT.Copy).then_inc(hi_done, 1)

        def expert_lo_of(dve, j, i):
            dve.wait_ge(hi_done, NPRE + j + 1 + i * PER)
            dve.tensor_tensor(lo_e[j % NS_E], ring_e[j % RING_E], hi_e[j % NS_E].bitcast(F32), SUB).then_inc(lo_done, 1)

        LO_PARTS = {}
        for l in range(DEPTH):
            for name in (("hT", l, 0), ("hT", l, 1), ("mT", l), ("hT", l, 2), ("oT", l), ("hT", l, 3)):
                LO_PARTS[name] = 4 * (len(LO_PARTS) + 1)

        H_SPLIT0 = 4 * len(LO_PARTS)

        block = ctx.enter_context(nc.Block())

        @block.tensor
        def _(pe):
            at = B.taken
            n_used = [0]
            work = [0]

            def take(kind, cw=512):
                n = at[0]
                at[0] += 1
                pe.wait_ge(lo_done, n + 1)
                return shaped(w_hi[:, n % NS, :], kind, cw), shaped(w_lo[:, n % NS, :], kind, cw)

            def product(o, h, w, start, stop):
                pe.matmul(o, h[0], w[0], start=start, stop=False, skip_group_check=True)
                pe.matmul(o, h[0], w[1], start=False, stop=False, skip_group_check=True)
                return pe.matmul(o, h[1], w[0], start=False, stop=stop, skip_group_check=True)

            def used(last):
                last.then_inc(block_used, 1)
                n_used[0] += 1
                freed.append((block_used, n_used[0], MOE_USED))

            def used_with(name):
                bank, nth = B.use[name]
                freed.append((ready[bank], nth + 1, MOE_PER[bank]))

            def open_work(name):
                work[0] += 1
                return B.open(pe, name, 4 + (work[0] - 1) % 4)
            nproj = [0]

            def transposes(name, srcs, opener=None):
                bank = (opener or open_work)(name)
                for i, s in enumerate(srcs):
                    n = s.shape[0]
                    m = s.shape[1]
                    last = pe.transpose(bank[0:m, i * P:i * P + n], s, ident[0:n, 0:n])
                B.filled(last, name)

            def to_hT(name, src, wait):
                for t in range(TT):
                    wait(t)
                for g in range(2):
                    for t in range(TT):
                        transposes((*name, t, g), [src[:, t, (4 * g + i) * P:(4 * g + i + 1) * P] for i in range(4)])

            def project_steps(name, n_cols, src_ready):
                for c, (c0, cw) in enumerate(n_cols):
                    banks = []
                    for t in range(TT):
                        banks.append(B.open(pe, (*name, c, t), nproj[0] % 4))
                        nproj[0] += 1
                    for kb in range(0, KD, 2):
                        if c == 0 and kb % 4 == 0:
                            src_ready(kb // 4)
                        wh, wl = take("w", cw)
                        for t in range(TT):
                            for k in range(2):
                                last = product(banks[t][:, 0:cw], lhs_h(kb + k, t), (wh[:, k, :], wl[:, k, :]), kb + k == 0, kb + k == 7)
                            if kb == KD - 2:
                                B.filled(last, (*name, c, t))
                        if kb == KD - 2:
                            used_with((*name, c, TT - 1))
                        else:
                            used(last)
                        yield

            def project(name, n_cols, src_ready):
                for _ in project_steps(name, n_cols, src_ready):
                    pass

            pe.wait_ge(small_in, 48)

            def lhs_h(kk, t):
                a = kk * SEQ + t * P
                return h_hi[:, a:a + P], h_lo[:, a:a + P]

            def h_ready(name):
                def wait(g=1):
                    for t in range(TT):
                        B.wait_evacuated(pe, (*name, t, g))
                    pe.wait_ge(h_split, LO_PARTS[name] - (TT if g == 0 else 0))
                return wait

            for l in range(DEPTH):
                to_hT(("hT", l, 0), hNv, lambda t: pe.wait_ge(hn_done, 2 * 3 * l + t + 1))
                project(("in", l), chunks_in[0:4], h_ready(("hT", l, 0)))
                if l:
                    pe.wait_ge(lw_in, 80)
                    for t in range(TT):
                        bank = B.open(pe, ("vr", l, t), nproj[0] % 4)
                        nproj[0] += 1
                        for k in range(KD):
                            last = pe.matmul(bank[:, 0:VR], hTv[:, k, t * P:(t + 1) * P], vresd_w[:, k, :], start=(k == 0), stop=(k == 7))
                        B.filled(last, ("vr", l, t))
                rest = project_steps(("inb", l), chunks_in[4:], lambda g: None)

                def fill(n):
                    for _ in range(n):
                        next(rest, None)
                fill(2)
                pe.wait_ge(lora_ready, l + 1)
                transposes(("lt", l), [pv[:, t, 1536 + b * P:1536 + (b + 1) * P] for b in range(2) for t in range(TT)])
                if l:
                    pe.wait_ge(lora_ready, l + 2)
                    transposes(("vt", l), [pv[:, t, RC:RC + VR] for t in range(TT)])
                fill(1)
                pe.wait_ge(lw_in, 80 + 64 * l)
                B.wait_evacuated(pe, ("lt", l))
                for t in range(TT):
                    ts = slice(t * P, (t + 1) * P)
                    for name, lhs, rhs in (("wup", lT[0:64, 0, ts], lora_w[0:64, :]), ("aup", lT[64:128, 0, ts], lora_w[64:128, :]),
                                           ("gup", lT[:, 1, ts], gate_w[:, :])):
                        bank = open_work((name, l, t))
                        B.filled(pe.matmul(bank[:, :], lhs, rhs, start=True, stop=True), (name, l, t))
                    if l:
                        if t == 0:
                            B.wait_evacuated(pe, ("vt", l))
                        bank = open_work(("vup", l, t))
                        B.filled(pe.matmul(bank[:, :], vrT[:, ts], vres_w[:, :], start=True, stop=True), ("vup", l, t))
                for t in range(TT):
                    if t == 0:
                        fill(1)
                    pe.wait_ge(sg_scan, TT * l + t + 1)
                    for name, m in (("cum", C("tri")), ("cums", C("tri_s"))):
                        bank = open_work((name, l, t))
                        B.filled(pe.matmul(bank[:, :], m, nb(TMP)[:, t, :], start=True, stop=True), (name, l, t))
                fill(1)
                pe.wait_ge(expc, 2 * l + 2)
                bank = open_work(("wt", l))
                for t in range(TT):
                    for b in range(4):
                        last = pe.matmul(bank[:, (t * 4 + b) * 2:(t * 4 + b) * 2 + 2], nb(EC)[:, t, b * P:(b + 1) * P], C("last"),
                                         start=True, stop=True)
                B.filled(last, ("wt", l))

                fill(5)
                for t in range(TT):
                    pe.wait_ge(elem, l + 1)
                    for name, q in (("aT", ECP), ("rT", RHO), ("bT", B_), ("kT", ENC)):
                        transposes((name, l, t), [nb(q)[:, t, b * P:(b + 1) * P] for b in range(4)])
                    for name in ("aT", "rT", "bT", "kT"):
                        B.wait_evacuated(pe, (name, l, t))
                    for h in (0, 2, 4, 6, 1, 3, 5, 7):
                        b, r = h // 2, slice(64 * (h % 2), 64 * (h % 2) + 64)
                        bank = open_work(("m12", l, t, h))
                        pe.matmul(bank[:, 0:256], bT[r, b, :], arT[r, b, :, :].rearrange("p q t -> p (q t)"), start=True, stop=True)
                        B.filled(pe.matmul(bank[:, 256:512], kT[r, b, :], arT[r, b, :, :].rearrange("p q t -> p (q t)"),
                                           start=True, stop=True), ("m12", l, t, h))
                    for par in range(2):
                        r = slice(64 * par, 64 * par + 64)
                        bank = open_work(("m3", l, t, par))
                        for b in range(4):
                            last = pe.matmul(bank[:, b * P:(b + 1) * P], arT[r, b, 0, :], bT[r, b, :], start=True, stop=True)
                        B.filled(last, ("m3", l, t, par))
                    for par in range(2):
                        for h in range(par, 8, 2):
                            B.wait_evacuated(pe, ("m12", l, t, h))
                    bank = open_work(("U", l, t))
                    for h in range(8):
                        last = pe.matmul(bank[:, h * HD:(h + 1) * HD], mats[:, h, 2, :], pv[:, t, 2 * RW + h * HD:2 * RW + (h + 1) * HD],
                                         start=True, stop=True)
                    B.filled(last, ("U", l, t))
                    for lv in range(5):
                        for g in range(2):
                            pe.wait_ge(c_ready, 10 * (TT * l + t) + lv * 2 + g + 1)
                            if lv == 0:
                                pe.wait_ge(t_ready, TT * l + t + 1)
                            else:
                                B.wait_evacuated(pe, ("Z", l, t, lv - 1, g))
                                B.wait_evacuated(pe, ("ZT", l, t, lv - 1, g))
                            bank = open_work(("X", l, t, lv, g))
                            for h in range(4 * g, 4 * g + 4):
                                last = pe.matmul(bank[:, (h % 4) * P:(h % 4 + 1) * P], Cm[:, h, :], Tm[:, h, :], start=True, stop=True)
                            B.filled(last, ("X", l, t, lv, g))
                        fill(t == 0 and lv % 2 == 0)
                        b2 = 2 << lv
                        for g in range(2):
                            B.wait_evacuated(pe, ("X", l, t, lv, g))
                            if lv < 4:
                                bank = open_work(("Z", l, t, lv, g))
                                for h in range(4 * g, 4 * g + 4):
                                    last = pe.matmul(halves(bank[:, (h % 4) * 64:(h % 4 + 1) * 64], b2), TTm[:, h, :], half_cols(Xm[:, h, :], b2, 0),
                                                     start=True, stop=True)
                                B.filled(last, ("Z", l, t, lv, g))
                            bank = open_work(("ZT", l, t, lv, g))
                            for h in range(4 * g, 4 * g + 4):
                                last = pe.matmul(halves(bank[:, (h % 4) * 64:(h % 4 + 1) * 64], b2), Xm[:, h, :], half_cols(TTm[:, h, :], b2, 1),
                                                 start=True, stop=True)
                            B.filled(last, ("ZT", l, t, lv, g))
                    for g in range(2):
                        B.wait_evacuated(pe, ("ZT", l, t, 4, g))
                    for par in range(2):
                        bank = open_work(("ai", l, t, par))
                        for h in range(par, 8, 2):
                            last = pe.matmul(bank[64 * par:64 * par + 64, (h // 2) * P:(h // 2 + 1) * P],
                                             nb(ECP)[:, t, h * HD:(h + 1) * HD], TTm[:, h, :], start=True, stop=True)
                        B.filled(last, ("ai", l, t, par))
                    B.wait_evacuated(pe, ("U", l, t))
                    bank = open_work(("SA0", l, t))
                    for h in range(8):
                        last = pe.matmul(bank[:, h * HD:(h + 1) * HD], TTm[:, h, :], U_[:, h * HD:(h + 1) * HD], start=True, stop=True)
                    B.filled(last, ("SA0", l, t))
                    for par in range(2):
                        B.wait_evacuated(pe, ("ai", l, t, par))
                    ybank = None
                    for p in range(2):
                        tk = slice(64 * p, 64 * p + 64)
                        n = 2 * (TT * l + t) + p
                        pe.wait_ge(state_ready, n + l + 1)
                        bank = open_work(("sa", l, t, p))
                        for b in range(4):
                            last = pe.matmul(bank[tk, b * P:(b + 1) * P], aiT[:, b, tk], state[:, b, :], start=True, stop=True)
                        B.filled(last, ("sa", l, t, p))
                        bank = open_work(("y1", l, t, p))
                        for b in range(4):
                            last = pe.matmul(bank[tk, b * P:(b + 1) * P], arT[:, b, 1, tk], state[:, b, :], start=True, stop=True)
                        B.filled(last, ("y1", l, t, p))
                        bank = open_work(("s", l, t, p))
                        pe.wait_ge(sa_ready, n + 1)
                        for b in range(4):
                            cs = slice(b * P, (b + 1) * P)
                            pe.matmul(bank[:, cs], nb(ENC)[tk, t, cs], pv[tk, t, 2 * RW + b * P:2 * RW + (b + 1) * P], start=True, stop=False)
                            last = pe.matmul(bank[:, cs], nb(B_)[tk, t, cs], SA[tk, cs], start=False, stop=True)
                        B.filled(last, ("s", l, t, p))
                    bank = open_work(("y2", l, t))
                    for h in range(8):
                        hs = slice(h * HD, (h + 1) * HD)
                        pe.matmul(bank[:, hs], mats[:, h, 1, :], SA[:, hs], start=True, stop=False)
                        last = pe.matmul(bank[:, hs], mats[:, h, 3, :], pv[:, t, 2 * RW + h * HD:2 * RW + (h + 1) * HD],
                                         start=False, stop=True)
                    B.filled(last, ("y2", l, t))

                qT = hT[:, 0:1024].rearrange("p (h t) -> p h t", h=4)
                kTd = hT[:, 1024:2048].rearrange("p (h t) -> p h t", h=4)
                pe.wait_ge(qs_ready, l + 1)
                for which in range(2):
                    for t in range(TT):
                        transposes(("qkT", l, which, t), [dproj[:, t, which * RW + h * P:which * RW + (h + 1) * P] for h in range(4)])
                for which in range(2):
                    for t in range(TT):
                        B.wait_evacuated(pe, ("qkT", l, which, t))
                aT = W1[:, :].rearrange("p (s n) -> p s n", s=2)

                def diff_scores(h):
                    for m in range(2):
                        r = slice(64 * m, 64 * m + 64)
                        bank = open_work(("ds", l, h, m))
                        pe.matmul(bank[:, 0:128], qT[r, h, 0:128], kTd[r, h, 0:128], start=True, stop=True)
                        B.filled(pe.matmul(bank[:, 128:384], qT[r, h, 128:256], kTd[r, h, :], start=True, stop=True), ("ds", l, h, m))
                diff_scores(0)
                for h in range(4):
                    if h < 3:
                        diff_scores(h + 1)
                    pe.wait_ge(attn_ready, 4 * l + h + 1)
                    bank = open_work(("atT", l, h))
                    att = SH[:, 2304 + 384 * (h % 2):2304 + 384 * (h % 2) + 384]
                    for i in range(3):
                        last = pe.transpose(bank[:, i * P:(i + 1) * P], att[:, i * P:(i + 1) * P], ident)
                    B.filled(last, ("atT", l, h))
                    B.wait_evacuated(pe, ("atT", l, h))
                    bank = open_work(("pv", l, h))
                    vv = [dproj[:, t, 2 * RW + h * DV:2 * RW + (h + 1) * DV] for t in range(TT)]
                    pe.matmul(bank[:, 0:128], aT[:, h % 2, 0:128], vv[0], start=True, stop=True)
                    pe.matmul(bank[:, 128:256], aT[:, h % 2, 128:256], vv[0], start=True, stop=False)
                    B.filled(pe.matmul(bank[:, 128:256], aT[:, h % 2, 256:384], vv[1], start=False, stop=True), ("pv", l, h))
                to_hT(("hT", l, 1), hNv, lambda t: pe.wait_ge(ycat, 2 * l + 2))
                memn = nbf[:, 4096:6144].rearrange("p (t c) -> p t c", t=TT)
                op_steps = project_steps(("op", l), half_chunks(2), h_ready(("hT", l, 1)))
                next(op_steps)
                next(op_steps)
                next(op_steps)
                to_hT(("mT", l), memn, lambda t: pe.wait_ge(mn_done, 2 * l + t + 1))
                for _ in op_steps:
                    pass

                kv_steps = project_steps(("kv", l), half_chunks(4), h_ready(("mT", l)))
                for _ in range(10):
                    next(kv_steps)
                to_hT(("hT", l, 2), hNv, lambda t: pe.wait_ge(hn_done, 2 * (3 * l + 1) + t + 1))
                for _ in kv_steps:
                    pass
                project(("xq", l), half_chunks(2), h_ready(("hT", l, 2)))
                qn = proj[:, 0:2048].rearrange("p (t c) -> p t c", t=TT)
                kn = dproj[:, :, :].rearrange("p t c -> p (t c)")[:, 0:2048].rearrange("p (t c) -> p t c", t=TT)
                vx = SH[:, 0:2048].rearrange("p (t c) -> p t c", t=TT)
                kTx = nbf[:, 0:2048].rearrange("p (k t) -> p k t", k=KD)
                qTx = nbf[:, 2048:4096].rearrange("p (k t) -> p k t", k=KD)
                to_hT(("xqT", l), qn, lambda t: pe.wait_ge(xq_n, l + 1))
                to_hT(("xkT", l), kn, lambda t: pe.wait_ge(xk_n, l + 1))
                for nm in ("xqT", "xkT"):
                    for t in range(TT):
                        for g in range(2):
                            B.wait_evacuated(pe, (nm, l, t, g))
                PT = nbf[:, 8192:9216].rearrange("p (s n) -> p s n", s=2)
                px = SH[:, 2048:3072].rearrange("p (s q k) -> p s q k", s=2, q=2)

                def x_scores(h):
                    bank = open_work(("xs", l, h))
                    for t in range(TT):
                        for kb in range(2):
                            last = pe.matmul(bank[:, t * 256:(t + 1) * 256], qTx[:, 2 * h + kb, t * P:(t + 1) * P], kTx[:, 2 * h + kb, :],
                                             start=(kb == 0), stop=(kb == 1))
                    B.filled(last, ("xs", l, h))
                x_scores(0)
                for h in range(XH):
                    if h < XH - 1:
                        x_scores(h + 1)
                    B.wait_evacuated(pe, ("xs", l, h))
                    transposes(("xpT", l, h), [px[:, h % 2, q, m * P:(m + 1) * P] for m in range(2) for q in range(2)])
                    B.wait_evacuated(pe, ("xpT", l, h))
                    bank = open_work(("xo", l, h))
                    for q in range(TT):
                        for m in range(2):
                            last = pe.matmul(bank[:, q * 256:(q + 1) * 256], PT[:, h % 2, (m * 2 + q) * P:(m * 2 + q + 1) * P],
                                             vx[:, m, h * XD:(h + 1) * XD], start=(m == 0), stop=(m == 1))
                    B.filled(last, ("xo", l, h))
                on = memn
                to_hT(("oT", l), on, lambda t: [B.wait_evacuated(pe, ("xo", l, h)) for h in range(XH)])
                project(("wo", l), half_chunks(2), h_ready(("oT", l)))

                to_hT(("hT", l, 3), hNv, lambda t: pe.wait_ge(hn_done, 2 * (3 * l + 2) + t + 1))
                if l == 0:
                    h_ready(("hT", l, 3))()
                    nch = FD // FC
                    ybanks = []
                    act = nbf[:, 0:1024].rearrange("p (s t n) -> p s t n", s=2, t=2)

                    def hidden_T(c):
                        bank = B.open(pe, ("fT", c), 2 + c % 2)
                        for k in range(2):
                            for t in range(TT):
                                if k == 0:
                                    B.wait_evacuated(pe, ("gu", c, t))
                                last = pe.transpose(bank[:, (k * 2 + t) * P:(k * 2 + t + 1) * P], act[:, c % 2, t, k * P:(k + 1) * P], ident)
                        B.filled(last, ("fT", c))

                    def down(c):
                        B.wait_evacuated(pe, ("fT", c))
                        if c == 0:
                            ybanks.extend(B.open(pe, ("fy", i), 4 + i) for i in range(4))
                        for k in range(2):
                            wh, wl = take("down")
                            for t in range(TT):
                                a = 2048 + k * SEQ + t * P
                                for n in range(2):
                                    ns = slice(n * 512, (n + 1) * 512)
                                    last = product(ybanks[t * 2 + n][:, :], (h_hi[:, a:a + P], h_lo[:, a:a + P]), (wh[:, ns], wl[:, ns]),
                                                   c == 0 and k == 0, c == nch - 1 and k == 1)
                                    if c == nch - 1 and k == 1:
                                        B.filled(last, ("fy", t * 2 + n))
                            if c == nch - 1 and k == 1:
                                used_with(("fy", 3))
                            else:
                                used(last)
                    for c in range(nch):
                        banks = [B.open(pe, ("gu", c, t), t) for t in range(TT)]
                        for j, (g, half) in enumerate(GU):
                            wh, wl = take("gu")
                            for t in range(TT):
                                for k in range(4):
                                    last = product(banks[t][:, g * FC:(g + 1) * FC], lhs_h(half * 4 + k, t), (wh[:, k, :], wl[:, k, :]),
                                                   half == 0 and k == 0, half == 1 and k == 3)
                                if j == 3:
                                    B.filled(last, ("gu", c, t))
                            if j == 3:
                                used_with(("gu", c, TT - 1))
                            else:
                                used(last)
                            if j == 1 and c:
                                hidden_T(c - 1)
                        if c:
                            down(c - 1)
                    hidden_T(nch - 1)
                    down(nch - 1)

            assert at[0] == NPRE == len(freed)
            l = 1
            h_ready(("hT", l, 3))()
            pe.wait_ge(lw_in, 80)
            bank = B.open(pe, ("logit",), 6)
            for t in range(TT):
                for k in range(KD):
                    last = pe.matmul(bank[:, t * NE:(t + 1) * NE], hTv[:, k, t * P:(t + 1) * P], router_w[:, k, :], start=(k == 0), stop=(k == KD - 1))
            B.filled(last, ("logit",))
            sel = nbf[:, 8192:8192 + 2 * NE].rearrange("p (t e) -> p t e", t=TT)
            pe.wait_ge(rt_sel, 1)
            bank = B.open(pe, ("pos",), 7)
            pe.matmul(bank[:, 0:8], C("utri"), sel[:, 0, :], start=True, stop=True)
            pe.matmul(bank[:, 8:16], C("ones"), sel[:, 0, :], start=True, stop=False)
            pe.matmul(bank[:, 8:16], C("utri"), sel[:, 1, :], start=False, stop=True)
            pe.matmul(bank[:, 16:24], C("ones"), sel[:, 0, :], start=True, stop=False)
            B.filled(pe.matmul(bank[:, 16:24], C("ones"), sel[:, 1, :], start=False, stop=True), ("pos",))

            Psel = nbf[:, 2048:2304].rearrange("p (t j) -> p t j", t=TT)
            Pg = nbf[:, 2304:2560].rearrange("p (t j) -> p t j", t=TT)
            PgT = nbf[:, 2560:2816]
            Ysb = nbf[:, 4096:5120]
            act = nbf[:, 0:512].rearrange("p (s n) -> p s n", s=2)

            def bring(more):
                for g in range(2):
                    bank = B.open(pe, ("he", g), 6 + g, more(6 + g))
                    for k in range(4):
                        for t in range(TT):
                            last = pe.matmul(bank[:, k * P:(k + 1) * P], hNv[:, t, (4 * g + k) * P:(4 * g + k + 1) * P], Psel[:, t, :],
                                             start=(t == 0), stop=(t == 1))
                    B.filled(last, ("he", g))

            def scatter(t, more):
                for n in range(2):
                    if t == 0:
                        pe.wait_ge(evacuated[4 + n], start[4 + n] + more(4 + n))
                    bank = B.open(pe, ("sc", t, n), 6 + n, more(6 + n))
                    B.filled(pe.matmul(bank[:, :], PgT[:, t * P:(t + 1) * P], Ysb[:, n * 512:(n + 1) * 512], start=True, stop=True), ("sc", t, n))

            pe.wait_ge(sel_done, 1)
            bring(lambda bank: 0)
            for n in range(2):
                bank = B.open(pe, ("ey", n), 4 + n)
                B.filled(pe.matmul(bank[:, :], PgT[:, 0:P], Ysb[:, n * 512:(n + 1) * 512], start=True, stop=True), ("ey", n))

            start, start_used = list(B.n), n_used[0]

            def expert(i):
                B.n = list(start)
                n_used[0] = start_used
                del freed[NPRE:]

                def more(bank):
                    return i * MOE_PER[bank]

                def open_(name, bank):
                    return B.open(pe, name, bank, more(bank))

                def take_e(j, kind):
                    pe.wait_ge(lo_done, NPRE + j + 1 + i * PER)
                    return shaped(hi_e[j % NS_E], kind, 512), shaped(lo_e[j % NS_E], kind, 512)
                pe.wait_ge(h_split, H_SPLIT0 + 1 + i)
                ybanks = []

                def hidden_T(c):
                    bank = open_(("eT", c), 2)
                    B.wait_evacuated(pe, ("egu", c), more(c % 2))
                    for k in range(2):
                        last = pe.transpose(bank[:, k * P:(k + 1) * P], act[:, c % 2, k * P:(k + 1) * P], ident)
                    B.filled(last, ("eT", c))

                def down(c):
                    B.wait_evacuated(pe, ("eT", c), more(2))
                    if c == 0:
                        ybanks.extend(open_(("ey", n), 4 + n) for n in range(2))
                    for k in range(2):
                        wh, wl = take_e(6 * c + 8 + k if c < STEPS - 1 else 6 * c + 4 + k, "down")
                        a = 2048 + k * P
                        for n in range(2):
                            ns = slice(n * 512, (n + 1) * 512)
                            last = product(ybanks[n][:, :], (h_hi[:, a:a + P], h_lo[:, a:a + P]), (wh[:, ns], wl[:, ns]),
                                           c == 0 and k == 0, c == STEPS - 1 and k == 1)
                            if c == STEPS - 1 and k == 1:
                                B.filled(last, ("ey", n))
                        if c == STEPS - 1 and k == 1:
                            used_with(("ey", 1))
                        else:
                            used(last)
                for c in range(STEPS):
                    bank = open_(("egu", c), c % 2)
                    for j, (g, half) in enumerate(GU):
                        wh, wl = take_e((6 * c - 2 if c else 0) + j, "gu")
                        for k in range(4):
                            a = (half * 4 + k) * P
                            last = product(bank[:, g * FC:(g + 1) * FC], (h_hi[:, a:a + P], h_lo[:, a:a + P]), (wh[:, k, :], wl[:, k, :]),
                                           half == 0 and k == 0, half == 1 and k == 3)
                        if j < 3:
                            used(last)
                        else:
                            B.filled(last, ("egu", c))
                            used_with(("egu", c))
                        if j == 1 and c:
                            hidden_T(c - 1)
                    if c:
                        down(c - 1)
                    if c < TT:
                        scatter(c, more)
                    if c == GATE_STEP:
                        pe.wait_ge(sel_done, i * 2 + 2)
                        bank = open_(("pgT",), 3)
                        for t in range(TT):
                            last = pe.transpose(bank[:, t * P:(t + 1) * P], Pg[:, t, :], ident)
                        B.filled(last, ("pgT",))
                    if c == NEXT_STEP:
                        pe.wait_ge(sel_done, i * 2 + 3)
                        bring(more)
                hidden_T(STEPS - 1)
                down(STEPS - 1)

            with pe.Fori(0, NE) as i:
                expert(i)
            pe.wait_ge(items_in, 1)
            n_over = pe.value_load(sb_items[0:1, 0:1], min_val=0, max_val=NOVER)
            with pe.If(n_over > 0):
                with pe.Fori(NE, n_over + NE) as i:
                    expert(i)
            B.n = list(start)
            for t in range(TT):
                scatter(t, lambda bank: (n_over + NE) * MOE_PER[bank])

        @block.sync
        def _(sp):
            sp.dma_start(cst[:, :], consts).then_inc(small_in, 16)
            for n, (kind, src, cw) in enumerate(blocks):
                if n >= RING:
                    sp.wait_ge(lo_done, n - RING + 1)
                sp.dma_start(shaped(ring[:, n % RING, :], kind, cw), src).then_inc(block_in[n % RING], 16)

            def expert_blocks(e, i):
                j = 0
                for c in range(STEPS + 1):
                    todo = [gu(e, c, *g) for g in GU] if c < STEPS else []
                    todo += [down(e, c - 1, k) for k in range(2)] if c else []
                    for kind, src in todo:
                        sp.wait_ge(lo_done, NPRE + j - RING_E + 1 + i * PER)
                        s = j % RING_E
                        sp.dma_start(shaped(ring_e[s], kind, 0), src).then_inc(expert_block_in[s], 16)
                        j += 1

            def gu(e, c, g, half):
                c0 = g * FE + c * FC
                return "gu", expert_gu[0, bass.ds(e, 1), half * 512:(half + 1) * 512, c0:c0 + FC].rearrange("a (k p) f -> p (a k) f", p=P)

            def down(e, c, k):
                return "down", expert_down[0, bass.ds(e, 1), c * FC + k * P:c * FC + (k + 1) * P, :].rearrange("a p n -> p (a n)")
            sp.wait_ge(lo_done, NPRE)
            with sp.Fori(0, NE) as i:
                expert_blocks(i, i)
            sp.wait_ge(items_in, 1)
            n_over = sp.value_load(sb_items[0:1, 0:1], min_val=0, max_val=NOVER)
            with sp.If(n_over > 0):
                with sp.Fori(NE, n_over + NE) as i:
                    e = sp.value_load(sb_items[0:1, bass.ds(i - (NE - 1), 1)], min_val=0, max_val=NE - 1)
                    expert_blocks(e, i)
            sp.wait_ge(final, 2)
            sp.dma_start(out[0].rearrange("(t p) d -> p t d", p=P), x[:, :, :]).then_inc(out_s, 16)
            sp.wait_ge(out_s, 16)

        @block.gpsimd
        def _(pool):
            n = [0]

            def step(ins):
                n[0] += 1
                ins.then_inc(pool_step, 1)
                pool.wait_ge(pool_step, n[0])
            pool.wait_ge(x_in_s, 16)
            pool.wait_ge(small_in, 48)
            for w, s in ((vresd_w[:, :, :], vres_down[0].rearrange("(k p) n -> p k n", p=P)),
                         (router_w[:, :, :], router[0].rearrange("(k p) n -> p k n", p=P))):
                pool.dma_start(w, s).then_inc(lw_in, 16)
            pool.dma_start(vec[:, :], vecs[0].partition_broadcast(P)).then_inc(vec_in, 16)
            for l in range(DEPTH):
                if l:
                    pool.wait_ge(ycat, 2 * l)
                    pool.dma_start(vec[:, :], vecs[l].partition_broadcast(P)).then_inc(vec_in, 16)
                    B.wait_evacuated(pool, ("wo", l - 1, 1, 1))
                pool.dma_start(lora_w[0:64, :], decay_up[l]).then_inc(lw_in, 16)
                pool.dma_start(lora_w[64:128, :], iclr_up[l]).then_inc(lw_in, 16)
                pool.dma_start(gate_w, gate_up[l]).then_inc(lw_in, 16)
                if l:
                    pool.dma_start(vres_w, vres_up[l - 1]).then_inc(lw_in, 16)
                    B.wait_evacuated(pool, ("fy", 3))
                pool.dma_start(mu, mus[l].partition_broadcast(P)).then_inc(mu_in, 16)
                pool.memset(prev[0:1, 0, :], 0.0).then_inc(row0_ready, 1)
                for t in range(TT):
                    for lv in range(5):
                        for g in range(2):
                            if lv == 0:
                                for h in range(4 * g, 4 * g + 4):
                                    B.wait_evacuated(pool, ("m12", l, t, h))
                                if t:
                                    B.wait_filled(pool, ("X", l, t - 1, 4, g))
                            else:
                                B.wait_filled(pool, ("X", l, t, lv - 1, g))
                            m = C("lvl")[:, lv * P:(lv + 1) * P].unsqueeze(1)
                            pool.tensor_tensor(Cm[:, 4 * g:4 * g + 4, :], mats[:, 4 * g:4 * g + 4, 0, :], bc(m, 4, P), MUL)\
                                .then_inc(c_ready, 1)
                    for p in range(2):
                        c = TT * t + p
                        if c:
                            pool.wait_ge(state_ready, 5 * l + c + 1)
                        else:
                            B.wait_evacuated(pool, ("wt", l))
                        wts = sm[:, 0:16].rearrange("p (t b c) -> p t b c", t=TT, b=4)[:, t, :, p:p + 1]
                        pool.tensor_tensor(keep[:, :, :], bc(C("bd").unsqueeze(1), 4, P), bc(wts, 4, P), MUL).then_inc(keep_ready, 1)
                B.wait_filled(pool, ("y2", l, 1))
                pool.dma_start(nbf[:, 4096:6144].rearrange("p (t c) -> p t c", t=TT), mem_in[0].rearrange("(t p) d -> p t d", p=P))\
                    .then_inc(mem_in_s, 16)
                vh = pv[:, :, 2 * RW:3 * RW].rearrange("p t (n c) -> p t n c", c=HD)
                bon = sm[:, 16:32].rearrange("p (t n) -> p t n", t=TT).unsqueeze(3)
                step(pool.tensor_tensor(nb(ENC).rearrange("p t (n c) -> p t n c", c=HD), vh, bc(bon, TT, 8, HD), MUL))
                step(pool.tensor_tensor(nb(ENC), nb(ENC), bc(V("gn_b").unsqueeze(1), TT, RW), ADD))
                pool.wait_ge(gn_ready, l + 1)
                step(pool.tensor_tensor(nb(EC), nb(EC), bc(V("gn_w").unsqueeze(1), TT, RW), MUL))
                step(pool.tensor_tensor(nb(EC), nb(EC), nb(ENC), ADD))
                pool.tensor_tensor(hNv[:, :, 0:RW], nb(EC), nb(G_), MUL).then_inc(ycat, 1)

        @block.scalar
        def _(act):
            act.dma_start(x[:, :, :], x_in[0].rearrange("(t p) d -> p t d", p=P)).then_inc(x_in_s, 16)
            act.dma_start(col[:, :, :], cols.rearrange("l p c -> p l c")).then_inc(small_in, 16)
            act.dma_start(posi[:, :], pos_in).then_inc(small_in, 16)

            split_to, ahead = splitter(act, lambda n: hi_of(act, n))

            def copy(dst, name, src=None, scale=1.0, func=ACT.Copy):
                ahead(name)
                bank = B.wait_filled(act, name)
                B.release(act.activation(dst, bank[:, :] if src is None else src(bank), func, scale=scale), name)

            def squares(srcs, junk, cols_, done):
                for t in range(TT):
                    act.activation(junk[:, t, :], srcs[:, t, :], ACT.Square, accum_out=cols_[:, t:t + 1]).then_inc(done, 1)

            def h_parts(name):
                for g in range(2):
                    for t in range(TT):
                        ahead((*name, t, g))
                        B.wait_evacuated(act, (*name, t, g))
                        act.activation(h_hi[:, 0:2048].rearrange("p (k t) -> p k t", k=KD)[:, 4 * g:4 * g + 4, t * P:(t + 1) * P],
                                       hTv[:, 4 * g:4 * g + 4, t * P:(t + 1) * P], ACT.Copy).then_inc(h_hi_done, 1)

            act.wait_ge(x_in_s, 16)
            squares(x, hNv, sm[:, 32:34], sq_done)
            act.wait_ge(rope_in, 1)
            act.activation(rope[:, 0:2, :], rope[:, 2:4, :], ACT.Sin).then_inc(rope_sin, 1)
            for l in range(DEPTH):
                h_parts(("hT", l, 0))
                for g, (c0, cw) in enumerate(chunks_in[0:4] + ([(RC, VR)] if l else [])):
                    names = [("in", l, g, t) if g < 4 else ("vr", l, t) for t in range(TT)]
                    for t in range(TT):
                        copy(pv[:, t, c0:c0 + cw], names[t], lambda b, cw=cw: b[:, 0:cw])
                    for t in range(TT):
                        B.wait_evacuated(act, names[t])
                    if g == 0:
                        act.wait_ge(row0_ready, l + 1)
                    cs = slice(c0, c0 + cw)
                    act.dma_start(prev[1:113, :, cs], pv[0:112, :, cs]).then_inc(shifted_in[g], 16)
                    act.dma_start(prev[113:128, :, cs], pv[112:127, :, cs]).then_inc(shifted_in[g], 16)
                    act.dma_start(prev[0:1, 1, cs], pv[127:128, 0, cs]).then_inc(shifted_in[g], 16)
                ahead(("lt", l))
                bank = B.wait_filled(act, ("lt", l))
                act.activation(lT[0:64, 0, :], bank[0:64, 0:256], ACT.Tanh)
                act.activation(lT[64:128, 0, :], bank[64:128, 0:256], ACT.Copy)
                B.release(act.activation(lT[:, 1, :], bank[:, 256:512], ACT.Sigmoid), ("lt", l))
                if l:
                    copy(vrT, ("vt", l), lambda b: b[0:VR, 0:256])
                for t in range(TT):
                    ahead(("wup", l, t))
                    B.wait_evacuated(act, ("wup", l, t))
                    act.activation(nb(TMP)[:, t, :], nb(TMP)[:, t, :], ACT.Sigmoid).then_inc(sg_scan, 1)
                    ahead(("aup", l, t))
                    B.wait_evacuated(act, ("aup", l, t))
                    act.activation(nb(A_)[:, t, :], nb(A_)[:, t, :], ACT.Sigmoid).then_inc(rate_done, 1)
                    if l:
                        ahead(("vup", l, t))
                        B.wait_evacuated(act, ("vup", l, t))
                        act.activation(nb(KK)[:, t, :], nb(KK)[:, t, :], ACT.Sigmoid).then_inc(vmix_done, 1)
                    copy(nb(G_)[:, t, :], ("gup", l, t))
                diff_in = [(c, t) for c in range(3) for t in range(TT)]

                def diff_proj(before):
                    while diff_in and B.before[("inb", l, *diff_in[0])] <= B.before[before]:
                        c, t = diff_in.pop(0)
                        copy(dproj[:, t, c * RW:(c + 1) * RW], ("inb", l, c, t))
                for t in range(TT):
                    diff_proj(("cum", l, t))
                    ahead(("cum", l, t))
                    bank = B.wait_filled(act, ("cum", l, t))
                    act.activation(nb(EC)[:, t, :], bank[:, :], ACT.Exp).then_inc(expc, 1)
                    copy(nb(ENC)[:, t, :], ("cum", l, t), scale=-1.0, func=ACT.Exp)
                    copy(nb(ECP)[:, t, :], ("cums", l, t), func=ACT.Exp)
                diff_proj(("wt", l))
                copy(sm[:, 0:16], ("wt", l), lambda b: b[:, 0:16])
                diff_proj(("aT", l, 0))
                for t in range(TT):
                    copy(arT[:, :, 0, :], ("aT", l, t))
                    copy(arT[:, :, 1, :], ("rT", l, t))
                    copy(bT, ("bT", l, t))
                    copy(kT, ("kT", l, t))
                    copy(U_, ("U", l, t), scale=-1.0)
                    for lv in range(5):
                        for g in range(2):
                            copy(Xm[:, 4 * g:4 * g + 4, :], ("X", l, t, lv, g))
                        if t == 0:
                            diff_proj(("ZT", l, t, lv, 0))
                    for par in range(2):
                        r = slice(64 * par, 64 * par + 64)
                        copy(aiT[r, :, :], ("ai", l, t, par), lambda b, r=r: b[r, :])
                    copy(SA0, ("SA0", l, t))
                    for p in range(2):
                        r = slice(64 * p, 64 * p + 64)
                        copy(yraw[r, t, :], ("y1", l, t, p), lambda b, r=r: b[r, :])
                assert not diff_in
                act.wait_ge(lam_in, l + 1)
                act.activation(sm[:, 38:40], sm[:, 36:38], ACT.Exp).then_inc(lam_exp, 1)
                qk = hT[:, :].rearrange("p (w h t) -> p w h t", w=2, h=4)
                for which in range(2):
                    for t in range(TT):
                        copy(qk[:, which, :, t * P:(t + 1) * P], ("qkT", l, which, t))

                def diff_out(h):
                    copy(W1[:, 512 * (h % 2):512 * (h % 2) + 384], ("atT", l, h), lambda b: b[:, 0:384])
                    copy(hNv[:, :, RW + h * DV:RW + (h + 1) * DV], ("pv", l, h), lambda b: b[:, 0:256].rearrange("p (t c) -> p t c", t=TT))
                for h in range(DH):
                    for m in range(2):
                        ahead(("ds", l, h, m))
                        act.wait_ge(smx, 8 * l + 2 * h + m + 1)
                        if h >= 2:
                            act.wait_ge(attn_ready, 4 * l + h - 1)
                        s_, p_ = 384 * m, 768 + 384 * (2 * (h % 2) + m)
                        for q, (a, b) in enumerate(((0, 128), (128, 384))):
                            j = 4 * h + 2 * m + q
                            ins = act.activation(SH[:, p_ + a:p_ + b], SH[:, s_ + a:s_ + b], ACT.Exp, bias=ss[:, j:j + 1],
                                                 scale=DQ ** -0.5, accum_out=ss2[:, j:j + 1])
                        ins.then_inc(pexp, 1)
                    if h:
                        diff_out(h - 1)
                diff_out(DH - 1)
                act.wait_ge(mem_in_s, 16 * (l + 1))
                memn = nbf[:, 4096:6144].rearrange("p (t c) -> p t c", t=TT)
                squares(memn, nbf[:, 6144:8192].rearrange("p (t c) -> p t c", t=TT), sm[:, 34:36], msq_done)

                def x_squares(name, first=lambda: None):
                    for c in range(2):
                        for t in range(TT):
                            ahead((*name, c, t))
                            B.wait_evacuated(act, (*name, c, t))
                    first()
                    for t in range(TT):
                        act.activation(hNv[:, t, :], x[:, t, :], ACT.Square, accum_out=sm[:, 32 + t:33 + t]).then_inc(sq_done, 1)
                h_parts(("hT", l, 1))
                x_squares(("op", l), lambda: h_parts(("mT", l)))
                qn = proj[:, 0:2048].rearrange("p (t c) -> p t c", t=TT)
                kn = dproj[:, :, :].rearrange("p t c -> p (t c)")[:, 0:2048].rearrange("p (t c) -> p t c", t=TT)
                vx = SH[:, 0:2048].rearrange("p (t c) -> p t c", t=TT)
                for c in range(4):
                    for t in range(TT):
                        copy((kn if c < 2 else vx)[:, t, (c % 2) * 512:(c % 2 + 1) * 512], ("kv", l, c, t))
                h_parts(("hT", l, 2))
                for c in range(2):
                    for t in range(TT):
                        copy(qn[:, t, c * 512:(c + 1) * 512], ("xq", l, c, t))
                px = SH[:, 2048:3072].rearrange("p (s q k) -> p s q k", s=2, q=2)
                for h in range(XH):
                    ahead(("xs", l, h))
                    bank = B.wait_filled(act, ("xs", l, h))
                    act.wait_ge(xs_mx, XH * l + h + 1)
                    if h >= 2:
                        B.wait_filled(act, ("xpT", l, h - 2))
                    for q in range(TT):
                        ins = act.activation(px[:, h % 2, q, :], bank[:, q * 256:(q + 1) * 256], ACT.Exp, bias=ss[:, 16 + 2 * h + q:17 + 2 * h + q],
                                             scale=XD ** -0.5, accum_out=ss2[:, 16 + 2 * h + q:17 + 2 * h + q])
                    B.release(ins, ("xs", l, h))
                h_parts(("oT", l))
                x_squares(("wo", l))
                h_parts(("hT", l, 3))
                if l == 0:
                    sil = nbf[:, 1536:2048].rearrange("p (t n) -> p t n", t=TT)
                    for c in range(FD // FC):
                        for t in range(TT):
                            ahead(("gu", c, t))
                            bank = B.wait_filled(act, ("gu", c, t))
                            act.activation(sil[:, t, :], bank[:, 0:FC], ACT.Silu).then_inc(silu_done, 1)
                        ahead(("fT", c))
                        bank = B.wait_filled(act, ("fT", c))
                        act.activation(h_hi[:, 2048:2560], bank[:, :], ACT.Copy).then_inc(act_hi, 1)
                    for t in range(TT):
                        for n in range(2):
                            ahead(("fy", 2 * t + n))
                            B.wait_evacuated(act, ("fy", 2 * t + n))
                    squares(x, hNv, sm[:, 32:34], sq_done)
            wt = nbf[:, 8256:8260]
            act.wait_ge(w_in, 1)
            act.activation(wt, wt, ACT.Sigmoid).then_inc(w_sig, 1)

            def next_hi():
                act.activation(h_hi[:, 0:1024], hT[:, 0:1024], ACT.Copy).then_inc(h_hi_done, 1)

            def result(i):
                bank = B.wait_filled(act, ("ey", 0), (i - 1) * MOE_PER[4])
                B.release(act.activation(nbf[:, 4096:4608], bank[:, :], ACT.Copy), ("ey", 0))

            def expert(i):
                done = [0]

                def split_to(m):
                    while done[0] < min(m, PER):
                        expert_hi_of(act, done[0], i)
                        done[0] += 1
                split_to(LOOK)
                result(i)
                sil = nbf[:, 1536:2048].rearrange("p (s n) -> p s n", s=2)
                for c in range(STEPS):
                    g_last = 6 * c + 1 if c else 3
                    split_to(g_last + 1 + LOOK)
                    bank = B.wait_filled(act, ("egu", c), i * MOE_PER[c % 2])
                    act.activation(sil[:, c % 2, :], bank[:, 0:FC], ACT.Silu).then_inc(silu_done, 1)
                    if c == STEPS - 1:
                        next_hi()
                    split_to((6 * c + 6 if c < STEPS - 1 else PER) + LOOK)
                    bank = B.wait_filled(act, ("eT", c), i * MOE_PER[2])
                    act.activation(h_hi[:, 2048:2304], bank[:, 0:256], ACT.Copy).then_inc(act_hi, 1)
                    if c == GATE_STEP:
                        bank = B.wait_filled(act, ("pgT",), i * MOE_PER[3])
                        B.release(act.activation(nbf[:, 2560:2816], bank[:, 0:256], ACT.Copy), ("pgT",))
                    if c == NEXT_STEP + 1:
                        for g in range(2):
                            B.wait_evacuated(act, ("he", g), i * MOE_PER[6 + g])
            B.wait_filled(act, ("logit",))
            for g in range(2):
                act.wait_ge(evacuated[6 + g], B.use[("he", g)][1] + 1 - MOE_PER[6 + g])
            next_hi()
            with act.Fori(0, NE) as i:
                expert(i)
            act.wait_ge(items_in, 1)
            n_over = act.value_load(sb_items[0:1, 0:1], min_val=0, max_val=NOVER)
            with act.If(n_over > 0):
                with act.Fori(NE, n_over + NE) as i:
                    expert(i)
            result(n_over + NE)

        @block.vector
        def _(dve):
            n = [0]

            def step(ins, more=0):
                n[0] += 1
                ins.then_inc(dve_step, 1)
                dve.wait_ge(dve_step, n[0] + more)

            def tt(o, a, b, op, more=0):
                step(dve.tensor_tensor(o, a, b, op), more)

            def ts(o, a, s1, s2, op0, op1=None, more=0):
                step(dve.tensor_scalar(o, a, s1, s2, op0, op1) if op1 is not None else dve.tensor_scalar(o, a, s1, None, op0), more)

            def stt(o, a, s, b, op0, op1):
                step(dve.scalar_tensor_tensor(o, a, s, b, op0, op1))

            def total(o, a):
                step(dve.tensor_reduce(o, a, AX.X, ADD))

            def rsqrt(v, w, scale, eps):
                y, t, z = rst[:, 0:w], rtmp[:, 0:w], v[:, 0:w]
                ts(z, z, scale, eps, MUL, ADD)
                ts(y.bitcast(I32), z.bitcast(I32), 1, None, ALU.logical_shift_right)
                ts(y.bitcast(I32), y.bitcast(I32), -1.0, 1597463007.0, MUL, ADD)
                for _ in range(3):
                    tt(t, y, y, MUL)
                    stt(t, t, -0.5, z, MUL, MUL)
                    stt(y, t, 1.5, y, ADD, MUL)
                return y

            split_to, ahead = splitter(dve, lambda n: lo_of(dve, n))

            def evac(dst, name, src, other, op):
                ahead(name)
                bank = B.wait_filled(dve, name)
                B.release(dve.tensor_tensor(dst, src(bank), other, op), name)
                B.wait_evacuated(dve, name)

            def four(b):
                return b[:, :].rearrange("p (b t) -> p b t", b=4)

            def gain_hT(name, dst, gains):
                for g in range(2):
                    for t in range(TT):
                        evac(dst[:, 4 * g:4 * g + 4, t * P:(t + 1) * P], (*name, t, g), four, bc(gains[:, 4 * g:4 * g + 4].unsqueeze(2), 4, P), MUL)

            n_lo = [0]

            def h_lo_parts(name):
                for g in range(2):
                    for t in range(TT):
                        n_lo[0] += 1
                        dve.wait_ge(h_hi_done, n_lo[0])
                        a = lambda z: z.rearrange("p (k t) -> p k t", k=KD)[:, 4 * g:4 * g + 4, t * P:(t + 1) * P]
                        dve.tensor_tensor(a(h_lo[:, 0:2048]), a(hT[:, :]), a(h_hi[:, 0:2048]).bitcast(F32), SUB).then_inc(h_split, 1)
                assert n_lo[0] == LO_PARTS[name]

            def plain_hT(name):
                for g in range(2):
                    for t in range(TT):
                        ahead((*name, t, g))
                        bank = B.wait_filled(dve, (*name, t, g))
                        B.release(dve.tensor_copy(hTv[:, 4 * g:4 * g + 4, t * P:(t + 1) * P], bank[:, :]), (*name, t, g))
                h_lo_parts(name)

            def gains(l, name, w=8):
                return col[:, l, COL[name]:COL[name] + w]

            def normalize(l, s, gain, name, parts=True):
                for t in range(TT):
                    dve.wait_ge(sq_done, 2 * (3 * l + s) + t + 1)
                r = rsqrt(sm[:, 32:34], TT, 1.0 / D, EPS)
                for t in range(TT):
                    dve.tensor_scalar(hNv[:, t, :], x[:, t, :], r[:, t:t + 1], None, MUL).then_inc(hn_done, 1)
                gain_hT(name, hTv, gains(l, gain))
                if parts:
                    h_lo_parts(name)

            def add_x(name):
                for c in range(2):
                    for t in range(TT):
                        xs = x[:, t, c * 512:(c + 1) * 512]
                        evac(xs, (*name, c, t), lambda b: b[:, :], xs, ADD)

            dve.wait_ge(small_in, 48)
            posf = sm[:, 40:42]
            step(dve.tensor_copy(posf, posi[:, :]))
            ang, k_, r_ = rope[:, 0, :], rope[:, 1, :], rope[:, 2, :]
            tt(ang.rearrange("p (t f) -> p t f", t=TT), bc(posf.unsqueeze(2), TT, 8), bc(C("freq").unsqueeze(1), TT, 8), MUL)
            ts(k_, ang, 1.0 / (2 * math.pi), 12582912.0, MUL, ADD)
            ts(k_, k_, -12582912.0, None, ADD)
            stt(r_, k_, -6.28125, ang, MUL, ADD)
            stt(r_, k_, -(2 * math.pi - 6.28125), r_, MUL, ADD)
            ts(r_, r_, -3.1415925, 3.1415925, ALU.max, ALU.min)
            ts(rope[:, 3, :], r_, 0.5, None, MUL)
            step(dve.tensor_copy(rope[:, 0, :], r_))
            dve.tensor_copy(rope[:, 1, :], r_).then_inc(rope_in, 1)
            dve.wait_ge(rope_sin, 1)
            tt(rope[:, 1, :], rope[:, 1, :], rope[:, 1, :], MUL)
            ts(rope[:, 1, :], rope[:, 1, :], -2.0, 1.0, MUL, ADD)
            sin = rope[:, 0, :].rearrange("p (t f) -> p t f", t=TT)
            cos = rope[:, 1, :].rearrange("p (t f) -> p t f", t=TT)

            for l in range(DEPTH):
                lam_init = 0.8 - 0.6 * math.exp(-0.3 * l)
                normalize(l, 0, "mix", ("hT", l, 0))
                dve.wait_ge(vec_in, 16 * (l + 1))
                dve.wait_ge(mu_in, 16 * (l + 1))
                for g, (c0, cw) in enumerate(chunks_in[0:4] + ([(RC, VR)] if l else [])):
                    ahead(("in", l, g + 1, 1) if g < 3 else ("lt", l))
                    dve.wait_ge(shifted_in[g], 48 * (l + 1) if g < 4 else 48)
                    p_, q_ = pv[:, :, c0:c0 + cw], prev[:, :, c0:c0 + cw]
                    mu_ = mu[:, c0:c0 + cw].unsqueeze(1)
                    tt(q_, q_, p_, SUB)
                    tt(q_, q_, bc(mu_, TT, cw), MUL)
                    if g < 3:
                        tt(p_, p_, q_, ADD)
                    else:
                        dve.tensor_tensor(p_, p_, q_, ADD).then_inc(lora_ready, 1)
                r_, k_, v_ = (pv[:, :, i * RW:(i + 1) * RW] for i in range(3))
                for t in range(TT):
                    evac(nb(TMP)[:, t, :], ("wup", l, t), lambda b: b[:, :], V("decay_b"), ADD)
                    evac(nb(A_)[:, t, :], ("aup", l, t), lambda b: b[:, :], V("iclr_b"), ADD)
                    if l:
                        evac(nb(KK)[:, t, :], ("vup", l, t), lambda b: b[:, :], V("vres_b"), ADD)
                if l:
                    tt(nb(B_), v_first[:, :, :], v_, SUB)
                    dve.wait_ge(vmix_done, TT)
                    tt(nb(B_), nb(B_), nb(KK), MUL)
                    tt(v_, v_, nb(B_), ADD)
                else:
                    step(dve.tensor_copy(v_first[:, :, :], v_))
                heads = lambda a: a.rearrange("p (n c) -> p n c", c=HD)
                kkf, bf = NB[:, KK, :], NB[:, B_, :]
                tt(nb(KK), k_, bc(V("kk_s").unsqueeze(1), TT, RW), MUL)
                tt(bf, kkf, kkf, MUL)
                total(ss[:, 0:16], heads(bf))
                ts(ss[:, 0:16], ss[:, 0:16], 1e-24, None, ALU.max)
                rs = rsqrt(ss, 16, 1.0, 0.0)
                tt(heads(kkf), heads(kkf), bc(rs.unsqueeze(2), 16, HD), MUL)
                dve.wait_ge(rate_done, TT * (l + 1))
                stt(nb(B_), nb(A_), -1.0, bc(V("ka_s").unsqueeze(1), TT, RW), ADD, MUL)
                stt(k_, nb(B_), 1.0, k_, ADD, MUL)
                tt(bf, kkf, NB[:, A_, :], MUL)
                for t in range(TT):
                    ahead(("cums", l, t))
                    B.wait_evacuated(dve, ("cum", l, t))
                    B.wait_evacuated(dve, ("cums", l, t))
                tt(NB[:, ECP, :], kkf, NB[:, ECP, :], MUL)
                tt(bf, bf, NB[:, ENC, :], MUL)
                ahead(("wt", l))
                tt(nb(ENC), k_, nb(ENC), MUL)
                tt(nb(RHO), r_, nb(EC), MUL)
                if l:
                    dve.wait_ge(state_ready, 5 * l)
                dve.memset(state[:, :, :], 0.0).then_inc(state_ready, 1)
                tt(nb(KK), r_, k_, MUL)
                dve.engine_nop().then_inc(elem, 1)
                ahead(("aT", l, 0))
                tt(nb(KK), nb(KK), bc(V("bonus").unsqueeze(1), TT, RW), MUL)
                total(sm[:, 16:32], heads(kkf))

                def qk_norm():
                    for c in range(2):
                        for t in range(TT):
                            B.wait_evacuated(dve, ("inb", l, c, t))
                    qk = dproj[:, :, 0:1024].rearrange("p t (n c) -> p t n c", c=DQ)
                    sq = pv[:, :, 0:1024].rearrange("p t (n c) -> p t n c", c=DQ)
                    for t in range(TT):
                        tt(sq[:, t], qk[:, t], qk[:, t], MUL)
                        yield
                        total(ss[:, 16 * t:16 * t + 16], sq[:, t])
                        yield
                    rs = rsqrt(ss, 32, 1.0 / DQ, EPS).rearrange("p (t n) -> p t n", t=TT).unsqueeze(3)
                    yield
                    for t in range(TT):
                        tt(qk[:, t], qk[:, t], bc(rs[:, t], 16, DQ), MUL)
                        yield
                    for w, nm in ((0, "q_norm"), (1, "k_norm")):
                        part = qk[:, :, 8 * w:8 * w + 8, :]
                        tt(part, part, bc(V(nm).unsqueeze(1).unsqueeze(1), TT, 8, DQ), MUL)
                        yield
                    x1, x2 = qk[:, :, :, 0:8], qk[:, :, :, 8:16]
                    t1 = pv[:, :, 0:128].rearrange("p t (n c) -> p t n c", c=8)
                    t2 = pv[:, :, 128:256].rearrange("p t (n c) -> p t n c", c=8)
                    sn, cs = bc(sin.unsqueeze(2), TT, 16, 8), bc(cos.unsqueeze(2), TT, 16, 8)
                    tt(t1, x1, sn, MUL)
                    tt(t2, x2, sn, MUL)
                    tt(x1, x1, cs, MUL)
                    yield
                    tt(x2, x2, cs, MUL)
                    tt(x1, x1, t2, SUB)
                    dve.tensor_tensor(x2, x2, t1, ADD).then_inc(qs_ready, 1)
                qk_steps = qk_norm()
                for t in range(TT):
                    for h in (0, 2, 4, 6, 1, 3, 5, 7):
                        evac(mats[:, h, :, :].rearrange("p (a q) t -> p a (q t)", a=2), ("m12", l, t, h),
                             lambda b: b[:, :].rearrange("p (a q) -> p a q", a=2), bc(C("mask_in").unsqueeze(1), 2, 256), MUL)
                    for par in range(2):
                        tp = Tm.rearrange("p (b q) t -> p b q t", q=2)[:, :, par, :]
                        evac(tp, ("m3", l, t, par), four, bc(C("neg1").unsqueeze(1), 4, P), MUL)
                    tt(Tm, Tm, bc(ident.unsqueeze(1), 8, P), ADD)
                    tt(TTm, mats[:, :, 0, :], bc(C("neg1T").unsqueeze(1), 8, P), MUL)
                    dve.tensor_tensor(TTm, TTm, bc(ident.unsqueeze(1), 8, P), ADD).then_inc(t_ready, 1)
                    dve.wait_ge(t_ready, TT * l + t + 1)
                    for lv in range(5):
                        b2 = 2 << lv

                        def sub(m, name, q):
                            bank = B.wait_filled(dve, name)
                            mc = m.rearrange("p h (n q b) -> p h n q b", q=2, b=b2)[:, :, :, q, :]
                            B.release(dve.tensor_tensor(mc, mc, bank[:, 0:256].rearrange("p (h n b) -> p h n b", h=4, b=b2), SUB), name)
                        ahead(("ZT", l, t, lv, 0))
                        for g in range(2):
                            hs = slice(4 * g, 4 * g + 4)
                            if lv < 4:
                                sub(Tm[:, hs, :], ("Z", l, t, lv, g), 0)
                            sub(TTm[:, hs, :], ("ZT", l, t, lv, g), 1)
                            if lv < 4:
                                B.wait_evacuated(dve, ("Z", l, t, lv, g))
                            B.wait_evacuated(dve, ("ZT", l, t, lv, g))
                        next(qk_steps, None)
                    B.wait_evacuated(dve, ("SA0", l, t))
                    for p in range(2):
                        c = 2 * (TT * l + t) + p
                        r = slice(64 * p, 64 * p + 64)
                        bank = B.wait_filled(dve, ("sa", l, t, p))
                        step(dve.tensor_tensor(SA[r, :], SA0[r, :], bank[r, :], SUB))
                        B.release(dve.engine_nop(), ("sa", l, t, p))
                        dve.engine_nop().then_inc(sa_ready, 1)
                        evac(state[:, :, :], ("s", l, t, p), four, state[:, :, :], ADD)
                        if p == 0:
                            next(qk_steps, None)
                        dve.wait_ge(keep_ready, c + 1)
                        dve.tensor_tensor(state[:, :, :], state[:, :, :], keep[:, :, :], MUL).then_inc(state_ready, 1)
                        dve.wait_ge(state_ready, c + l + 2)
                    for p in range(2):
                        B.wait_evacuated(dve, ("y1", l, t, p))
                    evac(yraw[:, t, :], ("y2", l, t), lambda b: b[:, :], yraw[:, t, :], ADD)
                assert next(qk_steps, "end") == "end"

                def group_norm():
                    y, yf, rho, gs = NB[:, EC, :], heads(NB[:, EC, :]), NB[:, RHO, :], ss[:, 16:32]
                    total(gs, yf)
                    ts(gs, gs, 1.0 / HD, None, MUL)
                    yield
                    tt(yf, yf, bc(gs.unsqueeze(2), 16, HD), SUB)
                    yield
                    tt(rho, y, y, MUL)
                    yield
                    total(gs, heads(rho))
                    yield
                    rs = rsqrt(gs, 16, 1.0 / HD, GN_EPS)
                    dve.tensor_tensor(yf, yf, bc(rs.unsqueeze(2), 16, HD), MUL).then_inc(gn_ready, 1)
                gn_steps = group_norm()

                lp = SH[:, 3072:3200]
                tt(lp, vec[:, VEC["lq1"][0]:VEC["lq1"][0] + 128], vec[:, VEC["lk1"][0]:VEC["lk1"][0] + 128], MUL)
                step(dve.tensor_reduce(sm[:, 36:38], lp.rearrange("p (a c) -> p a c", a=2), AX.X, ADD))
                dve.engine_nop().then_inc(lam_in, 1)
                dve.wait_ge(lam_exp, l + 1)
                nlam = sm[:, 42:43]
                tt(nlam, sm[:, 39:40], sm[:, 38:39], SUB)
                ts(nlam, nlam, -lam_init, None, ADD)

                def row_max(h):
                    for m in range(2):
                        S = SH[:, 384 * m:384 * m + 384]
                        if h:
                            dve.wait_ge(pexp, 8 * l + 2 * (h - 1) + m + 1)
                        evac(S, ("ds", l, h, m), lambda b: b[:, 0:384], C("causal"), ADD)
                        j = 4 * h + 2 * m
                        step(dve.tensor_reduce(ss[:, j:j + 1], S[:, 0:128], AX.X, ALU.max))
                        step(dve.tensor_reduce(ss[:, j + 1:j + 2], S[:, 128:384], AX.X, ALU.max))
                        dve.tensor_scalar(ss[:, j:j + 2], ss[:, j:j + 2], -DQ ** -0.5, None, MUL).then_inc(smx, 1)

                def attend(h):
                    dve.wait_ge(pexp, 8 * l + 2 * h + 2)
                    j = 4 * h
                    step(dve.reciprocal(ss2[:, j:j + 4], ss2[:, j:j + 4]))
                    ts(ss2[:, j + 2:j + 4], ss2[:, j + 2:j + 4], nlam, None, MUL)
                    if h >= 2:
                        B.wait_filled(dve, ("atT", l, h - 2))
                    o, p0, p1 = 2304 + 384 * (h % 2), 768 + 768 * (h % 2), 768 + 768 * (h % 2) + 384
                    for q, (a, b) in enumerate(((0, 128), (128, 384))):
                        ts(SH[:, o + a:o + b], SH[:, p0 + a:p0 + b], ss2[:, j + q:j + q + 1], None, MUL)
                        stt(SH[:, o + a:o + b], SH[:, p1 + a:p1 + b], ss2[:, j + 2 + q:j + 3 + q], SH[:, o + a:o + b], MUL, ADD)
                    dve.engine_nop().then_inc(attn_ready, 1)
                for h in range(DH + 1):
                    if h < DH:
                        row_max(h)
                    if h:
                        attend(h - 1)
                    next(gn_steps, None)
                    next(gn_steps, None)
                for _ in gn_steps:
                    pass
                for h in range(DH):
                    B.wait_evacuated(dve, ("pv", l, h))
                o4 = hNv[:, :, RW:].rearrange("p t (h c) -> p t h c", h=DH)
                tt(SH[:, 0:1024].rearrange("p (t h c) -> p t h c", t=TT, h=DH), o4, o4, MUL)
                total(ss[:, 0:8], SH[:, 0:1024].rearrange("p (n c) -> p n c", c=DV))
                rs = rsqrt(ss, 8, 1.0 / DV, EPS)
                ts(rs, rs, 1.0 - lam_init, None, MUL)
                tt(o4, o4, bc(rs.rearrange("p (t h) -> p t h", t=TT).unsqueeze(3), TT, DH, DV), MUL)
                dve.tensor_tensor(o4, o4, bc(V("subln").unsqueeze(1).unsqueeze(1), TT, DH, DV), MUL).then_inc(ycat, 1)
                dve.wait_ge(ycat, 2 * l + 2)
                memn = nbf[:, 4096:6144].rearrange("p (t c) -> p t c", t=TT)
                dve.wait_ge(msq_done, 2 * l + 2)
                r = rsqrt(sm[:, 34:36], TT, 1.0 / D, EPS)
                for t in range(TT):
                    dve.tensor_scalar(memn[:, t, :], memn[:, t, :], r[:, t:t + 1], None, MUL).then_inc(mn_done, 1)
                dve.wait_ge(mn_done, 2 * l + 2)
                plain_hT(("hT", l, 1))
                gain_hT(("mT", l), hTv, gains(l, "mem"))
                add_x(("op", l))
                h_lo_parts(("mT", l))
                normalize(l, 1, "xattn", ("hT", l, 2), parts=False)

                def head_norm(src, scratch, done):
                    half = src.shape[1] // 2
                    for a in (0, half):
                        tt(scratch[:, a:a + half], src[:, a:a + half], src[:, a:a + half], MUL)
                    total(ss[:, 0:8], scratch.rearrange("p (n c) -> p n c", c=XD))
                    yield
                    rs = rsqrt(ss, 8, 1.0 / XD, EPS)
                    s8 = src.rearrange("p (n c) -> p n c", c=XD)
                    dve.tensor_tensor(s8, s8, bc(rs.unsqueeze(2), 8, XD), MUL).then_inc(done, 1)
                    dve.wait_ge(done, l + 1)

                for c in range(2):
                    for t in range(TT):
                        ahead(("kv", l, c, t))
                        B.wait_evacuated(dve, ("kv", l, c, t))
                for c, _ in enumerate(head_norm(dproj[:, :, :].rearrange("p t c -> p (t c)")[:, 0:2048], nbf[:, 0:2048], xk_n)):
                    ahead(("kv", l, 2, 1))
                for t in range(TT):
                    ahead(("kv", l, 3, t))
                    B.wait_evacuated(dve, ("kv", l, 3, t))
                h_lo_parts(("hT", l, 2))
                for c in range(2):
                    for t in range(TT):
                        ahead(("xq", l, c, t))
                        B.wait_evacuated(dve, ("xq", l, c, t))
                for _ in head_norm(proj[:, 0:2048], nbf[:, 2048:4096], xq_n):
                    pass
                gain_hT(("xqT", l), nbf[:, 2048:4096].rearrange("p (k t) -> p k t", k=KD), gains(l, "xq"))
                gain_hT(("xkT", l), nbf[:, 0:2048].rearrange("p (k t) -> p k t", k=KD), gains(l, "xk"))
                PT = nbf[:, 8192:9216].rearrange("p (s n) -> p s n", s=2)
                ahead(("xq", l, 1, 1))
                for h in range(XH + 1):
                    if h < XH:
                        ahead(("xs", l, h))
                        bank = B.wait_filled(dve, ("xs", l, h))
                        j = 16 + 2 * h
                        step(dve.tensor_reduce(ss[:, j:j + 2], bank[:, :].rearrange("p (q k) -> p q k", q=2), AX.X, ALU.max))
                        dve.tensor_scalar(ss[:, j:j + 2], ss[:, j:j + 2], -XD ** -0.5, None, MUL).then_inc(xs_mx, 1)
                    if h:
                        bank = B.wait_filled(dve, ("xpT", l, h - 1))
                        B.release(dve.tensor_copy(PT[:, (h - 1) % 2, :], bank[:, :]), ("xpT", l, h - 1))
                        j = 16 + 2 * (h - 1)
                        B.wait_evacuated(dve, ("xs", l, h - 1))
                        step(dve.reciprocal(ss2[:, j:j + 2], ss2[:, j:j + 2]))
                        bank = B.wait_filled(dve, ("xo", l, h - 1))
                        for q in range(TT):
                            ins = dve.tensor_scalar(memn[:, q, (h - 1) * XD:h * XD], bank[:, q * 256:(q + 1) * 256], ss2[:, j + q:j + q + 1], None, MUL)
                        B.release(ins, ("xo", l, h - 1))
                plain_hT(("oT", l))
                add_x(("wo", l))
                normalize(l, 2, "ffn", ("hT", l, 3))
                if l == 0:
                    sil = nbf[:, 1536:2048].rearrange("p (t n) -> p t n", t=TT)
                    actv = nbf[:, 0:1024].rearrange("p (s t n) -> p s t n", s=2, t=2)
                    for c in range(FD // FC):
                        for t in range(TT):
                            ahead(("gu", c, t))
                            bank = B.wait_filled(dve, ("gu", c, t))
                            dve.wait_ge(silu_done, TT * c + t + 1)
                            B.release(dve.tensor_tensor(actv[:, c % 2, t, :], sil[:, t, :], bank[:, FC:2 * FC], MUL), ("gu", c, t))
                        ahead(("fT", c))
                        bank = B.wait_filled(dve, ("fT", c))
                        dve.wait_ge(act_hi, c + 1)
                        B.release(dve.tensor_tensor(h_lo[:, 2048:2560], bank[:, :], h_hi[:, 2048:2560].bitcast(F32), SUB), ("fT", c))
                    for t in range(TT):
                        for nn in range(2):
                            xs = x[:, t, nn * 512:(nn + 1) * 512]
                            evac(xs, ("fy", t * 2 + nn), lambda b: b[:, :], xs, ADD)
            SILU0, HI0 = TT * (FD // FC), FD // FC

            sc = nbf[:, 8192:9216]
            sel, lg = (sc[:, a:a + 16].rearrange("p (t e) -> p t e", t=TT) for a in (0, 16))
            mx8 = sc[:, 32:48].rearrange("p (t e) -> p t e", t=TT)
            w4 = sc[:, 64:68].rearrange("p (t j) -> p t j", t=TT)
            ix = sc[:, 80:96]
            ixf = sc[:, 96:112].rearrange("p (t e) -> p t e", t=TT)
            oh = sc[:, 112:144].rearrange("p (j t e) -> p j t e", j=2, t=TT)
            gate = sc[:, 144:160].rearrange("p (t e) -> p t e", t=TT)
            pos = sc[:, 160:184]
            ov, rank, R, tmp = (sc[:, a:a + 8] for a in (184, 192, 200, 208))
            tmp2 = sc[:, 224:240].rearrange("p (t e) -> p t e", t=TT)
            itf = sc[:, 240:244]
            IT = sc[:, 256:256 + 6 * (NITEM + 1)].rearrange("p (q t i) -> p q t i", q=3, t=TT)
            iota8 = C("iota")[:, 0:NE]
            dve.memset(nbf[:, 2560:2816], 0.0)
            dve.memset(nbf[:, 4096:5120], 0.0)
            bank = B.wait_filled(dve, ("logit",))
            B.release(dve.tensor_copy(sc[:, 16:32], bank[:, 0:16]), ("logit",))
            B.wait_evacuated(dve, ("logit",))
            for t in range(TT):
                step(dve.max(mx8[:, t, :], lg[:, t, :]))
                step(dve.max_index(ix.bitcast(U32)[:, t * 8:(t + 1) * 8], mx8[:, t, :], lg[:, t, :]))
            step(dve.tensor_copy(sc[:, 96:112], ix.bitcast(U32)))
            tt(w4[:, :, 0], mx8[:, :, 0], mx8[:, :, 1], SUB)
            dve.tensor_tensor(w4[:, :, 1], mx8[:, :, 1], mx8[:, :, 0], SUB).then_inc(w_in, 1)
            for j in range(2):
                for t in range(TT):
                    ts(oh[:, j, t, :], iota8, ixf[:, t, j:j + 1], None, ALU.is_equal)
            dve.tensor_tensor(sel, oh[:, 0, :, :], oh[:, 1, :, :], ADD).then_inc(rt_sel, 1)
            dve.wait_ge(rt_sel, 1)
            dve.wait_ge(w_sig, 1)
            for t in range(TT):
                ts(gate[:, t, :], oh[:, 0, t, :], w4[:, t, 0:1], None, MUL)
                stt(gate[:, t, :], oh[:, 1, t, :], w4[:, t, 1:2], gate[:, t, :], MUL, ADD)
            bank = B.wait_filled(dve, ("pos",))
            B.release(dve.tensor_copy(pos, bank[:, 0:24]), ("pos",))
            B.wait_evacuated(dve, ("pos",))
            posv = pos[:, 0:16].rearrange("p (t e) -> p t e", t=TT)
            for q, src in enumerate((posv, sel, gate)):
                step(dve.tensor_copy(IT[:, q, :, 0:NE], src))
            step(dve.memset(IT[:, :, :, NITEM], 0.0))
            ts(ov, pos[:, 16:24], float(P), None, ALU.is_gt)
            step(dve.tensor_tensor_scan(rank, C("ones")[:, 0:NE], ov, 0.0, MUL, ADD))
            step(dve.tensor_copy(itf[:, 0:1], rank[:, NE - 1:NE]))
            tt(rank, rank, ov, SUB)
            for r in range(NOVER):
                ts(R, rank, float(r), None, ALU.is_equal)
                tt(R, R, ov, MUL)
                for q, src in enumerate((posv, sel, gate)):
                    tt(tmp2, src, bc(R.unsqueeze(1), TT, NE), MUL)
                    step(dve.tensor_reduce(IT[:, q, :, NE + r], tmp2, AX.X, ADD))
                ts(IT[:, 0, :, NE + r], IT[:, 0, :, NE + r], -float(P), None, ADD)
                tt(tmp, R, iota8, MUL)
                step(dve.tensor_reduce(itf[:, r + 1:r + 2], tmp, AX.X, ADD))
            dve.tensor_copy(sb_items[:, :], itf[0:1, :]).then_inc(items_in, 1)

            Psel = nbf[:, 2048:2304].rearrange("p (t j) -> p t j", t=TT)
            Pg = nbf[:, 2304:2560].rearrange("p (t j) -> p t j", t=TT)
            cur = sm[:, 44:50]

            def select(i, q, dst, more=0):
                step(dve.tensor_copy(cur.rearrange("p (q t) -> p q t", q=3).unsqueeze(3), IT[:, :, :, bass.ds(i, 1)]), more)
                for t in range(TT):
                    ins = dve.tensor_scalar(dst[:, t, :], C("iota"), cur[:, t:t + 1], cur[:, 2 * q + t:2 * q + t + 1], ALU.is_equal, MUL)
                ins.then_inc(sel_done, 1)

            def evac_e(dst, name, src, other, op, more):
                bank_no, nth = B.use[name]
                dve.wait_ge(ready[bank_no], nth + 1 + more(bank_no))
                B.release(dve.tensor_tensor(dst, src(psum[bank_no]), other, op), name)
                dve.wait_ge(evacuated[bank_no], nth + 1 + more(bank_no))

            def next_tokens(more):
                heT = hT[:, 0:1024].rearrange("p (k j) -> p k j", k=KD)
                for g in range(2):
                    evac_e(heT[:, 4 * g:4 * g + 4, :], ("he", g), four, bc(gains(1, "ffn")[:, 4 * g:4 * g + 4].unsqueeze(2), 4, P), MUL, more)

            def next_lo(more):
                dve.wait_ge(h_hi_done, H_SPLIT0 + 1 + more)
                dve.tensor_tensor(h_lo[:, 0:1024], hT[:, 0:1024], h_hi[:, 0:1024].bitcast(F32), SUB).then_inc(h_split, 1)

            def result(i):
                bank = B.wait_filled(dve, ("ey", 1), (i - 1) * MOE_PER[5])
                B.release(dve.tensor_copy(nbf[:, 4608:5120], bank[:, :]), ("ey", 1))

            def add_result(t, more):
                for nn in range(2):
                    xs = x[:, t, nn * 512:(nn + 1) * 512]
                    evac_e(xs, ("sc", t, nn), lambda b: b[:, :], xs, ADD, more)

            step(dve.tensor_copy(cur.rearrange("p (q t) -> p q t", q=3), IT[:, :, :, 0]))
            for t in range(TT):
                ins = dve.tensor_scalar(Psel[:, t, :], C("iota"), cur[:, t:t + 1], cur[:, 2 + t:3 + t], ALU.is_equal, MUL)
            ins.then_inc(sel_done, 1)
            next_tokens(lambda bank: -MOE_PER[bank])
            next_lo(0)

            first_step = n[0]

            def expert(i):
                n[0] = first_step

                def more(bank):
                    return i * MOE_PER[bank]
                done = [0]

                def split_to(m):
                    while done[0] < min(m, PER):
                        expert_lo_of(dve, done[0], i)
                        done[0] += 1
                split_to(LOOK)
                result(i)
                actv = nbf[:, 0:512].rearrange("p (s n) -> p s n", s=2)
                sil = nbf[:, 1536:2048].rearrange("p (s n) -> p s n", s=2)
                for c in range(STEPS):
                    split_to((6 * c + 1 if c else 3) + 1 + LOOK)
                    bank = B.wait_filled(dve, ("egu", c), i * MOE_PER[c % 2])
                    dve.wait_ge(silu_done, SILU0 + c + 1 + i * STEPS)
                    B.release(dve.tensor_tensor(actv[:, c % 2, :], sil[:, c % 2, :], bank[:, FC:2 * FC], MUL), ("egu", c))
                    if c == STEPS - 1:
                        next_lo(1 + i)
                    if c == GATE_STEP - 1:
                        select(i, 2, Pg, i * DVE_STEPS)
                    if c == NEXT_STEP - 1:
                        select(i + 1, 1, Psel, i * DVE_STEPS)
                    split_to((6 * c + 6 if c < STEPS - 1 else PER) + LOOK)
                    bank = B.wait_filled(dve, ("eT", c), i * MOE_PER[2])
                    dve.wait_ge(act_hi, HI0 + c + 1 + i * STEPS)
                    B.release(dve.tensor_tensor(h_lo[:, 2048:2304], bank[:, 0:256], h_hi[:, 2048:2304].bitcast(F32), SUB), ("eT", c))
                    if c < TT:
                        add_result(c, more)
                    if c == NEXT_STEP:
                        next_tokens(more)
                assert n[0] == first_step + DVE_STEPS
            with dve.Fori(0, NE) as i:
                expert(i)
            n_over = dve.value_load(sb_items[0:1, 0:1], min_val=0, max_val=NOVER)
            with dve.If(n_over > 0):
                with dve.Fori(NE, n_over + NE) as i:
                    expert(i)
            result(n_over + NE)
            for t in range(TT):
                for nn in range(2):
                    xs = x[:, t, nn * 512:(nn + 1) * 512]
                    bank = B.wait_filled(dve, ("sc", t, nn), (n_over + NE) * MOE_PER[6 + nn])
                    ins = dve.tensor_tensor(xs, bank[:, :], xs, ADD)
                    ins.then_inc(final if t == TT - 1 else evacuated[6 + nn], 1)


def constants():
    import numpy as np
    f = np.float32
    i = np.arange(P)
    row, c = i[:, None], i[None, :]
    same = (row // CH) == (c // CH)
    part = {
        "ident": (row == c), "bd": same, "ones": np.ones((P, P)), "utri": row < c, "iota": np.broadcast_to(c, (P, P)),
        "mask_in": np.concatenate([same & (row < c), same & (row <= c)], 1),
        "tri": DEC * (same & (row <= c)), "tri_s": DEC * (same & (row < c)),
        "neg1": -1.0 * ((row == c + 1) & (row % 2 == 1)), "neg1T": -1.0 * ((c == row + 1) & (c % 2 == 1)),
        "lvl": np.concatenate([(row // (2 * b) == c // (2 * b)) & (row % (2 * b) < b) & (c % (2 * b) >= b) for b in (2, 4, 8, 16, 32)], 1),
        "causal": np.concatenate([-1e30 * (c > row), np.zeros((P, P)), -1e30 * (c > row)], 1),
        "last": np.stack([i == CH - 1, i == 2 * CH - 1], 1),
        "freq": np.broadcast_to(f(500000.0) ** (-np.arange(0, ROPE, 2, dtype=f) / f(ROPE)), (P, 8)),
    }
    return np.ascontiguousarray(np.concatenate([np.asarray(part[n], f).reshape(P, w) for n, (_, w) in CST.items()], 1))


def kernel(**inputs):
    import numpy as np
    import concourse.bacc as bacc
    from concourse import mybir as mb
    from concourse.bass_utils import run_bass_kernel_spmd

    a = {k: np.ascontiguousarray(v) for k, v in inputs.items()}
    L = DEPTH
    last = lambda n: np.broadcast_to(a[n][-1], (L, *a[n].shape[1:]))
    mus = np.ascontiguousarray(np.concatenate([a["shift_mu"], last("vres_shift_mu")], 1))
    src = {"decay_b": a["decay_bias"], "iclr_b": a["iclr_bias"],
           "kk_s": a["key_kk_scale"], "ka_s": a["key_iclr_scale"], "bonus": a["bonus_rk"].reshape(L, -1), "gn_w": a["rwkv_gn_w"],
           "gn_b": a["rwkv_gn_b"], "vres_b": last("vres_bias"), "q_norm": a["q_norm"], "k_norm": a["k_norm"],
           "lq1": a["lambda_q1"], "lq2": a["lambda_q2"], "lk1": a["lambda_k1"], "lk2": a["lambda_k2"], "subln": a["diff_subln"]}
    vecs = np.ascontiguousarray(np.concatenate([src[n] for n in VEC], 1))
    fold = lambda v: v.reshape(L, -1, P).transpose(0, 2, 1)
    cols = np.ascontiguousarray(np.concatenate(
        [fold(a[n]) for n in ("mix_norm", "xattn_norm", "mem_norm", "ffn_norm")]
        + [np.tile(fold(a[n]), (1, 1, XH)) for n in ("xattn_q_norm", "xattn_k_norm")], 2))
    feeds = {"x": a["x"], "mem": a["mem"], "positions": np.ascontiguousarray(a["positions"].reshape(TT, P).T), "mus": mus, "vecs": vecs, "cols": cols, "consts": constants()}
    for n in ("in_proj", "decay_up", "iclr_up", "gate_up", "vres_down", "vres_up", "out_proj", "xattn_wq", "xattn_wkv", "xattn_wo",
              "dense_w_gu", "dense_w_down", "router", "expert_w_gu", "expert_w_down"):
        feeds[n] = a[n]
    nc = bacc.Bacc("TRN2", target_bir_lowering=False, num_devices=1)
    args = [nc.dram_tensor(f"in_{n}", v.shape, mb.dt.from_np(v.dtype), kind="ExternalInput").ap() for n, v in feeds.items()]
    args.append(nc.dram_tensor("out_0", (1, SEQ, D), mb.dt.float32, kind="ExternalOutput").ap())
    decoder_trunk(nc, *args)
    r = run_bass_kernel_spmd(nc, [{f"in_{n}": v for n, v in feeds.items()}], core_ids=[0])
    return r.results[0]["out_0"]
```
